# Optimizing a Trainium2 kernel written in Bass

```python
import math
import jax, jax.numpy as jnp
from jax import lax
import numpy as np

D_MODEL = 1024
BATCH = 1
SEQ = 1024
DEPTH = 1
DEC_BATCH = 8
DEC_SEQ = 1
PAST_LEN = 8192
PAGE_SIZE = 128

D_MIX = 2 * D_MODEL
D_SSD = D_MIX // 2
SSD_HEAD_DIM = 64
SSD_HEADS = D_SSD // SSD_HEAD_DIM
SSD_STATE = 128
SSD_GROUPS = 2
CONV_K = 4
SSD_CONV_DIM = D_SSD + 2 * SSD_GROUPS * SSD_STATE
D_MLSTM = D_MIX - D_SSD
MLSTM_HEADS = 4
MLSTM_DK = D_MLSTM // MLSTM_HEADS
MLSTM_DV = D_MLSTM // MLSTM_HEADS
CHUNK = 128
PEER_HEADS = 8
PEER_NKEYS = 128
PEER_EXPERTS = PEER_NKEYS * PEER_NKEYS
PEER_DKEY = 256
PEER_TOPK = 16
PEER_BLOCK = 256
ALPHA = (2.0 * DEPTH) ** 0.25
BETA = (8.0 * DEPTH) ** -0.25
LN_EPS = 1e-5
IN_SPLITS = (D_SSD, SSD_CONV_DIM, SSD_HEADS, D_MLSTM, D_MLSTM, D_MLSTM, MLSTM_HEADS, MLSTM_HEADS)
IN_COLS = sum(IN_SPLITS)

kernel_name = 'hybrid_ssd_mlstm_peer_step'

def _layer_norm(x, g, b):
    xf = x.astype(jnp.float32)
    mu = xf.mean(-1, keepdims=True)
    var = jnp.square(xf - mu).mean(-1, keepdims=True)
    return ((xf - mu) * lax.rsqrt(var + LN_EPS) * g.astype(jnp.float32) + b.astype(jnp.float32)).astype(x.dtype)

def _rms_norm(x, g):
    xf = x.astype(jnp.float32)
    return (xf * lax.rsqrt(jnp.mean(xf * xf, -1, keepdims=True) + LN_EPS) * g.astype(jnp.float32)).astype(x.dtype)

def _chunk_len(L):
    return CHUNK if L % CHUNK == 0 else L

def _to_chunks(a, T):
    b, L = a.shape[:2]
    return a.reshape((b, L // T, T) + a.shape[2:]).swapaxes(0, 1)

def _from_chunks(a):
    nc, b, T = a.shape[:3]
    return a.swapaxes(0, 1).reshape((b, nc * T) + a.shape[3:])

def _causal_conv(x, buf, w, b):
    L = x.shape[1]
    xp = jnp.concatenate([buf.astype(x.dtype), x], axis=1)
    y = b + xp[:, 0:L] * w[0]
    for j in range(1, CONV_K):
        y = y + xp[:, j:j + L] * w[j]
    return y, xp[:, L:]

def _ssd_scan(xs, dt, a, bm, cm, h0):
    T = _chunk_len(xs.shape[1])
    mask = jnp.tril(jnp.ones((T, T), bool))[None, :, :, None, None]

    def step(h, inp):
        xc, dtc, bc, cc = inp
        acs = jnp.cumsum(dtc * a, axis=1)
        lmat = jnp.exp(jnp.where(mask, acs[:, :, None] - acs[:, None], -jnp.inf))
        cb = jnp.einsum('btgn,bsgn->btsg', cc, bc)
        mm = cb[..., None] * lmat * dtc[:, None]
        y = jnp.einsum('btsgh,bsghp->btghp', mm, xc)
        y = y + jnp.einsum('btgn,bghpn->btghp', cc, h) * jnp.exp(acs)[..., None]
        decay = jnp.exp(acs[:, -1:] - acs) * dtc
        h_new = h * jnp.exp(acs[:, -1])[..., None, None] + jnp.einsum('bsgn,bsgh,bsghp->bghpn', bc, decay, xc)
        return h_new, y

    h, ys = lax.scan(step, h0, tuple(_to_chunks(t, T) for t in (xs, dt, bm, cm)))
    return _from_chunks(ys), h

def _mlstm_scan(q, k, v, logi, logf, c0, n0, m0):
    T = _chunk_len(q.shape[1])
    mask = jnp.tril(jnp.ones((T, T), bool))[None, :, :, None]

    def step(carry, inp):
        c, n, m = carry
        qc, kc, vc, ic, fc = inp
        bcs = jnp.cumsum(fc, axis=1)
        dmat = jnp.where(mask, bcs[:, :, None] - bcs[:, None] + ic[:, None], -jnp.inf)
        inter = bcs + m[:, None]
        m_t = jnp.maximum(inter, dmat.max(axis=2))
        w_inter = jnp.exp(inter - m_t)
        att = jnp.einsum('bthd,bshd->btsh', qc, kc) * jnp.exp(dmat - m_t[:, :, None])
        num = jnp.einsum('btsh,bshv->bthv', att, vc) + w_inter[..., None] * jnp.einsum('bthd,bhdv->bthv', qc, c)
        den = att.sum(axis=2) + w_inter * jnp.einsum('bthd,bhd->bth', qc, n)
        h = num / jnp.maximum(jnp.abs(den), jnp.exp(-m_t))[..., None]
        b_end = bcs[:, -1]
        g = b_end[:, None] - bcs + ic
        m_new = jnp.maximum(b_end + m, g.max(axis=1))
        w_old = jnp.exp(b_end + m - m_new)
        w_s = jnp.exp(g - m_new[:, None])
        c_new = w_old[..., None, None] * c + jnp.einsum('bsh,bshd,bshv->bhdv', w_s, kc, vc)
        n_new = w_old[..., None] * n + jnp.einsum('bsh,bshd->bhd', w_s, kc)
        return (c_new, n_new, m_new), h

    (c, n, m), hs = lax.scan(step, (c0, n0, m0), tuple(_to_chunks(t, T) for t in (q, k, v, logi, logf)))
    return _from_chunks(hs), c, n, m

def _peer(x, wq, keys, u, v):
    bsz, seq, d = x.shape
    n = bsz * seq
    blk = min(PEER_BLOCK, n)
    n_pad = -(-n // blk) * blk
    xt = jnp.pad(x.reshape(n, d), ((0, n_pad - n), (0, 0)))

    def block(xb):
        q = jnp.einsum('td,dc->tc', xb, wq).reshape(blk, PEER_HEADS, 2, PEER_DKEY // 2).astype(jnp.float32)
        s = jnp.einsum('thcd,hckd->thck', q, keys.astype(jnp.float32))
        s1, i1 = lax.top_k(s[:, :, 0], PEER_TOPK)
        s2, i2 = lax.top_k(s[:, :, 1], PEER_TOPK)
        cand = (s1[..., :, None] + s2[..., None, :]).reshape(blk, PEER_HEADS, PEER_TOPK * PEER_TOPK)
        cidx = (i1[..., :, None] * PEER_NKEYS + i2[..., None, :]).reshape(blk, PEER_HEADS, PEER_TOPK * PEER_TOPK)
        top, pos = lax.top_k(cand, PEER_TOPK)
        eidx = jnp.take_along_axis(cidx, pos, axis=-1)
        gate = jax.nn.softmax(top, axis=-1)
        hid = jax.nn.gelu(jnp.einsum('td,thkd->thk', xb, jnp.take(u, eidx, axis=0)).astype(jnp.float32), approximate=False)
        return jnp.einsum('thk,thkd->td', (gate * hid).astype(xb.dtype), jnp.take(v, eidx, axis=0))

    out = lax.map(block, xt.reshape(n_pad // blk, blk, d))
    return out.reshape(n_pad, d)[:n].reshape(bsz, seq, d)

def _hybrid_layer(x, st_ssd, st_ssd_conv, st_c, st_n, st_m, st_mconv,
                  w_in, conv_ssd_w, conv_ssd_b, dt_bias, a_log, d_skip, ssd_norm_g,
                  conv_m_w, conv_m_b, w_mq, w_mk, b_igate, b_fgate, mlstm_norm_g,
                  w_out, ln1_g, ln1_b, peer_wq, peer_keys, peer_u, peer_v, ln2_g, ln2_b):
    f32 = jnp.float32
    bsz, seq, _ = x.shape
    proj = jnp.einsum('bld,dc->blc', x, w_in)
    offs = [int(o) for o in np.cumsum(IN_SPLITS)[:-1]]
    z_s, xbc, dt_pre, u_m, v_m, o_m, i_pre, f_pre = jnp.split(proj, offs, axis=-1)

    xbc, new_ssd_conv = _causal_conv(xbc, st_ssd_conv, conv_ssd_w, conv_ssd_b)
    xbc = jax.nn.silu(xbc)
    xs, bm, cm = jnp.split(xbc, [D_SSD, D_SSD + SSD_GROUPS * SSD_STATE], axis=-1)
    hg = SSD_HEADS // SSD_GROUPS
    xs5 = xs.reshape(bsz, seq, SSD_GROUPS, hg, SSD_HEAD_DIM).astype(f32)
    bm4 = bm.reshape(bsz, seq, SSD_GROUPS, SSD_STATE).astype(f32)
    cm4 = cm.reshape(bsz, seq, SSD_GROUPS, SSD_STATE).astype(f32)
    dt = jax.nn.softplus(dt_pre.astype(f32) + dt_bias.astype(f32)).reshape(bsz, seq, SSD_GROUPS, hg)
    a = -jnp.exp(a_log.astype(f32)).reshape(SSD_GROUPS, hg)
    h0 = st_ssd.astype(f32).reshape(bsz, SSD_GROUPS, hg, SSD_HEAD_DIM, SSD_STATE)
    y_s, h_new = _ssd_scan(xs5, dt, a, bm4, cm4, h0)
    y_s = y_s + d_skip.astype(f32).reshape(SSD_GROUPS, hg)[:, :, None] * xs5
    y_s = y_s.reshape(bsz, seq, D_SSD).astype(x.dtype)
    y_s = _rms_norm(y_s * jax.nn.silu(z_s), ssd_norm_g)
    new_ssd = h_new.reshape(bsz, SSD_HEADS, SSD_HEAD_DIM, SSD_STATE).astype(st_ssd.dtype)

    u_c, new_mconv = _causal_conv(u_m, st_mconv, conv_m_w, conv_m_b)
    u_c = jax.nn.silu(u_c).reshape(bsz, seq, MLSTM_HEADS, MLSTM_DK).astype(f32)
    q = jnp.einsum('blhd,hde->blhe', u_c, w_mq.astype(f32))
    k = jnp.einsum('blhd,hde->blhe', u_c, w_mk.astype(f32)) * (MLSTM_DK ** -0.5)
    v = v_m.reshape(bsz, seq, MLSTM_HEADS, MLSTM_DV).astype(f32)
    logi = i_pre.astype(f32) + b_igate.astype(f32)
    logf = jax.nn.log_sigmoid(f_pre.astype(f32) + b_fgate.astype(f32))
    h_m, c_new, n_new, m_new = _mlstm_scan(q, k, v, logi, logf, st_c.astype(f32), st_n.astype(f32), st_m.astype(f32))
    mu = h_m.mean(-1, keepdims=True)
    var = jnp.square(h_m - mu).mean(-1, keepdims=True)
    h_m = (h_m - mu) * lax.rsqrt(var + LN_EPS) * mlstm_norm_g.astype(f32)
    h_m = jax.nn.sigmoid(o_m.astype(f32)).reshape(bsz, seq, MLSTM_HEADS, MLSTM_DV) * h_m
    h_m = h_m.reshape(bsz, seq, D_MLSTM).astype(x.dtype)

    mix = jnp.einsum('blc,cd->bld', jnp.concatenate([y_s, h_m], axis=-1), w_out)
    x1 = _layer_norm(ALPHA * x + mix, ln1_g, ln1_b)
    x2 = _layer_norm(ALPHA * x1 + _peer(x1, peer_wq, peer_keys, peer_u, peer_v), ln2_g, ln2_b)
    new_states = (new_ssd, new_ssd_conv.astype(st_ssd_conv.dtype), c_new.astype(st_c.dtype),
                  n_new.astype(st_n.dtype), m_new.astype(st_m.dtype), new_mconv.astype(st_mconv.dtype))
    return x2, new_states

def setup_inputs(seed: int = 0) -> dict:
    key = jax.random.key(seed)
    ks = jax.random.split(key, 32)

    def nrm(k, shape, s):
        return jax.random.normal(k, shape, jnp.float32) * s

    L = DEPTH
    dt0 = jnp.exp(jax.random.uniform(ks[11], (L, SSD_HEADS), jnp.float32, math.log(1e-3), math.log(1e-1)))
    return {
        'x_prompt': nrm(ks[0], (BATCH, SEQ, D_MODEL), 1.0),
        'x_sample': nrm(ks[1], (DEC_BATCH, DEC_SEQ, D_MODEL), 1.0),
        'state_ssd': nrm(ks[2], (L, DEC_BATCH, SSD_HEADS, SSD_HEAD_DIM, SSD_STATE), 0.5),
        'state_ssd_conv': nrm(ks[3], (L, DEC_BATCH, CONV_K - 1, SSD_CONV_DIM), 1.0),
        'state_mlstm_c': nrm(ks[4], (L, DEC_BATCH, MLSTM_HEADS, MLSTM_DK, MLSTM_DV), 0.1),
        'state_mlstm_n': nrm(ks[5], (L, DEC_BATCH, MLSTM_HEADS, MLSTM_DK), 0.1),
        'state_mlstm_m': nrm(ks[6], (L, DEC_BATCH, MLSTM_HEADS), 1.0),
        'state_mlstm_conv': nrm(ks[7], (L, DEC_BATCH, CONV_K - 1, D_MLSTM), 1.0),
        'w_in': nrm(ks[8], (L, D_MODEL, IN_COLS), D_MODEL ** -0.5),
        'conv_ssd_w': nrm(ks[9], (L, CONV_K, SSD_CONV_DIM), CONV_K ** -0.5),
        'conv_ssd_b': nrm(ks[10], (L, SSD_CONV_DIM), 0.02),
        'dt_bias': dt0 + jnp.log(-jnp.expm1(-dt0)),
        'a_log': jnp.log(jax.random.uniform(ks[12], (L, SSD_HEADS), jnp.float32, 1.0, 16.0)),
        'd_skip': 1.0 + nrm(ks[13], (L, SSD_HEADS), 0.02),
        'ssd_norm_g': 1.0 + nrm(ks[14], (L, D_SSD), 0.02),
        'conv_m_w': nrm(ks[15], (L, CONV_K, D_MLSTM), CONV_K ** -0.5),
        'conv_m_b': nrm(ks[16], (L, D_MLSTM), 0.02),
        'w_mq': nrm(ks[17], (L, MLSTM_HEADS, MLSTM_DK, MLSTM_DK), MLSTM_DK ** -0.5),
        'w_mk': nrm(ks[18], (L, MLSTM_HEADS, MLSTM_DK, MLSTM_DK), MLSTM_DK ** -0.5),
        'b_igate': nrm(ks[19], (L, MLSTM_HEADS), 0.1),
        'b_fgate': jnp.linspace(3.0, 6.0, MLSTM_HEADS, dtype=jnp.float32)[None] + nrm(ks[20], (L, MLSTM_HEADS), 0.02),
        'mlstm_norm_g': 1.0 + nrm(ks[21], (L, MLSTM_HEADS, MLSTM_DV), 0.02),
        'w_out': nrm(ks[22], (L, D_MIX, D_MODEL), BETA * D_MIX ** -0.5),
        'ln1_g': 1.0 + nrm(ks[23], (L, D_MODEL), 0.02),
        'ln1_b': nrm(ks[24], (L, D_MODEL), 0.02),
        'peer_wq': nrm(ks[25], (L, D_MODEL, PEER_HEADS * PEER_DKEY), D_MODEL ** -0.5),
        'peer_keys': nrm(ks[26], (L, PEER_HEADS, 2, PEER_NKEYS, PEER_DKEY // 2), (PEER_DKEY // 2) ** -0.5),
        'peer_u': nrm(ks[27], (L, PEER_EXPERTS, D_MODEL), D_MODEL ** -0.5),
        'peer_v': nrm(ks[28], (L, PEER_EXPERTS, D_MODEL), BETA),
        'ln2_g': 1.0 + nrm(ks[29], (L, D_MODEL), 0.02),
        'ln2_b': nrm(ks[30], (L, D_MODEL), 0.02),
    }

def reference(x_prompt, x_sample, state_ssd, state_ssd_conv, state_mlstm_c, state_mlstm_n,
              state_mlstm_m, state_mlstm_conv, w_in, conv_ssd_w, conv_ssd_b, dt_bias, a_log,
              d_skip, ssd_norm_g, conv_m_w, conv_m_b, w_mq, w_mk, b_igate, b_fgate, mlstm_norm_g,
              w_out, ln1_g, ln1_b, peer_wq, peer_keys, peer_u, peer_v, ln2_g, ln2_b):
    states = (state_ssd, state_ssd_conv, state_mlstm_c, state_mlstm_n, state_mlstm_m, state_mlstm_conv)
    bp = x_prompt.shape[0]
    yp, ys = x_prompt, x_sample
    p_list, s_list = [], []
    for l in range(DEPTH):
        weights = (w_in[l], conv_ssd_w[l], conv_ssd_b[l], dt_bias[l], a_log[l], d_skip[l], ssd_norm_g[l],
                   conv_m_w[l], conv_m_b[l], w_mq[l], w_mk[l], b_igate[l], b_fgate[l], mlstm_norm_g[l],
                   w_out[l], ln1_g[l], ln1_b[l], peer_wq[l], peer_keys[l], peer_u[l], peer_v[l], ln2_g[l], ln2_b[l])
        zero_states = tuple(jnp.zeros((bp,) + s.shape[2:], s.dtype) for s in states)
        yp, p_new = _hybrid_layer(yp, *zero_states, *weights)
        ys, s_new = _hybrid_layer(ys, *(s[l] for s in states), *weights)
        p_list.append(p_new)
        s_list.append(s_new)
    p_ssd, p_ssd_conv, p_c, p_n, p_m, p_mconv = (jnp.stack([p[i] for p in p_list]) for i in range(6))
    s_ssd, s_ssd_conv, s_c, s_n, s_m, s_mconv = (jnp.stack([s[i] for s in s_list]) for i in range(6))
    return (yp, ys, p_ssd, p_ssd_conv, p_c, p_n, p_m, p_mconv, s_ssd, s_ssd_conv, s_c, s_n, s_m, s_mconv)


_drawn_inputs = setup_inputs


def setup_inputs(seed=0):
    import zlib

    import numpy as np

    out = dict(_drawn_inputs(seed))
    spreads = {}
    factors = {'d_skip': 3.354, 'mlstm_norm_g': 3.179, 'ln2_g': 2.893, 'ln2_b': 2.769}
    for name, (base, spread) in spreads.items():
        noise = np.random.default_rng([zlib.crc32(name.encode()), seed]).standard_normal(out[name].shape)
        drawn = base * np.exp(spread * noise) if base else spread * noise
        out[name] = __import__('jax').numpy.asarray(drawn.astype(out[name].dtype))
    for name, factor in factors.items():
        out[name] = (out[name] * factor).astype(out[name].dtype)
    return out
```

```python
import concourse.bass as bass
from concourse import mybir
from concourse.alu_op_type import AluOpType as ALU
from contextlib import ExitStack
import numpy as np

P = 128
D = 1024
KD = D // P
SEQ = 1024
CH = 128
NCH = SEQ // CH
NSMP = 8
NTOK = SEQ + NSMP
NH, HD, NST, NG = 16, 64, 128, 2
MH, DK = 4, 256
KT = DK // P
NCT = 20
BT0, CT0, UT0 = 8, 10, 12
PH, NK, TOPK = 8, 128, 16
NE = NK * NK
NHC = 2 * PH
TAPS = 4
ALPHA = 2.0 ** 0.25
EPS = 1e-5
BIG = 1e30
NEG = -3e38
R_NACS, R_M, R_WLOG, R_DT, R_G, R_MT, NROW = 0, 16, 20, 24, 40, 44, 48
NB = 8


class Chain:

    def __init__(self, eng, sem, base=0, plain=None):
        self.eng, self.sem, self.base, self.plain, self.n = eng, sem, base, plain, 0

    def link(self, ins):
        ins.then_inc(self.sem, 1)
        self.n += 1
        self.eng.wait_ge(self.sem, self.base + self.n)

    def link_plain(self, ins):
        self.link(ins)
        self.eng.sem_inc(self.plain, 1)


def steps(eng, n):
    yield 0
    with eng.Fori(1, n) as i:
        yield i


def inner(eng, outer, n):
    if isinstance(outer, int):
        yield from steps(eng, n)
    else:
        with eng.Fori(0, n) as i:
            yield i


def build(nc, a, o):
    f32, u32 = mybir.dt.float32, mybir.dt.uint32
    ACT = mybir.ActivationFunctionType
    X = mybir.AxisListType.X

    def dram(name, shape, dt=f32):
        return nc.dram_tensor(name, shape, dt).ap()

    cht_d = dram("cht_d", (NCT, P, NTOK))
    tok_d = dram("tok_d", (6, NTOK, 512))
    rows_d = dram("rows_d", (NROW, SEQ))
    rows_s_d = dram("rows_s_d", (NROW, NSMP))
    wp_d = dram("wp_d", (NHC, P, KD, NK))
    mixt_d = dram("mixt_d", (16, P, NTOK))
    x1_d = dram("x1_d", (NTOK, D))
    eidx_d = dram("eidx_d", (PH, NTOK, TOPK), u32)
    gate_d = dram("gate_d", (PH, NTOK, TOPK))
    bc_d = dram("bc_d", (NSMP, 4, P))

    top = ExitStack()
    with top:
        phase_sems = []

        def sem(name):
            phase_sems.append(nc.alloc_semaphore(name=name))
            return phase_sems[-1]

        def end_phase():
            nc.clear_and_free_semaphores(phase_sems)
            nc.all_engine_barrier()
            phase_sems.clear()

        PB = top.enter_context(nc.psum_tensor("PB", [P, 8, 512], f32))
        ident = top.enter_context(nc.sbuf_tensor("ident", [P, P], f32))

        def two(b):
            return PB[:, b:b + 2, :].rearrange("p a n -> p (a n)")

        with ExitStack() as ctx:
            def sb(name, shape, dt=f32):
                return ctx.enter_context(nc.sbuf_tensor(name, shape, dt))

            xT = sb("xT", [P, KD, NTOK])
            wch = [sb(f"wch{i}", [P, KD, P]) for i in range(2)]
            wtk = [sb(f"wtk{i}", [P, KD, 512]) for i in range(2)]
            wrow = sb("wrow", [P, KD, P])
            cw = [sb(f"cw{i}", [P, TAPS + 1]) for i in range(2)]
            xp = [sb(f"xp{i}", [P, TAPS - 1 + SEQ]) for i in range(2)]
            xps = [sb(f"xps{i}", [P, TAPS, NSMP]) for i in range(2)]
            cv = [sb(f"cv{i}", [P, NTOK]) for i in range(2)]
            so = [sb(f"so{i}", [P, NTOK]) for i in range(2)]
            stg = [sb(f"stg{i}", [P, 512]) for i in range(6)]
            gb = sb("gb", [16, 4])
            dtr = sb("dtr", [NH, NTOK])
            ir = sb("ir", [MH, NTOK])
            fr = sb("fr", [MH, NTOK])
            t1 = sb("t1", [NH, NTOK])
            t2 = sb("t2", [NH, NTOK])
            t3 = sb("t3", [MH, NTOK])
            nacs = sb("nacs", [NH, NTOK])
            bcs = sb("bcs", [MH, NTOK])
            mrun = sb("mrun", [MH, NTOK])
            wlog = sb("wlog", [MH, NTOK])
            mt = sb("mt", [MH, NTOK])
            ones = sb("ones", [16, CH])
            zros = sb("zros", [16, CH])
            mcar = sb("mcar", [MH, NCH + 1])
            m0s = sb("m0s", [MH, NSMP])
            ea = sb("ea", [NH, 1])
            kk_ = [sb(f"wqt{i}", [P, D]) for i in range(2)]
            kyt = [sb(f"kyt{i}", [P, NK]) for i in range(2)]
            wps = [sb(f"wps{i}", [P, KD, NK]) for i in range(2)]

            s_x, s_wr, s_gb = sem("x_loaded"), sem("wrow_loaded"), sem("gate_bias_loaded")
            s_w = [sem(f"chan_weights_loaded{i}") for i in range(2)]
            s_cw = [sem(f"conv_taps_loaded{i}") for i in range(2)]
            s_mm = [sem(f"chan_product{i}") for i in range(2)]
            s_ev = [sem(f"chan_evacuated{i}") for i in range(2)]
            s_cv = [sem(f"convolved{i}") for i in range(2)]
            s_si = [sem(f"silu_done{i}") for i in range(2)]
            s_st = [sem(f"chan_stored{i}") for i in range(2)]
            s_cs = [sem(f"conv_state_stored{i}") for i in range(2)]
            s_rw, s_re, s_z0 = sem("row_product"), sem("row_evacuated"), sem("zeroed")
            s_tw = [sem(f"tok_weights_loaded{i}") for i in range(2)]
            s_tm = [sem(f"tok_product{i}") for i in range(6)]
            s_te = [sem(f"tok_evacuated{i}") for i in range(6)]
            s_ts = [sem(f"tok_stored{i}") for i in range(6)]
            s_pw = [sem(f"wq_loaded{i}") for i in range(2)]
            s_pm = [sem(f"wp_product{i}") for i in range(2)]
            s_pe = [sem(f"wp_evacuated{i}") for i in range(2)]
            s_ps = [sem(f"wp_stored{i}") for i in range(2)]
            s_e1, s_l1, s_rs, s_abs = sem("gate_exp"), sem("gate_log"), sem("rows_stored"), sem("gate_abs")
            s_rr = sem("rows_ready")
            c_d, c_a = sem("dve_chain_a"), sem("act_chain_a")
            s_id0, s_id = sem("ident_zeroed"), sem("ident_ready")

            with nc.Block() as block:
                @block.sync
                def _(sp):
                    sp.dma_start(wrow[:, :, :], a["w_row"]).then_inc(s_wr, 16)
                    for k in range(KD):
                        sp.dma_start(xT[:, k, :], a["x_t"][:, k, :]).then_inc(s_x, 16)
                    sp.dma_start(gb[:, :], a["gate_b"]).then_inc(s_gb, 16)
                    sp.dma_start(m0s[:, :], a["m_state"]).then_inc(s_gb, 16)
                    for i in steps(sp, NCT // 2):
                        for q in range(2):
                            j = 2 * i + q
                            sp.wait_ge(s_mm[q], i)
                            sp.dma_start(wch[q][:, :, :], a["w_ch"][j, :, :, :]).then_inc(s_w[q], 16)
                            sp.wait_ge(s_cv[q], i)
                            sp.dma_start(cw[q][:, :], a["conv_w"][j, :, :]).then_inc(s_cw[q], 16)
                            sp.wait_ge(s_cs[q], 32 * i)
                            sp.dma_start(xps[q][:, 0:3, :], a["conv_s"][j, :, :, :]).then_inc(s_cw[q], 16)
                    for i in steps(sp, 3):
                        for q in range(2):
                            sp.wait_ge(s_tm[(2, 5)[q]], 3 * i)
                            sp.dma_start(wtk[q][:, :, :], a["w_tok"][2 * i + q, :, :, :]).then_inc(s_tw[q], 16)
                    for i in steps(sp, NHC // 2):
                        for q in range(2):
                            j = 2 * i + q
                            sp.wait_ge(s_pm[q], i)
                            sp.dma_start(kk_[q][:, :], a["wq_t"][j, :, :]).then_inc(s_pw[q], 16)
                            sp.dma_start(kyt[q][:, :], a["keys_t"][j, :, :]).then_inc(s_pw[q], 16)

                @block.tensor
                def _(pe):
                    pe.wait_ge(s_x, 16 * KD)
                    pe.wait_ge(s_wr, 16)
                    for out, lo, n in ((PB[:, 6, :], 0, 512), (PB[:, 7, :], 512, 512),
                                       (PB[:, 5, 256:256 + NSMP], SEQ, NSMP)):
                        for k in range(KD):
                            last = nc.tensor.matmul(out, wrow[:, k, :], xT[:, k, lo:lo + n],
                                                    start=k == 0, stop=k == KD - 1)
                    last.then_inc(s_rw, 1)
                    pe.wait_ge(s_re, 1)
                    for i in steps(pe, NCT // 2):
                        for q in range(2):
                            pe.wait_ge(s_w[q], 16 * (i + 1))
                            pe.wait_ge(s_ev[q], i)
                            for out, lo, n in ((PB[:, 3 * q, :], 0, 512), (PB[:, 3 * q + 1, :], 512, 512),
                                               (PB[:, 3 * q + 2, 0:NSMP], SEQ, NSMP)):
                                for k in range(KD):
                                    last = nc.tensor.matmul(out, wch[q][:, k, :], xT[:, k, lo:lo + n],
                                                            start=k == 0, stop=k == KD - 1)
                            last.then_inc(s_mm[q], 1)
                    for q in range(2):
                        pe.wait_ge(s_ev[q], NCT // 2)
                    for i in steps(pe, 3):
                        for u in range(18):
                            q, t, b = u // 9, u % 9, u % 6
                            n = CH if t < NCH else NSMP
                            if t == 0:
                                pe.wait_ge(s_tw[q], 16 * (i + 1))
                            pe.wait_ge(s_te[b], 3 * i + u // 6)
                            for k in range(KD):
                                last = nc.tensor.matmul(PB[0:n, b, :], xT[:, k, t * CH:t * CH + n],
                                                        wtk[q][:, k, :], start=k == 0, stop=k == KD - 1)
                            last.then_inc(s_tm[b], 1)
                    for b in range(6):
                        pe.wait_ge(s_te[b], 9)
                    for i in steps(pe, NHC // 2):
                        for q in range(2):
                            pe.wait_ge(s_pw[q], 32 * (i + 1))
                            pe.wait_ge(s_pe[q], i)
                            for k in range(KD):
                                last = nc.tensor.matmul(two(4 * q)[:, k * NK:(k + 1) * NK],
                                                        kk_[q][:, k * P:(k + 1) * P], kyt[q][:, :],
                                                        start=True, stop=True)
                            last.then_inc(s_pm[q], 1)

                @block.scalar
                def _(act):
                    act.wait_ge(s_rw, 1)
                    for lo, n, src in ((0, 512, PB[:, 6, :]), (512, 512, PB[:, 7, :]),
                                       (SEQ, NSMP, PB[:, 5, 256:256 + NSMP])):
                        nc.scalar.copy(dtr[:, lo:lo + n], src[0:16, :])
                        nc.scalar.copy(ir[:, lo:lo + n], src[32:36, :])
                        last = nc.scalar.copy(fr[:, lo:lo + n], src[64:68, :])
                    last.then_inc(s_re, 1)
                    act.wait_ge(s_abs, 1)
                    ch = Chain(act, c_a)
                    nc.scalar.activation(t1[:, :], t1[:, :], ACT.Exp, scale=-1.0)
                    nc.scalar.activation(ea[:, :], gb[0:NH, 3:4], ACT.Exp)
                    ch.link(nc.scalar.activation(t3[:, :], t3[:, :], ACT.Exp, scale=-1.0))
                    nc.scalar.activation(t1[:, :], t1[:, :], ACT.Ln, bias=1.0)
                    nc.scalar.activation(t3[:, :], t3[:, :], ACT.Ln, bias=1.0).then_inc(s_l1, 1)
                    act.wait_ge(s_z0, 1)
                    for i in steps(act, NCT // 2):
                        for q in range(2):
                            act.wait_ge(s_mm[q], i + 1)
                            act.wait_ge(s_cv[q], i)
                            act.wait_ge(s_cs[q], 32 * i)
                            nc.scalar.copy(xp[q][:, 3:3 + SEQ], two(3 * q))
                            nc.scalar.copy(xps[q][:, 3, :], PB[:, 3 * q + 2, 0:NSMP]).then_inc(s_ev[q], 1)
                            act.wait_ge(s_ev[q], i + 1)
                            act.wait_ge(s_cw[q], 32 * (i + 1))
                            act.dma_start(o["conv_p"][2 * i + q, :, :], xp[q][:, SEQ:SEQ + 3]).then_inc(s_cs[q], 16)
                            act.dma_start(o["conv_s"][2 * i + q, :, :, :], xps[q][:, 1:4, :]).then_inc(s_cs[q], 16)
                            act.wait_ge(s_cv[q], i + 1)
                            act.wait_ge(s_st[q], 16 * i)
                            nc.scalar.activation(so[q][:, :], cv[q][:, :], ACT.Silu).then_inc(s_si[q], 1)
                            act.wait_ge(s_si[q], i + 1)
                            act.dma_start(cht_d[2 * i + q, :, :], so[q][:, :]).then_inc(s_st[q], 16)
                    for i in steps(act, 3):
                        for u in range(18):
                            q, t, b = u // 9, u % 9, u % 6
                            n = CH if t < NCH else NSMP
                            act.wait_ge(s_tm[b], 3 * i + u // 6 + 1)
                            act.wait_ge(s_ts[b], 16 * (3 * i + u // 6))
                            nc.scalar.copy(stg[b][0:n, :], PB[0:n, b, :]).then_inc(s_te[b], 1)
                            act.wait_ge(s_te[b], 3 * i + u // 6 + 1)
                            act.dma_start(tok_d[2 * i + q, t * CH:t * CH + n, :], stg[b][0:n, :]).then_inc(s_ts[b], 16)
                    for i in steps(act, NHC // 2):
                        for q in range(2):
                            act.wait_ge(s_pm[q], i + 1)
                            act.wait_ge(s_ps[q], 16 * i)
                            nc.scalar.copy(wps[q][:, :, :].rearrange("p k n -> p (k n)"), two(4 * q)).then_inc(s_pe[q], 1)
                            act.wait_ge(s_pe[q], i + 1)
                            act.dma_start(wp_d[2 * i + q, :, :, :], wps[q][:, :, :]).then_inc(s_ps[q], 16)
                    act.wait_ge(s_rr, 1)
                    for src, r, n in ((nacs, R_NACS, NH), (mrun, R_M, MH), (wlog, R_WLOG, MH),
                                      (dtr, R_DT, NH), (ir, R_G, MH), (mt, R_MT, MH)):
                        act.dma_start(rows_d[r:r + n, :], src[0:n, 0:SEQ]).then_inc(s_rs, 16)
                        act.dma_start(rows_s_d[r:r + n, :], src[0:n, SEQ:NTOK]).then_inc(s_rs, 16)
                    act.dma_start(o["p_m"], mcar[:, NCH:NCH + 1]).then_inc(s_rs, 16)
                    act.dma_start(o["s_m"], mt[:, SEQ:NTOK]).then_inc(s_rs, 16)
                    act.wait_ge(s_rs, 16 * 14)
                    for q in range(2):
                        act.wait_ge(s_st[q], 16 * NCT // 2)
                        act.wait_ge(s_cs[q], 32 * NCT // 2)
                        act.wait_ge(s_ps[q], 16 * NHC // 2)
                    for b in range(6):
                        act.wait_ge(s_ts[b], 16 * 9)

                @block.gpsimd
                def _(pool):
                    nc.gpsimd.memset(ident[:, :], 0.0).then_inc(s_id0, 1)
                    pool.wait_ge(s_id0, 1)
                    nc.gpsimd.affine_select(out=ident[:, :], in_=ident[:, :], compare_op=ALU.not_equal, fill=1.0,
                                            base=0, pattern=[[-1, P]], channel_multiplier=1).then_inc(s_id, 1)
                    pool.wait_ge(s_id, 1)

                @block.vector
                def _(dve):
                    ch = Chain(dve, c_d)
                    for q in range(2):
                        nc.vector.memset(xp[q][:, 0:3], 0.0)
                    nc.vector.memset(mcar[:, 0:1], 0.0)
                    nc.vector.memset(ones[:, :], 1.0)
                    nc.vector.memset(zros[:, :], 0.0).then_inc(s_z0, 1)
                    dve.wait_ge(s_z0, 1)
                    dve.wait_ge(s_re, 1)
                    dve.wait_ge(s_gb, 32)
                    nc.vector.tensor_scalar(dtr[:, :], dtr[:, :], gb[0:NH, 0:1], None, ALU.add)
                    nc.vector.tensor_scalar(ir[:, :], ir[:, :], gb[0:MH, 1:2], None, ALU.add)
                    ch.link(nc.vector.tensor_scalar(fr[:, :], fr[:, :], gb[0:MH, 2:3], None, ALU.add))
                    nc.vector.scalar_tensor_tensor(t1[:, :], dtr[:, :], -1.0, dtr[:, :], ALU.mult, ALU.max)
                    nc.vector.scalar_tensor_tensor(t3[:, :], fr[:, :], -1.0, fr[:, :], ALU.mult, ALU.max).then_inc(s_abs, 1)
                    dve.wait_ge(s_l1, 1)
                    nc.vector.scalar_tensor_tensor(dtr[:, :], dtr[:, :], 0.0, t1[:, :], ALU.max, ALU.add)
                    ch.link(nc.vector.scalar_tensor_tensor(fr[:, :], fr[:, :], 0.0, t3[:, :], ALU.min, ALU.subtract))
                    ch.link(nc.vector.tensor_scalar(t2[:, :], dtr[:, :], ea[:, :], None, ALU.mult))
                    for c in range(NCH):
                        s = slice(c * CH, (c + 1) * CH)
                        nc.vector.tensor_tensor_scan(nacs[:, s], ones[0:NH, :], t2[:, s], 0.0, ALU.mult, ALU.add)
                        nc.vector.tensor_tensor_scan(bcs[:, s], ones[0:MH, :], fr[:, s], 0.0, ALU.mult, ALU.add)
                    nc.vector.tensor_copy(nacs[:, SEQ:NTOK], t2[:, SEQ:NTOK])
                    ch.link(nc.vector.tensor_copy(bcs[:, SEQ:NTOK], fr[:, SEQ:NTOK]))
                    ch.link(nc.vector.tensor_tensor(ir[:, :], ir[:, :], bcs[:, :], ALU.subtract))
                    for c in range(NCH):
                        s, e = slice(c * CH, (c + 1) * CH), (c + 1) * CH - 1
                        ch.link(nc.vector.tensor_tensor_scan(mrun[:, s], zros[0:MH, :], ir[:, s], mcar[:, c:c + 1],
                                                             ALU.add, ALU.max))
                        nc.vector.tensor_scalar(wlog[:, s], mrun[:, s], -1.0, mcar[:, c:c + 1], ALU.mult, ALU.add)
                        ch.link(nc.vector.tensor_tensor(mcar[:, c + 1:c + 2], mrun[:, e:e + 1], bcs[:, e:e + 1], ALU.add))
                    s = slice(SEQ, NTOK)
                    ch.link(nc.vector.tensor_tensor(mrun[:, s], m0s[:, :], ir[:, s], ALU.max))
                    nc.vector.tensor_tensor(wlog[:, s], m0s[:, :], mrun[:, s], ALU.subtract)
                    nc.vector.tensor_tensor(mt[:, :], mrun[:, :], bcs[:, :], ALU.add).then_inc(s_rr, 1)
                    for i in steps(dve, NCT // 2):
                        cc = Chain(dve, s_e1, 6 * i)
                        for q in range(2):
                            dve.wait_ge(s_ev[q], i + 1)
                            dve.wait_ge(s_cw[q], 32 * (i + 1))
                            dve.wait_ge(s_si[q], i)
                            for tap in range(TAPS):
                                w = cw[q][:, tap:tap + 1]
                                for out, src in ((cv[q][:, 0:SEQ], xp[q][:, tap:tap + SEQ]),
                                                 (cv[q][:, SEQ:NTOK], xps[q][:, tap, :])):
                                    if tap == 0:
                                        last = nc.vector.tensor_scalar(out, src, w, cw[q][:, 4:5], ALU.mult, ALU.add)
                                    else:
                                        last = nc.vector.scalar_tensor_tensor(out, src, w, out, ALU.mult, ALU.add)
                                if tap < TAPS - 1:
                                    cc.link(last)
                            last.then_inc(s_cv[q], 1)

        end_phase()

        with ExitStack() as ctx:
            def sb(name, shape, dt=f32):
                return ctx.enter_context(nc.sbuf_tensor(name, shape, dt))

            wmq = sb("wmq", [P, MH, KT, DK])
            wmk = sb("wmk", [P, MH, KT, DK])
            cht = sb("cht", [P, NCT, CH])
            zvo = sb("zvo", [P, 6, 512])
            rows = sb("rows", [NROW, CH])
            rb = sb("rb", [P, R_DT, CH])
            L = sb("L", [P, NH + MH, CH])
            maskp = sb("maskp", [P, CH])
            onec = sb("onec", [P, 1])
            cols = sb("cols", [P, NROW])
            btok = sb("btok", [P, NG * NST])
            xtok = sb("xtok", [P, D])
            xdt = sb("xdt", [P, D])
            xdec = sb("xdec", [P, D])
            qT = sb("qT", [P, MH * KT, CH])
            kT = sb("kT", [P, MH * KT, CH])
            kw = sb("kw", [P, D])
            hT = sb("hT", [P, D])
            cst = sb("cst", [P, MH * KT, DK])
            nst = sb("nst", [P, MH * KT])
            sm = sb("sm", [P, 64])
            e_ea, e_wi, e_em = sm[:, 0:16], sm[:, 16:20], sm[:, 20:24]
            e_hd, e_wo = sb("e_hd", [P, NH]), sb("e_wo", [P, MH])
            e_de, e_ws = sb("e_de", [P, NH]), sb("e_ws", [P, MH])
            ysb = sb("ysb", [P, D])
            tmp = sb("tmp", [P, D])
            ez = sb("ez", [P, 2 * D])
            nx = sb("nx", [P, D])
            den = sb("den", [P, 8])
            num = sb("num", [P, D])
            stt = sb("stt", [P, MH, 6])
            mv = sb("mv", [P, MH, 2])
            var = sb("var", [P, 5])
            mix = sb("mix", [P, 2 * D])
            mixT = sb("mixT", [P, 16, CH])
            gs = sb("gs", [P, D])
            gm = sb("gm", [P, D])
            dsk = sb("dsk", [P, NH])
            epst = sb("epst", [P, 1])

            names = ("w ch tok rows rb pe_a pe_b pe_kk pe_st pe_ys pe_hn pe_y pe_ni pe_nx pe_c1 pe_c2 pe_tr "
                     "act_xt act_small act_qk act_l act_l2 act_ez act_nx act_sq act_mt stored "
                     "dve_arg dve_d dve_xdec dve_h dve_mm dve_kw dve_att dve_ys dve_y dve_c1 dve_c2 "
                     "dve_num dve_var dve_mix dve_end setup mask0 outs passed")
            s = {n: sem("scan_" + n) for n in names.split()}
            c_d, c_a = sem("dve_chain_s"), sem("act_chain_s")
            DVE_LINKS, ACT_LINKS = 19, 0

            def heads(ap, n):
                return ap.rearrange("p (h n) -> p h n", n=n)

            def scan_vector(dve, i):
                ch = Chain(dve, c_d, DVE_LINKS * i, s["passed"])
                V = nc.vector
                dve.wait_ge(s["act_xt"], i + 1)
                dve.wait_ge(s["rb"], 16 * (i + 1))
                dve.wait_ge(s["act_small"], i)
                V.tensor_tensor(e_de[:, :], cols[:, R_NACS:R_NACS + NH], rb[:, R_NACS:R_NACS + NH, CH - 1], ALU.subtract)
                V.tensor_tensor(e_ws[:, :], cols[:, R_G:R_G + MH], rb[:, R_M:R_M + MH, CH - 1], ALU.subtract).then_inc(s["dve_arg"], 1)
                dve.wait_ge(s["pe_ni"], i)
                V.tensor_tensor(L[:, :, :], rb[:, 0:NH + MH, :], maskp[:, :].unsqueeze(1).to_broadcast([P, NH + MH, CH]), ALU.add).then_inc(s["dve_d"], 1)
                dve.wait_ge(s["pe_y"], i)
                ch.link(V.tensor_tensor(heads(xdt[:, :], HD), heads(xtok[:, :], HD),
                                        cols[:, R_DT:R_DT + NH].unsqueeze(2).to_broadcast([P, NH, HD]), ALU.mult))
                dve.wait_ge(s["act_small"], i + 1)
                V.tensor_tensor(heads(xdec[:, :], HD), heads(xdt[:, :], HD),
                                e_de[:, :].unsqueeze(2).to_broadcast([P, NH, HD]), ALU.mult).then_inc(s["dve_xdec"], 1)
                dve.wait_ge(s["pe_kk"], i + 1)
                V.scalar_tensor_tensor(heads(kw[:, :], DK), heads(two(0), DK), DK ** -0.5,
                                       e_ws[:, :].unsqueeze(2).to_broadcast([P, MH, DK]), ALU.mult, ALU.mult).then_inc(s["dve_kw"], 1)
                dve.wait_ge(s["act_l"], i + 1)
                for g in range(NG):
                    last = V.tensor_tensor(L[:, g * 8:g * 8 + 8, :], L[:, g * 8:g * 8 + 8, :],
                                           PB[:, 3, g * CH:(g + 1) * CH].unsqueeze(1).to_broadcast([P, 8, CH]), ALU.mult)
                last.then_inc(s["dve_mm"], 1)
                dve.wait_ge(s["pe_st"], i + 1)
                dve.wait_ge(s["act_l2"], i + 1)
                V.tensor_tensor(L[:, NH:NH + MH, :], L[:, NH:NH + MH, :], heads(PB[:, 2, :], CH), ALU.mult).then_inc(s["dve_att"], 1)
                dve.wait_ge(s["pe_ys"], i + 1)
                V.tensor_tensor(heads(ysb[:, :], HD), heads(two(4), HD),
                                e_ea.unsqueeze(2).to_broadcast([P, NH, HD]), ALU.mult).then_inc(s["dve_ys"], 1)
                dve.wait_ge(s["dve_ys"], i + 1)
                V.tensor_tensor(heads(tmp[:, :], HD), heads(xtok[:, :], HD),
                                dsk[:, :].unsqueeze(2).to_broadcast([P, NH, HD]), ALU.mult)
                ch.link(V.tensor_tensor(heads(hT[:, :], HD), heads(hT[:, :], HD),
                                        e_hd[:, :].unsqueeze(2).to_broadcast([P, NH, HD]), ALU.mult))
                dve.wait_ge(s["pe_hn"], i + 1)
                V.tensor_tensor(hT[:, :], hT[:, :], two(6), ALU.add).then_inc(s["dve_h"], 1)
                ch.link(V.tensor_tensor(ysb[:, :], ysb[:, :], tmp[:, :], ALU.add))
                dve.wait_ge(s["pe_y"], i + 1)
                V.tensor_tensor(ysb[:, :], ysb[:, :], two(0), ALU.add).then_inc(s["dve_y"], 1)
                dve.wait_ge(s["dve_y"], i + 1)
                dve.wait_ge(s["act_ez"], i + 1)
                gate_z(dve, ch, P)
                dve.wait_ge(s["pe_ni"], i + 1)
                dve.wait_ge(s["act_nx"], i + 1)
                V.tensor_tensor(num[:, :], two(4), nx[:, :], ALU.add).then_inc(s["dve_num"], 1)
                ch.link(V.tensor_tensor(den[:, 0:4], PB[:, 3, 4:8], e_wi, ALU.mult))
                ch.link(V.tensor_tensor(den[:, 0:4], den[:, 0:4], PB[:, 3, 0:4], ALU.add))
                V.tensor_tensor(cst[:, :, :].rearrange("p (h k) v -> p h (k v)", h=MH),
                                cst[:, :, :].rearrange("p (h k) v -> p h (k v)", h=MH),
                                e_wo[:, :].unsqueeze(2).to_broadcast([P, MH, KT * DK]), ALU.mult)
                ch.link(V.tensor_tensor(heads(nst[:, :], KT), heads(nst[:, :], KT),
                                        e_wo[:, :].unsqueeze(2).to_broadcast([P, MH, KT]), ALU.mult))
                dve.wait_ge(s["pe_c1"], i + 1)
                V.tensor_tensor(nst[:, :], nst[:, :], PB[:, 2, 0:8], ALU.add)
                V.tensor_tensor(cst[:, 0:4, :].rearrange("p a v -> p (a v)"), cst[:, 0:4, :].rearrange("p a v -> p (a v)"),
                                two(0), ALU.add).then_inc(s["dve_c1"], 1)
                dve.wait_ge(s["pe_c2"], i + 1)
                V.tensor_tensor(cst[:, 4:8, :].rearrange("p a v -> p (a v)"), cst[:, 4:8, :].rearrange("p a v -> p (a v)"),
                                two(4), ALU.add).then_inc(s["dve_c2"], 1)
                head_out(dve, ch, P, i)
                assert ch.n == DVE_LINKS, ch.n

            def gate_z(dve, ch, r):
                V = nc.vector
                ch.link(V.tensor_scalar(ez[0:r, :], ez[0:r, :], 1.0, None, ALU.add))
                ch.link(V.reciprocal(ez[0:r, :], ez[0:r, :]))
                z = zvo[0:r, 0:2, :].rearrange("p a n -> p (a n)")
                ch.link(V.tensor_tensor(tmp[0:r, :], ez[0:r, 0:D], z, ALU.mult))
                ch.link(V.tensor_tensor(ysb[0:r, :], ysb[0:r, :], tmp[0:r, :], ALU.mult))
                V.tensor_tensor_reduce(out=tmp[0:r, :], in0=ysb[0:r, :], in1=ysb[0:r, :], scale=1.0 / D, scalar=EPS,
                                       op0=ALU.mult, op1=ALU.add, accum_out=var[0:r, 0:1])

            def head_out(dve, ch, r, i):
                V = nc.vector
                ch.link(V.scalar_tensor_tensor(den[0:r, 4:8], den[0:r, 0:4], -1.0, den[0:r, 0:4], ALU.mult, ALU.max))
                ch.link(V.tensor_tensor(den[0:r, 4:8], den[0:r, 4:8], e_em[0:r, :], ALU.max))
                ch.link(V.reciprocal(den[0:r, 4:8], den[0:r, 4:8]))
                ch.link(V.tensor_tensor(heads(num[0:r, :], DK), heads(num[0:r, :], DK),
                                        den[0:r, 4:8].unsqueeze(2).to_broadcast([r, MH, DK]), ALU.mult))
                for h in range(MH):
                    last = V.bn_stats(stt[0:r, h, :], num[0:r, h * DK:(h + 1) * DK])
                ch.link_plain(last)
                for h in range(MH):
                    last = V.bn_aggr(mv[0:r, h, :], stt[0:r, h, :])
                ch.link(last)
                V.tensor_scalar(var[0:r, 1:5], mv[0:r, :, 1], EPS, None, ALU.add).then_inc(s["dve_var"], 1)
                dve.wait_ge(s["act_sq"], i + 1)
                ch.link(V.reciprocal(var[0:r, :], var[0:r, :]))
                dve.wait_ge(s["pe_tr"], i)
                V.scalar_tensor_tensor(mix[0:r, 0:D], ysb[0:r, :], var[0:r, 0:1], gs[0:r, :], ALU.mult, ALU.mult)
                for h in range(MH):
                    last = V.tensor_scalar(num[0:r, h * DK:(h + 1) * DK], num[0:r, h * DK:(h + 1) * DK],
                                           mv[0:r, h, 0:1], var[0:r, 1 + h:2 + h], ALU.subtract, ALU.mult)
                ch.link(last)
                ch.link(V.tensor_tensor(num[0:r, :], num[0:r, :], gm[0:r, :], ALU.mult))
                V.tensor_tensor(mix[0:r, D:2 * D], num[0:r, :], ez[0:r, D:2 * D], ALU.mult).then_inc(s["dve_mix"], 1)

            def sqrt_step(act, r, i):
                act.wait_ge(s["dve_var"], i + 1)
                nc.scalar.activation(var[0:r, :], var[0:r, :], ACT.Sqrt).then_inc(s["act_sq"], 1)

            def mix_transposes(pe, r, i):
                pe.wait_ge(s["dve_mix"], i + 1)
                for j in range(16):
                    b = (0, 1, 6, 7)[j // 4]
                    last = nc.tensor.transpose(PB[:, b, (j % 4) * CH:(j % 4) * CH + r], mix[0:r, j * P:(j + 1) * P], ident[0:r, 0:r])
                last.then_inc(s["pe_tr"], 1)

            def mix_store(act, r, i, lo):
                act.wait_ge(s["pe_tr"], i + 1)
                act.wait_ge(s["stored"], 16 * i)
                for b, j in ((0, 0), (1, 4), (6, 8), (7, 12)):
                    last = nc.scalar.copy(mixT[:, j:j + 4, 0:r], PB[:, b, :].rearrange("p (a n) -> p a n", n=CH)[:, :, 0:r])
                last.then_inc(s["act_mt"], 1)
                act.wait_ge(s["act_mt"], i + 1)
                act.dma_start(mixt_d[:, :, bass.ds(lo, r)].rearrange("j p t -> p j t"), mixT[:, :, 0:r]).then_inc(s["stored"], 16)

            with nc.Block() as block:
                @block.sync
                def _(sp):
                    sp.dma_start(wmq[:, :, :, :], a["w_mq"]).then_inc(s["w"], 16)
                    sp.dma_start(wmk[:, :, :, :], a["w_mk"]).then_inc(s["w"], 16)
                    sp.dma_start(gs[:, :], a["ssd_g"].partition_broadcast(P)).then_inc(s["w"], 16)
                    sp.dma_start(gm[:, :], a["mlstm_g"].partition_broadcast(P)).then_inc(s["w"], 16)
                    sp.dma_start(dsk[:, :], a["d_skip"].partition_broadcast(P)).then_inc(s["w"], 16)
                    for i in steps(sp, NCH):
                        sp.wait_ge(s["pe_a"], i)
                        sp.dma_start(rows[:, :], rows_d[:, bass.ds(i * CH, CH)]).then_inc(s["rows"], 16)
                        sp.wait_ge(s["pe_ys"], i)
                        sp.dma_start(cht[:, :, :], cht_d[:, :, bass.ds(i * CH, CH)].rearrange("j p t -> p j t")).then_inc(s["ch"], 16)
                        sp.wait_ge(s["dve_d"], i)
                        sp.wait_ge(s["act_small"], i)
                        sp.dma_start(rb[:, :, :], rows_d[0:R_DT, bass.ds(i * CH, CH)].partition_broadcast(P)).then_inc(s["rb"], 16)
                        sp.wait_ge(s["pe_c2"], i)
                        sp.wait_ge(s["dve_mix"], i)
                        sp.dma_start(zvo[:, :, :], tok_d[:, bass.ds(i * CH, CH), :].rearrange("j t n -> t j n")).then_inc(s["tok"], 16)

                @block.tensor
                def _(pe):
                    pe.wait_ge(s["w"], 80)
                    pe.wait_ge(s["setup"], 1)
                    T = nc.tensor
                    for i in steps(pe, NCH):
                        v = zvo[:, 2:4, :].rearrange("p a n -> p (a n)")
                        pe.wait_ge(s["act_mt"], i)
                        pe.wait_ge(s["dve_mix"], i)
                        pe.wait_ge(s["rows"], 16 * (i + 1))
                        pe.sem_inc(s["passed"], 1)
                        T.transpose(PB[:, 2, 256:256 + NROW], rows[:, :], ident[0:NROW, 0:NROW])
                        pe.wait_ge(s["ch"], 16 * (i + 1))
                        for g in range(NG):
                            T.transpose(PB[:, 2, g * NST:(g + 1) * NST], cht[:, BT0 + g, :], ident[:, :])
                        for j in range(8):
                            T.transpose(two(0)[:, j * P:(j + 1) * P], cht[:, j, :], ident[:, :])
                        for g in range(NG):
                            last = T.matmul(PB[:, 3, g * CH:(g + 1) * CH], cht[:, BT0 + g, :], cht[:, CT0 + g, :], start=True, stop=True)
                        last.then_inc(s["pe_a"], 1)
                        for w, b in ((wmq, 4), (wmk, 6)):
                            for h in range(MH):
                                for e in range(KT):
                                    for k in range(KT):
                                        last = T.matmul(two(b)[:, (h * KT + e) * CH:(h * KT + e + 1) * CH],
                                                        w[:, h, k, e * P:(e + 1) * P], cht[:, UT0 + h * KT + k, :],
                                                        start=k == 0, stop=k == KT - 1)
                        last.then_inc(s["pe_b"], 1)
                        pe.wait_ge(s["act_xt"], i + 1)
                        for h in range(MH):
                            for k in range(KT):
                                last = T.matmul(two(0)[:, h * DK:(h + 1) * DK], cht[:, UT0 + h * KT + k, :], wmk[:, h, k, :],
                                                start=k == 0, stop=k == KT - 1)
                        last.then_inc(s["pe_kk"], 1)
                        pe.wait_ge(s["act_qk"], i + 1)
                        for h in range(MH):
                            for k in range(KT):
                                last = T.matmul(PB[:, 2, h * CH:(h + 1) * CH], kT[:, h * KT + k, :], qT[:, h * KT + k, :],
                                                start=k == 0, stop=k == KT - 1)
                        last.then_inc(s["pe_st"], 1)
                        for g in range(NG):
                            last = T.matmul(PB[:, 4 + g, :], cht[:, CT0 + g, :], hT[:, g * 512:(g + 1) * 512], start=True, stop=True)
                        last.then_inc(s["pe_ys"], 1)
                        pe.wait_ge(s["dve_xdec"], i + 1)
                        for g in range(NG):
                            last = T.matmul(PB[:, 6 + g, :], btok[:, g * NST:(g + 1) * NST], xdec[:, g * 512:(g + 1) * 512], start=True, stop=True)
                        last.then_inc(s["pe_hn"], 1)
                        pe.wait_ge(s["dve_mm"], i + 1)
                        pe.wait_ge(s["dve_kw"], i + 1)
                        for h in range(NH):
                            last = T.matmul(two(0)[:, h * HD:(h + 1) * HD], L[:, h, :], xdt[:, h * HD:(h + 1) * HD], start=True, stop=True)
                        last.then_inc(s["pe_y"], 1)
                        pe.wait_ge(s["dve_h"], i + 1)
                        pe.wait_ge(s["tok"], 16 * (i + 1))
                        for h in range(MH):
                            for k in range(KT):
                                last = T.matmul(two(6)[:, h * DK:(h + 1) * DK], qT[:, h * KT + k, :], cst[:, h * KT + k, :],
                                                start=k == 0, stop=k == KT - 1)
                        for h in range(MH):
                            for k in range(KT):
                                last = T.matmul(PB[:, 3, 4 + h:5 + h], qT[:, h * KT + k, :], nst[:, h * KT + k:h * KT + k + 1],
                                                start=k == 0, stop=k == KT - 1)
                        last.then_inc(s["pe_nx"], 1)
                        pe.wait_ge(s["dve_att"], i + 1)
                        pe.wait_ge(s["dve_ys"], i + 1)
                        for h in range(MH):
                            last = T.matmul(two(4)[:, h * DK:(h + 1) * DK], L[:, NH + h, :], v[:, h * DK:(h + 1) * DK], start=True, stop=True)
                        for h in range(MH):
                            last = T.matmul(PB[:, 3, h:h + 1], L[:, NH + h, :], onec[:, :], start=True, stop=True)
                        last.then_inc(s["pe_ni"], 1)
                        pe.wait_ge(s["dve_y"], i + 1)
                        for h in range(MH):
                            for k in range(KT):
                                j = h * KT + k
                                T.matmul(PB[:, 2, j:j + 1], kw[:, j * P:(j + 1) * P], onec[:, :], start=True, stop=True)
                        for j in range(4):
                            h = j // KT
                            last = T.matmul(two(0)[:, j * DK:(j + 1) * DK], kw[:, j * P:(j + 1) * P], v[:, h * DK:(h + 1) * DK], start=True, stop=True)
                        last.then_inc(s["pe_c1"], 1)
                        pe.wait_ge(s["dve_num"], i + 1)
                        for j in range(4, 8):
                            h = j // KT
                            last = T.matmul(two(4)[:, (j - 4) * DK:(j - 3) * DK], kw[:, j * P:(j + 1) * P], v[:, h * DK:(h + 1) * DK], start=True, stop=True)
                        last.then_inc(s["pe_c2"], 1)
                        pe.wait_ge(s["dve_c1"], i + 1)
                        mix_transposes(pe, P, i)

                @block.scalar
                def _(act):
                    S = nc.scalar
                    act.wait_ge(s["setup"], 1)
                    for i in steps(act, NCH):
                        ch = Chain(act, c_a, ACT_LINKS * i)
                        act.wait_ge(s["pe_a"], i + 1)
                        act.wait_ge(s["dve_mix"], i)
                        act.wait_ge(s["pe_hn"], i)
                        S.copy(cols[:, :], PB[:, 2, 256:256 + NROW])
                        S.copy(btok[:, :], PB[:, 2, 0:256])
                        S.copy(xtok[:, :], two(0)).then_inc(s["act_xt"], 1)
                        act.wait_ge(s["act_xt"], i + 1)
                        act.wait_ge(s["pe_b"], i + 1)
                        S.copy(qT[:, :, :].rearrange("p a n -> p (a n)"), two(4))
                        S.activation(kT[:, :, :].rearrange("p a n -> p (a n)"), two(6), ACT.Copy, scale=DK ** -0.5).then_inc(s["act_qk"], 1)
                        act.wait_ge(s["rb"], 16 * (i + 1))
                        S.activation(e_ea, cols[:, R_NACS:R_NACS + NH], ACT.Exp, scale=-1.0)
                        S.activation(e_wi, cols[:, R_WLOG:R_WLOG + MH], ACT.Exp)
                        S.activation(e_em, cols[:, R_MT:R_MT + MH], ACT.Exp, scale=-1.0)
                        S.activation(e_hd[:, :], rb[:, R_NACS:R_NACS + NH, CH - 1], ACT.Exp, scale=-1.0)
                        S.activation(e_wo[:, :], rb[:, R_WLOG:R_WLOG + MH, CH - 1], ACT.Exp)
                        act.wait_ge(s["dve_arg"], i + 1)
                        S.activation(e_de[:, :], e_de[:, :], ACT.Exp)
                        S.activation(e_ws[:, :], e_ws[:, :], ACT.Exp).then_inc(s["act_small"], 1)
                        act.wait_ge(s["dve_d"], i + 1)
                        for h in range(NH):
                            last = S.activation(L[:, h, :], L[:, h, :], ACT.Exp, scale=-1.0, bias=cols[:, R_NACS + h:R_NACS + h + 1])
                        last.then_inc(s["act_l"], 1)
                        for h in range(MH):
                            last = S.activation(L[:, NH + h, :], L[:, NH + h, :], ACT.Exp, scale=-1.0, bias=cols[:, R_G + h:R_G + h + 1])
                        last.then_inc(s["act_l2"], 1)
                        act.wait_ge(s["tok"], 16 * (i + 1))
                        S.activation(ez[:, 0:D], zvo[:, 0:2, :].rearrange("p a n -> p (a n)"), ACT.Exp, scale=-1.0)
                        S.activation(ez[:, D:2 * D], zvo[:, 4:6, :].rearrange("p a n -> p (a n)"), ACT.Exp, scale=-1.0).then_inc(s["act_ez"], 1)
                        act.wait_ge(s["pe_nx"], i + 1)
                        for h in range(MH):
                            last = S.activation(nx[:, h * DK:(h + 1) * DK], two(6)[:, h * DK:(h + 1) * DK], ACT.Copy, scale=e_wi[:, h:h + 1])
                        last.then_inc(s["act_nx"], 1)
                        sqrt_step(act, P, i)
                        mix_store(act, P, i, i * CH)
                    act.wait_ge(s["dve_c2"], NCH)
                    act.dma_start(o["p_ssd"], hT[:, :]).then_inc(s["outs"], 16)
                    act.dma_start(o["p_c"], cst[:, :, :]).then_inc(s["outs"], 16)
                    act.dma_start(o["p_n"], nst[:, :]).then_inc(s["outs"], 16)
                    act.wait_ge(s["outs"], 48)
                    act.wait_ge(s["stored"], 16 * NCH)

                @block.gpsimd
                def _(pool):
                    nc.gpsimd.memset(maskp[:, :], 0.0).then_inc(s["mask0"], 1)
                    pool.wait_ge(s["mask0"], 1)
                    nc.gpsimd.affine_select(out=maskp[:, :], in_=maskp[:, :], compare_op=ALU.is_ge, fill=BIG,
                                            base=0, pattern=[[1, CH]], channel_multiplier=-1).then_inc(s["mask0"], 1)
                    pool.wait_ge(s["mask0"], 2)

                @block.vector
                def _(dve):
                    nc.vector.memset(onec[:, :], 1.0)
                    nc.vector.memset(hT[:, :], 0.0)
                    nc.vector.memset(cst[:, :, :], 0.0)
                    nc.vector.memset(nst[:, :], 0.0).then_inc(s["setup"], 1)
                    dve.wait_ge(s["setup"], 1)
                    dve.wait_ge(s["mask0"], 2)
                    dve.wait_ge(s["w"], 80)
                    for i in steps(dve, NCH):
                        scan_vector(dve, i)
            build_sample(nc, a, o, locals())
        end_phase()
        build_peer(nc, a, o, locals())


def build_sample(nc, a, o, L_):
    f32 = mybir.dt.float32
    ACT = mybir.ActivationFunctionType
    ctx, PB, ident, two, heads, s, sem = (L_[k] for k in ("ctx", "PB", "ident", "two", "heads", "s", "sem"))
    zvo, den, num, ysb, ez, e_em, wmq, wmk, onec = (L_[k] for k in ("zvo", "den", "num", "ysb", "ez", "e_em", "wmq", "wmk", "onec"))
    cht_d, tok_d, rows_s_d, bc_d = (L_[k] for k in ("cht_d", "tok_d", "rows_s_d", "bc_d"))
    gate_z, head_out, sqrt_step, mix_transposes, mix_store = (
        L_[k] for k in ("gate_z", "head_out", "sqrt_step", "mix_transposes", "mix_store"))
    B = NSMP
    i = NCH

    def sb(name, shape, dt=f32):
        return ctx.enter_context(nc.sbuf_tensor(name, shape, dt))

    chs = sb("chs", [P, NCT, B])
    rsb = sb("rsb", [P, NROW, B])
    nas = sb("nas", [P, 8, B])
    dts = sb("dts", [P, 8, B])
    dxt = sb("dxt", [P, 8, B])
    wos, wss = sb("wos", [P, MH, B]), sb("wss", [P, MH, B])
    bcsb = sb("bcsb", [B, 4 * P])
    bb = [sb(f"bb{q}", [P, 4 * P]) for q in range(2)]
    st = [sb(f"st{q}", [P, 8, NST]) for q in range(2)]
    cs = [sb(f"cs{q}", [P, MH * KT, DK]) for q in range(2)]
    vb = [sb(f"vb{q}", [P, D]) for q in range(2)]
    tt = L_["tmp"]
    tc_ = L_["mix"]
    qs, ks = sb("qs", [P, 8, B]), sb("ks", [P, 8, B])
    ns = sb("ns", [P, 8, B])
    pr, pr2 = sb("pr", [P, 8, B]), sb("pr2", [P, 8, B])
    qd = sb("qd", [P, 8, B, B])
    ysc = sb("ysc", [P, 8, B])
    dsc = sb("dsc", [P, 8])
    ss = {n: sem("smp_" + n) for n in ("ld ld2 bct bcc bcd qk qkc exp arg ea1 kws qdz nn nst yt ytc "
                                       "st_new c_new num num_c num_e den_c").split()}
    s_in = [sem(f"smp_states_loaded{q}") for q in range(2)]
    s_out = [sem(f"smp_states_stored{q}") for q in range(2)]
    c_d = sem("dve_chain_smp")

    with nc.Block() as block:
        @block.sync
        def _(sp):
            sp.dma_start(chs[:, :, :], cht_d[:, :, SEQ:NTOK].rearrange("j p t -> p j t")).then_inc(ss["ld"], 16)
            sp.dma_start(rsb[:, :, :], rows_s_d.partition_broadcast(P)).then_inc(ss["ld"], 16)
            for half in range(2):
                sp.dma_start(nas[half * HD:(half + 1) * HD, :, :],
                             rows_s_d[R_NACS:R_NACS + NH, :].rearrange("(j two) b -> two j b", two=2)[half].partition_broadcast(HD)).then_inc(ss["ld"], 16)
                sp.dma_start(dts[half * HD:(half + 1) * HD, :, :],
                             rows_s_d[R_DT:R_DT + NH, :].rearrange("(j two) b -> two j b", two=2)[half].partition_broadcast(HD)).then_inc(ss["ld"], 16)
            sp.dma_start(ns[:, :, :], a["n_state"]).then_inc(ss["ld"], 16)
            sp.dma_start(dsc[:, :], a["d_skip_ch"]).then_inc(ss["ld"], 16)
            sp.dma_start(e_em[0:B, :], rows_s_d[R_MT:R_MT + MH, :].rearrange("h b -> b h"),
                         allow_slow_non_contiguous=True).then_inc(ss["ld"], 16)
            sp.dma_start(zvo[0:B, :, :], tok_d[:, SEQ:NTOK, :].rearrange("j t n -> t j n")).then_inc(ss["ld2"], 16)
            sp.wait_ge(ss["bcd"], 16)
            for b in range(B):
                q, n = b % 2, b // 2
                sp.wait_ge(s_out[q], 32 * n)
                sp.dma_start(st[q][:, :, :], a["ssd_state"][b].rearrange("(j p) n -> p j n", p=P)).then_inc(s_in[q], 16)
                sp.dma_start(cs[q][:, :, :], a["c_state"][b].rearrange("(j p) v -> p j v", p=P)).then_inc(s_in[q], 16)
                sp.dma_start(vb[q][:, :].rearrange("p (j n) -> p j n", j=2),
                             tok_d[2:4, SEQ + b, :].partition_broadcast(P)).then_inc(s_in[q], 16)
                sp.dma_start(bb[q][:, :], bc_d[b].rearrange("a n -> (a n)").partition_broadcast(P)).then_inc(s_in[q], 16)

        @block.tensor
        def _(pe):
            T = nc.tensor
            pe.wait_ge(ss["ld"], 16 * 9)
            for g in range(4):
                last = T.transpose(PB[0:B, 2, g * P:(g + 1) * P], chs[:, BT0 + g, :], ident[:, :])
            last.then_inc(ss["bct"], 1)
            for w, bank in ((wmq, 4), (wmk, 5)):
                for h in range(MH):
                    for e in range(KT):
                        for k in range(KT):
                            last = T.matmul(PB[:, bank, (h * KT + e) * B:(h * KT + e + 1) * B], w[:, h, k, e * P:(e + 1) * P],
                                            chs[:, UT0 + h * KT + k, :], start=k == 0, stop=k == KT - 1)
            last.then_inc(ss["qk"], 1)
            pe.wait_ge(ss["qdz"], 1)
            for b in range(B):
                pe.wait_ge(ss["c_new"], b + 1)
                for h in range(MH):
                    for k in range(KT):
                        j = h * KT + k
                        last = T.matmul(PB[0:B, (0, 1, 6, 7)[h], 0:DK],
                                        qd[:, j, b, :], cs[b % 2][:, j, :],
                                        start=b == 0 and k == 0, stop=b == B - 1 and k == KT - 1)
                last.then_inc(ss["num"], 1)
            pe.wait_ge(ss["nn"], 1)
            for h in range(MH):
                for k in range(KT):
                    last = T.matmul(PB[0:B, 3, h:h + 1], pr[:, h * KT + k, :], onec[:, :], start=k == 0, stop=k == KT - 1)
            pe.wait_ge(ss["yt"], 1)
            for j in range(8):
                last = T.transpose(two(4)[0:B, j * P:(j + 1) * P], ysc[:, j, :], ident[:, :])
            last.then_inc(ss["ytc"], 1)
            pe.wait_ge(ss["num_e"], 1)
            mix_transposes(pe, B, i)

        @block.scalar
        def _(act):
            S = nc.scalar
            act.wait_ge(ss["ld"], 16 * 9)
            S.activation(nas[:, :, :], nas[:, :, :], ACT.Exp, scale=-1.0)
            S.activation(wos[:, :, :], rsb[:, R_WLOG:R_WLOG + MH, :], ACT.Exp)
            S.activation(e_em[0:B, :], e_em[0:B, :], ACT.Exp, scale=-1.0)
            act.wait_ge(ss["arg"], 1)
            S.activation(wss[:, :, :], wss[:, :, :], ACT.Exp).then_inc(ss["exp"], 1)
            act.wait_ge(ss["bct"], 1)
            S.copy(bcsb[:, :], PB[0:B, 2, :]).then_inc(ss["bcc"], 1)
            act.wait_ge(ss["bcc"], 1)
            act.dma_start(bc_d.rearrange("b a n -> b (a n)"), bcsb[:, :]).then_inc(ss["bcd"], 16)
            act.wait_ge(ss["qk"], 1)
            S.copy(qs[:, :, :].rearrange("p a b -> p (a b)"), PB[:, 4, 0:64])
            S.activation(ks[:, :, :].rearrange("p a b -> p (a b)"), PB[:, 5, 0:64], ACT.Copy, scale=DK ** -0.5).then_inc(ss["qkc"], 1)
            act.wait_ge(ss["ld2"], 16)
            S.activation(ez[0:B, 0:D], zvo[0:B, 0:2, :].rearrange("p a n -> p (a n)"), ACT.Exp, scale=-1.0)
            S.activation(ez[0:B, D:2 * D], zvo[0:B, 4:6, :].rearrange("p a n -> p (a n)"), ACT.Exp, scale=-1.0).then_inc(ss["ea1"], 1)
            for b in range(B):
                act.wait_ge(ss["st_new"], b + 1)
                act.dma_start(o["s_ssd"][b].rearrange("(j p) n -> p j n", p=P), st[b % 2][:, :, :]).then_inc(s_out[b % 2], 16)
                act.wait_ge(ss["c_new"], b + 1)
                act.wait_ge(ss["num"], b + 1)
                act.dma_start(o["s_c"][b].rearrange("(j p) v -> p j v", p=P), cs[b % 2][:, :, :]).then_inc(s_out[b % 2], 16)
            act.wait_ge(ss["nn"], 1)
            act.dma_start(o["s_n"], ns[:, :, :]).then_inc(ss["nst"], 16)
            sqrt_step(act, B, i)
            mix_store(act, B, i, SEQ)
            act.wait_ge(ss["nst"], 16)
            for q in range(2):
                act.wait_ge(s_out[q], 16 * B)
            act.wait_ge(s["stored"], 16 * (NCH + 1))

        @block.vector
        def _(dve):
            V = nc.vector
            ch = Chain(dve, c_d, 0, s["passed"])
            ch.link(V.memset(qd[:, :, :, :], 0.0))
            dve.wait_ge(ss["ld"], 16 * 9)
            V.tensor_tensor(wss[:, :, :], rsb[:, R_G:R_G + MH, :], rsb[:, R_M:R_M + MH, :], ALU.subtract).then_inc(ss["arg"], 1)
            V.tensor_tensor(dxt[:, :, :], dts[:, :, :], chs[:, 0:8, :], ALU.mult)
            ch.link(V.tensor_tensor(ysc[:, :, :], chs[:, 0:8, :], dsc[:, :].unsqueeze(2).to_broadcast([P, 8, B]), ALU.mult))
            dve.wait_ge(ss["qkc"], 1)
            dve.wait_ge(ss["exp"], 1)
            V.tensor_copy(qd[:, :, :, :].rearrange("p a b c -> p a (b c)")[:, :, ::B + 1], qs[:, :, :]).then_inc(ss["qdz"], 1)

            def by_head(ap):
                return ap[:, :, :].rearrange("p (h k) b -> p h k b", k=KT)

            ch.link(V.tensor_tensor(by_head(ks), by_head(ks), wss[:, :, :].unsqueeze(2).to_broadcast([P, MH, KT, B]), ALU.mult))
            ch.link(V.tensor_tensor(by_head(ns), by_head(ns), wos[:, :, :].unsqueeze(2).to_broadcast([P, MH, KT, B]), ALU.mult))
            ch.link(V.tensor_tensor(ns[:, :, :], ns[:, :, :], ks[:, :, :], ALU.add))
            V.tensor_tensor(pr[:, :, :], ns[:, :, :], qs[:, :, :], ALU.mult).then_inc(ss["nn"], 1)
            for b in range(B):
                q = b % 2
                dve.wait_ge(s_in[q], 64 * (b // 2 + 1))
                x3 = [P, 8, NST]

                def group(col):
                    return bb[q][:, col * P:(col + 2) * P].rearrange("p (g n) -> p g n", g=2).unsqueeze(2).to_broadcast([P, 2, 4, NST])

                t3 = tt[:, :].rearrange("p (j n) -> p j n", j=8)
                V.tensor_tensor(st[q][:, :, :], st[q][:, :, :], nas[:, :, b:b + 1].to_broadcast(x3), ALU.mult)
                ch.link(V.tensor_tensor(t3.rearrange("p (g r) n -> p g r n", g=2), group(0),
                                        dxt[:, :, b:b + 1].rearrange("p (g r) n -> p g r n", g=2).to_broadcast([P, 2, 4, NST]), ALU.mult))
                V.tensor_tensor(st[q][:, :, :], st[q][:, :, :], t3, ALU.add).then_inc(ss["st_new"], 1)
                dve.wait_ge(ss["st_new"], b + 1)
                ch.link(V.tensor_tensor(t3.rearrange("p (g r) n -> p g r n", g=2), st[q][:, :, :].rearrange("p (g r) n -> p g r n", g=2), group(2), ALU.mult))
                ch.link(V.tensor_reduce(pr2[:, :, b], t3, mybir.AxisListType.X, ALU.add))
                c4 = cs[q][:, :, :].rearrange("p (h k) v -> p h (k v)", k=KT)
                V.tensor_tensor(c4, c4, wos[:, :, b:b + 1].to_broadcast([P, MH, KT * DK]), ALU.mult)
                t4 = tc_[:, :].rearrange("p (h k v) -> p h k v", h=MH, k=KT)
                ch.link(V.tensor_tensor(t4, vb[q][:, :].rearrange("p (h v) -> p h v", h=MH).unsqueeze(2).to_broadcast([P, MH, KT, DK]),
                                        ks[:, :, b:b + 1].rearrange("p (h k) b -> p h k b", k=KT).to_broadcast([P, MH, KT, DK]), ALU.mult))
                V.tensor_tensor(cs[q][:, :, :].rearrange("p a v -> p (a v)"), cs[q][:, :, :].rearrange("p a v -> p (a v)"), tc_[:, :], ALU.add).then_inc(ss["c_new"], 1)
                dve.wait_ge(ss["c_new"], b + 1)
            V.tensor_tensor(ysc[:, :, :], ysc[:, :, :], pr2[:, :, :], ALU.add).then_inc(ss["yt"], 1)
            dve.wait_ge(ss["ytc"], 1)
            V.tensor_copy(ysb[0:B, :], two(4)[0:B, :])
            for h in range(MH):
                V.tensor_copy(num[0:B, h * DK:(h + 1) * DK], PB[0:B, (0, 1, 6, 7)[h], 0:DK])
            ch.link(V.tensor_copy(den[0:B, 0:4], PB[0:B, 3, 0:4]))
            V.engine_nop().then_inc(ss["num_e"], 1)
            dve.wait_ge(ss["ea1"], 1)
            gate_z(dve, ch, B)
            head_out(dve, ch, B, i)


def build_peer(nc, a, o, L_):
    f32, u32 = mybir.dt.float32, mybir.dt.uint32
    ACT = mybir.ActivationFunctionType
    X = mybir.AxisListType.X
    PB, ident, two, sem = (L_[k] for k in ("PB", "ident", "two", "sem"))
    mixt_d, wp_d, x1_d, eidx_d, gate_d = (L_[k] for k in ("mixt_d", "wp_d", "x1_d", "eidx_d", "gate_d"))

    def norm_stats(dve, ch, x, r, st6, mv):
        for n in range(2):
            last = nc.vector.bn_stats(st6[0:r, n, :], x[0:r, n * 512:(n + 1) * 512])
        ch.link_plain(last)
        ch.link(nc.vector.bn_aggr(mv[0:r, :], st6[0:r, :, :]))
        return nc.vector.tensor_scalar(mv[0:r, 1:2], mv[0:r, 1:2], EPS, None, ALU.add)

    def norm_apply(dve, ch, x, r, mv, g, b):
        ch.link(nc.vector.reciprocal(mv[0:r, 1:2], mv[0:r, 1:2]))
        ch.link(nc.vector.tensor_scalar(x[0:r, :], x[0:r, :], mv[0:r, 0:1], mv[0:r, 1:2], ALU.subtract, ALU.mult))
        ch.link(nc.vector.tensor_tensor(x[0:r, :], x[0:r, :], g[0:r, :], ALU.mult))
        return nc.vector.tensor_tensor(x[0:r, :], x[0:r, :], b[0:r, :], ALU.add)

    with ExitStack() as ctx:
        def sb(name, shape, dt=f32):
            return ctx.enter_context(nc.sbuf_tensor(name, shape, dt))

        wo = sb("wo", [P, 16, D])
        wp = sb("wp", [P, NHC, KD, NK])
        mt = sb("mixt_t", [P, 16, CH])
        x1 = sb("x1", [P, D])
        x1T = sb("x1T", [P, KD, CH])
        g1, b1 = sb("g1", [P, D]), sb("b1", [P, D])
        sc = sb("sc", [P, NHC, NK])
        vals = sb("vals", [P, NHC, TOPK])
        idx = sb("idx", [P, NHC, TOPK], u32)
        idf = sb("idf", [P, NHC, TOPK])
        cand = sb("cand", [P, PH, TOPK * TOPK])
        eq = sc
        topv = sb("topv", [P, PH, TOPK])
        pos = sb("pos", [P, PH, TOPK], u32)
        pa = sb("pa", [P, 2, PH, TOPK], u32)
        paf = sb("paf", [P, 2, PH, TOPK])
        io = sb("io", [P, TOPK])
        iou = sb("iou", [P, TOPK], mybir.dt.int32)
        e2 = sb("e2", [P, 2, PH, TOPK])
        eo = sb("eo", [P, PH, TOPK], u32)
        gt = sb("gt", [P, PH, TOPK])
        sg = sb("sg", [P, PH])
        st6, mv = sb("st6", [P, 2, 6]), sb("mv1", [P, 2])
        names = ("w mt xr mix mt_used var sq x1 x1t x1tc sco scc top exp out stored iota iou passed")
        s = {n: sem("pick_" + n) for n in names.split()}
        c_d = sem("dve_chain_t")
        LINKS = 27

        def pe_step(pe, i, r):
            T = nc.tensor
            pe.wait_ge(s["mt"], 16 * (i + 1))
            pe.wait_ge(s["top"], i)
            for n in range(2):
                for k in range(16):
                    last = T.matmul(PB[0:r, 4 + n, :], mt[:, k, 0:r], wo[:, k, n * 512:(n + 1) * 512], start=k == 0, stop=k == 15)
            last.then_inc(s["mix"], 1)
            pe.wait_ge(s["x1"], i + 1)
            for k in range(KD):
                last = T.transpose(PB[:, 2 + k // 4, (k % 4) * CH:(k % 4) * CH + r], x1[0:r, k * P:(k + 1) * P], ident[0:r, 0:r])
            last.then_inc(s["x1t"], 1)
            pe.wait_ge(s["x1tc"], i + 1)
            for n in range(4):
                b = (0, 1, 6, 7)[n]
                for k in range(KD):
                    last = T.matmul(PB[0:r, b, :].rearrange("p (h n) -> p h n", h=4), x1T[:, k, 0:r], wp[:, 4 * n:4 * n + 4, k, :],
                                    start=k == 0, stop=k == KD - 1)
            last.then_inc(s["sco"], 1)

        def act_step(act, i, r, lo):
            act.wait_ge(s["var"], i + 1)
            nc.scalar.activation(mv[0:r, 1:2], mv[0:r, 1:2], ACT.Sqrt).then_inc(s["sq"], 1)
            act.wait_ge(s["x1"], i + 1)
            act.dma_start(x1_d[bass.ds(lo, r), :], x1[0:r, :]).then_inc(s["stored"], 16)
            act.wait_ge(s["x1t"], i + 1)
            for h in range(2):
                last = nc.scalar.copy(x1T[:, 4 * h:4 * h + 4, 0:r], PB[:, 2 + h, :].rearrange("p (a n) -> p a n", n=CH)[:, :, 0:r])
            last.then_inc(s["x1tc"], 1)
            act.wait_ge(s["sco"], i + 1)
            for n in range(4):
                last = nc.scalar.copy(sc[0:r, 4 * n:4 * n + 4, :].rearrange("p a n -> p (a n)"), PB[0:r, (0, 1, 6, 7)[n], :])
            last.then_inc(s["scc"], 1)
            act.wait_ge(s["top"], i + 1)
            nc.scalar.activation(gt[0:r, :, :], gt[0:r, :, :], ACT.Exp).then_inc(s["exp"], 1)
            act.wait_ge(s["out"], i + 1)
            act.dma_start(eidx_d[:, bass.ds(lo, r), :].rearrange("h t k -> t h k"), eo[0:r, :, :]).then_inc(s["stored"], 16)
            act.dma_start(gate_d[:, bass.ds(lo, r), :].rearrange("h t k -> t h k"), gt[0:r, :, :]).then_inc(s["stored"], 16)

        def top16(ch, r, n, src, val, ind):
            V = nc.vector
            for h in range(n):
                last = V.max(val[0:r, h, 0:8], src[0:r, h, :])
            ch.link_plain(last)
            for h in range(n):
                last = V.max_index(ind[0:r, h, 0:8], val[0:r, h, 0:8], src[0:r, h, :])
            ch.link_plain(last)
            for h in range(n):
                last = V.match_replace(src[0:r, h, :], val[0:r, h, 0:8], src[0:r, h, :], NEG)
            ch.link_plain(last)
            for h in range(n):
                last = V.max(val[0:r, h, 8:16], src[0:r, h, :])
            ch.link_plain(last)
            for h in range(n):
                last = V.max_index(ind[0:r, h, 8:16], val[0:r, h, 8:16], src[0:r, h, :])
            ch.link_plain(last)

        def dve_step(dve, i, r):
            V = nc.vector
            ch = Chain(dve, c_d, LINKS * i, s["passed"])
            dve.wait_ge(s["mix"], i + 1)
            dve.wait_ge(s["xr"], 16 * (i + 1))
            dve.wait_ge(s["stored"], 48 * i)
            ch.link(V.scalar_tensor_tensor(x1[0:r, :], x1[0:r, :], ALPHA, two(4)[0:r, :], ALU.mult, ALU.add))
            norm_stats(dve, ch, x1, r, st6, mv).then_inc(s["var"], 1)
            dve.wait_ge(s["sq"], i + 1)
            norm_apply(dve, ch, x1, r, mv, g1, b1).then_inc(s["x1"], 1)
            dve.wait_ge(s["scc"], i + 1)
            dve.sem_inc(s["passed"], 1)
            top16(ch, r, NHC, sc, vals, idx)
            V.tensor_copy(idf[0:r, :, :], idx[0:r, :, :])
            v4 = vals[0:r, :, :].rearrange("p (h c) k -> p h c k", c=2)
            for h in range(PH):
                last = V.tensor_tensor(cand[0:r, h, :].rearrange("p (x y) -> p x y", x=TOPK),
                                       vals[0:r, 2 * h, :].unsqueeze(2).to_broadcast([r, TOPK, TOPK]),
                                       vals[0:r, 2 * h + 1, :].unsqueeze(1).to_broadcast([r, TOPK, TOPK]), ALU.add)
            ch.link_plain(last)
            top16(ch, r, PH, cand, topv, pos)
            V.tensor_tensor(gt[0:r, :, :], topv[0:r, :, :], topv[0:r, :, 0:1].to_broadcast([r, PH, TOPK]), ALU.subtract).then_inc(s["top"], 1)
            V.tensor_scalar(pa[0:r, 0, :, :], pos[0:r, :, :], 4, None, ALU.logical_shift_right)
            ch.link(V.tensor_scalar(pa[0:r, 1, :, :], pos[0:r, :, :], TOPK - 1, None, ALU.bitwise_and))
            ch.link(V.tensor_copy(paf[0:r, :, :, :], pa[0:r, :, :, :]))
            q = eq[0:r, :, :].rearrange("p a n -> p (a n)").rearrange("p (g k) -> p g k", k=TOPK)
            for c in range(2):
                ch.link(V.tensor_tensor(q, paf[0:r, c, :, :].rearrange("p h k -> p (h k)").unsqueeze(2).to_broadcast([r, P, TOPK]),
                                        io[0:r, :].unsqueeze(1).to_broadcast([r, P, TOPK]), ALU.is_equal))
                q4 = q.rearrange("p (h k) x -> p h k x", h=PH)
                ch.link(V.tensor_tensor(q4, q4, idf[0:r, :, :].rearrange("p (h c) k -> p h c k", c=2)[:, :, c, :].unsqueeze(2).to_broadcast([r, PH, TOPK, TOPK]), ALU.mult))
                ch.link(V.tensor_reduce(e2[0:r, c, :, :].rearrange("p h k -> p (h k)"), q, X, ALU.add))
            V.scalar_tensor_tensor(eo[0:r, :, :], e2[0:r, 0, :, :], float(NK), e2[0:r, 1, :, :], ALU.mult, ALU.add)
            dve.wait_ge(s["exp"], i + 1)
            ch.link(V.tensor_reduce(sg[0:r, :], gt[0:r, :, :], X, ALU.add))
            ch.link(V.reciprocal(sg[0:r, :], sg[0:r, :]))
            V.tensor_tensor(gt[0:r, :, :], gt[0:r, :, :], sg[0:r, :].unsqueeze(2).to_broadcast([r, PH, TOPK]), ALU.mult).then_inc(s["out"], 1)
            assert ch.n == LINKS, ch.n

        with nc.Block() as block:
            @block.sync
            def _(sp):
                sp.dma_start(wo[:, :, :], a["w_out"]).then_inc(s["w"], 16)
                for j in range(NHC):
                    sp.dma_start(wp[:, j, :, :], wp_d[j]).then_inc(s["w"], 16)
                sp.dma_start(g1[:, :], a["ln1_g"].partition_broadcast(P)).then_inc(s["w"], 16)
                sp.dma_start(b1[:, :], a["ln1_b"].partition_broadcast(P)).then_inc(s["w"], 16)

                def load(i, r, lo):
                    sp.wait_ge(s["mix"], i)
                    sp.dma_start(mt[:, :, 0:r], mixt_d[:, :, bass.ds(lo, r)].rearrange("j p t -> p j t")).then_inc(s["mt"], 16)
                    sp.wait_ge(s["x1t"], i)
                    if r == CH:
                        sp.sem_inc(s["passed"], 1)
                    sp.wait_ge(s["stored"], 48 * i)
                    sp.dma_start(x1[0:r, :], a["x_tok"][bass.ds(lo, r), :]).then_inc(s["xr"], 16)

                for i in steps(sp, NCH):
                    load(i, CH, i * CH)
                load(NCH, NSMP, SEQ)

            @block.tensor
            def _(pe):
                pe.wait_ge(s["w"], 16 * (NHC + 3))
                for i in steps(pe, NCH):
                    pe_step(pe, i, CH)
                pe_step(pe, NCH, NSMP)

            @block.scalar
            def _(act):
                for i in steps(act, NCH):
                    act_step(act, i, CH, i * CH)
                act_step(act, NCH, NSMP, SEQ)
                act.wait_ge(s["stored"], 48 * (NCH + 1))

            @block.gpsimd
            def _(pool):
                nc.gpsimd.iota(iou[:, :], [[1, TOPK]], 0, 0).then_inc(s["iou"], 1)
                pool.wait_ge(s["iou"], 1)

            @block.vector
            def _(dve):
                dve.wait_ge(s["iou"], 1)
                nc.vector.tensor_copy(io[:, :], iou[:, :]).then_inc(s["iota"], 1)
                dve.wait_ge(s["iota"], 1)
                dve.wait_ge(s["w"], 16 * (NHC + 3))
                for i in steps(dve, NCH):
                    dve_step(dve, i, CH)
                dve_step(dve, NCH, NSMP)

    L_["end_phase"]()

    with ExitStack() as ctx:
        def sb(name, shape, dt=f32):
            return ctx.enter_context(nc.sbuf_tensor(name, shape, dt))

        ub = sb("ub", [P, NB, D])
        vbf = sb("vbf", [P, NB, D])
        ix = [sb(f"ix{q}", [P, TOPK], u32) for q in range(2)]
        gg = [sb(f"gg{q}", [P, TOPK]) for q in range(2)]
        hid = [sb(f"hid{q}", [P, TOPK]) for q in range(2)]
        wg = [sb(f"wg{q}", [P, TOPK]) for q in range(2)]
        dg = sb("dg", [P, 4, P])
        x1 = sb("x1g", [P, D])
        acc = sb("acc", [P, D])
        g2, b2 = sb("g2", [P, D]), sb("b2", [P, D])
        st6, mv = sb("st62", [P, 2, 6]), sb("mv2", [P, 2])
        NIT = NCH * PH
        x1s = sb("x1s", [P, NSMP, D])
        ixs = sb("ixs", [P, NSMP], u32)
        ggs, hids, wgs = sb("ggs", [P, NSMP]), sb("hids", [P, NSMP]), sb("wgs", [P, NSMP, NSMP])
        s_ix = [sem(f"picks_loaded{q}") for q in range(2)]
        s_gg = [sem(f"gates_loaded{q}") for q in range(2)]
        s_u = [sem(f"u_rows{n}") for n in range(NB)]
        s_v = [sem(f"v_rows{n}") for n in range(NB)]
        s = {n: sem("exp_" + n) for n in ("w x1 dot gelu gate diag pv accd acc0 var sq y stored smp dots gates gz go passed".split())}
        c_d = sem("dve_chain_g")
        c_g = sem("dve_chain_h")

        with nc.Block() as block:
            @block.sync
            def _(sp):
                sp.dma_start(g2[:, :], a["ln2_g"].partition_broadcast(P)).then_inc(s["w"], 16)
                sp.dma_start(b2[:, :], a["ln2_b"].partition_broadcast(P)).then_inc(s["w"], 16)
                sp.dma_start(x1s[:, :, :], x1_d[SEQ:NTOK, :].partition_broadcast(P)).then_inc(s["smp"], 16)
                for h in range(PH):
                    sp.dma_start(ixs[h * TOPK:(h + 1) * TOPK, :], eidx_d[h, SEQ:NTOK, :].rearrange("t k -> k t"), allow_slow_non_contiguous=True).then_inc(s["smp"], 16)
                    sp.dma_start(ggs[h * TOPK:(h + 1) * TOPK, :], gate_d[h, SEQ:NTOK, :].rearrange("t k -> k t"), allow_slow_non_contiguous=True).then_inc(s["smp"], 16)
                for c in steps(sp, NCH):
                    sp.wait_ge(s["acc0"], c)
                    sp.wait_ge(s["y"], c)
                    sp.dma_start(x1[:, :], x1_d[bass.ds(c * CH, CH), :]).then_inc(s["x1"], 16)
                    for hh in inner(sp, c, PH // 2):
                        for q in range(2):
                            it = c * (PH // 2) + hh
                            sp.wait_ge(s_v[NB - 1], 64 * it)
                            sp.sem_inc(s["passed"], 1)
                            sp.wait_ge(s["gate"], 2 * it)
                            sp.sem_inc(s["passed"], 1)
                            sp.wait_ge(s["pv"], 16 * (2 * it))
                            sp.dma_start(ix[q][:, :], eidx_d[2 * hh + q, bass.ds(c * CH, CH), :]).then_inc(s_ix[q], 16)
                            sp.dma_start(gg[q][:, :], gate_d[2 * hh + q, bass.ds(c * CH, CH), :]).then_inc(s_gg[q], 16)
                sp.wait_ge(s["y"], NCH)
                sp.dma_start(x1[0:NSMP, :], x1_d[SEQ:NTOK, :]).then_inc(s["x1"], 16)

            @block.gpsimd
            def _(pool):
                def gather(buf, table, index, done):
                    pool.indirect_dma_start(out=buf, out_offset=None, in_=table,
                                            in_offset=bass.IndirectOffsetOnAxis(ap=index, axis=0)).then_inc(done, 16)

                for it in steps(pool, NIT // 2):
                    for q in range(2):
                        base = TOPK * (2 * it + q)
                        pool.wait_ge(s_ix[q], 16 * (it + 1))
                        for k in range(TOPK):
                            if k % 4 == 0:
                                pool.wait_ge(s["dot"], base + k + 4)
                                pool.sem_inc(s["passed"], 1)
                            gather(ub[:, k % NB, :], a["peer_u"], ix[q][:, k:k + 1], s_u[k % NB])
                        for k in range(TOPK):
                            if k % 4 == 0:
                                pool.wait_ge(s["pv"], base + k + 4)
                                pool.sem_inc(s["passed"], 1)
                            gather(vbf[:, k % NB, :], a["peer_v"], ix[q][:, k:k + 1], s_v[k % NB])
                pool.wait_ge(s["smp"], 16 * 17)
                for b in range(NSMP):
                    pool.wait_ge(s["dot"], NIT * TOPK + NB)
                    pool.wait_ge(s["pv"], NIT * TOPK + NB)
                    gather(ub[:, b, :], a["peer_u"], ixs[:, b:b + 1], s_u[b])
                    gather(vbf[:, b, :], a["peer_v"], ixs[:, b:b + 1], s_v[b])

            @block.vector
            def _(dve):
                V = nc.vector
                V.memset(wgs[:, :, :], 0.0)
                V.memset(hid[0][:, :], 0.0)
                V.memset(acc[:, :], 0.0).then_inc(s["dot"], NB)
                dve.wait_ge(s["dot"], NB)
                dve.wait_ge(s["w"], 32)
                for c in steps(dve, NCH):
                    ch = Chain(dve, c_d, 5 * c, s["passed"])
                    dve.wait_ge(s["x1"], 16 * (c + 1))
                    dve.wait_ge(s["stored"], 16 * c)
                    V.tensor_scalar(acc[:, :], x1[:, :], ALPHA, None, ALU.mult).then_inc(s["acc0"], 1)
                    dve.wait_ge(s["acc0"], c + 1)
                    dve.sem_inc(s["passed"], 1)
                    for hh in inner(dve, c, PH // 2):
                        it = c * (PH // 2) + hh
                        for q in range(2):
                            base = TOPK * (2 * it + q)
                            for k in range(TOPK):
                                dve.wait_ge(s_u[k % NB], 16 * (4 * it + 2 * q + k // NB + 1))
                                V.tensor_tensor_reduce(out=ub[:, k % NB, :], in0=ub[:, k % NB, :], in1=x1[:, :], scale=1.0, scalar=0.0,
                                                       op0=ALU.mult, op1=ALU.add, accum_out=hid[q][:, k:k + 1]).then_inc(s["dot"], 1)
                            dve.wait_ge(s["gelu"], 2 * it + q + 1)
                            dve.wait_ge(s_gg[q], 16 * (it + 1))
                            V.tensor_tensor(wg[q][:, :], hid[q][:, :], gg[q][:, :], ALU.mult).then_inc(s["gate"], 1)
                            dve.wait_ge(s["pv"], base + TOPK + NB)
                            V.tensor_tensor(acc[:, :], acc[:, :], two(2 * q), ALU.add).then_inc(s["accd"], 1)
                            dve.wait_ge(s["accd"], 2 * it + q + 1)
                    norm_stats(dve, ch, acc, P, st6, mv).then_inc(s["var"], 1)
                    dve.wait_ge(s["sq"], c + 1)
                    norm_apply(dve, ch, acc, P, mv, g2, b2).then_inc(s["y"], 1)
                ch = Chain(dve, c_g, 0, s["passed"])
                r = NSMP
                dve.wait_ge(s["smp"], 16 * 17)
                dve.wait_ge(s["x1"], 16 * (NCH + 1))
                dve.wait_ge(s["stored"], 16 * NCH)
                for b in range(r):
                    dve.wait_ge(s_u[b], 16 * (NIT * TOPK // NB + 1))
                    last = V.tensor_tensor_reduce(out=ub[:, b, :], in0=ub[:, b, :], in1=x1s[:, b, :], scale=1.0, scalar=0.0,
                                                  op0=ALU.mult, op1=ALU.add, accum_out=hids[:, b:b + 1])
                last.then_inc(s["dots"], 1)
                dve.wait_ge(s["gates"], 1)
                V.tensor_tensor(wgs[:, :, :].rearrange("p a b -> p (a b)")[:, ::r + 1], hids[:, :], ggs[:, :], ALU.mult).then_inc(s["gz"], 1)
                dve.wait_ge(s["go"], 1)
                ch.link(V.scalar_tensor_tensor(acc[0:r, :], x1[0:r, :], ALPHA, two(0)[0:r, :], ALU.mult, ALU.add))
                norm_stats(dve, ch, acc, r, st6, mv).then_inc(s["var"], 1)
                dve.wait_ge(s["sq"], NCH + 1)
                norm_apply(dve, ch, acc, r, mv, g2, b2).then_inc(s["y"], 1)

            @block.scalar
            def _(act):
                for c in steps(act, NCH):
                    for hh in inner(act, c, PH // 2):
                        it = c * (PH // 2) + hh
                        for q in range(2):
                            base = TOPK * (2 * it + q)
                            act.wait_ge(s["dot"], base + TOPK + NB)
                            nc.scalar.activation(hid[q][:, :], hid[q][:, :], ACT.Gelu).then_inc(s["gelu"], 1)
                            act.wait_ge(s["gate"], 2 * it + q + 1)
                            for k in range(TOPK):
                                act.wait_ge(s["pv"], base + k + NB - 3)
                                nc.scalar.activation(dg[:, k % 4, :], ident[:, :], ACT.Copy, scale=wg[q][:, k:k + 1]).then_inc(s["diag"], 1)
                    act.wait_ge(s["var"], c + 1)
                    nc.scalar.activation(mv[:, 1:2], mv[:, 1:2], ACT.Sqrt).then_inc(s["sq"], 1)
                    act.wait_ge(s["y"], c + 1)
                    act.dma_start(o["y"][bass.ds(c * CH, CH), :], acc[:, :]).then_inc(s["stored"], 16)
                act.wait_ge(s["dots"], 1)
                nc.scalar.activation(hids[:, :], hids[:, :], ACT.Gelu).then_inc(s["gates"], 1)
                act.wait_ge(s["var"], NCH + 1)
                nc.scalar.activation(mv[0:NSMP, 1:2], mv[0:NSMP, 1:2], ACT.Sqrt).then_inc(s["sq"], 1)
                act.wait_ge(s["y"], NCH + 1)
                act.dma_start(o["y"][SEQ:NTOK, :], acc[0:NSMP, :]).then_inc(s["stored"], 16)
                act.wait_ge(s["stored"], 16 * (NCH + 1))

            @block.tensor
            def _(pe):
                pe.nop().then_inc(s["pv"], NB)
                for it in steps(pe, NIT // 2):
                    for q in range(2):
                        base = TOPK * (2 * it + q)
                        pe.wait_ge(s["accd"], 2 * it)
                        for k in range(TOPK):
                            pe.wait_ge(s["diag"], base + k + 1)
                            pe.wait_ge(s_v[k % NB], 16 * (4 * it + 2 * q + k // NB + 1))
                            for n in range(2):
                                last = nc.tensor.matmul(PB[:, 2 * q + n, :], dg[:, k % 4, :], vbf[:, k % NB, n * 512:(n + 1) * 512],
                                                        start=k == 0, stop=k == TOPK - 1)
                            last.then_inc(s["pv"], 1)
                pe.wait_ge(s["gz"], 1)
                pe.wait_ge(s["accd"], NIT)
                for b in range(NSMP):
                    pe.wait_ge(s_v[b], 16 * (NIT * TOPK // NB + 1))
                    for n in range(2):
                        last = nc.tensor.matmul(PB[0:NSMP, n, :], wgs[:, b, :], vbf[:, b, n * 512:(n + 1) * 512],
                                                start=b == 0, stop=b == NSMP - 1)
                last.then_inc(s["go"], 1)


def kernel(x_prompt, x_sample, state_ssd, state_ssd_conv, state_mlstm_c, state_mlstm_n, state_mlstm_m,
           state_mlstm_conv, w_in, conv_ssd_w, conv_ssd_b, dt_bias, a_log, d_skip, ssd_norm_g, conv_m_w, conv_m_b,
           w_mq, w_mk, b_igate, b_fgate, mlstm_norm_g, w_out, ln1_g, ln1_b, peer_wq, peer_keys, peer_u, peer_v,
           ln2_g, ln2_b):
    import concourse.bacc as bacc
    from concourse.bass_utils import run_bass_kernel_spmd

    x = np.concatenate([x_prompt[0], x_sample[:, 0]], axis=0)
    w = np.asarray(w_in[0])
    cols = np.cumsum((D, D + 2 * NG * NST, NH, D, D, D, MH, MH))
    z, xbc, dtw, um, vm, om, iw, fw = np.split(w, cols[:-1], axis=1)

    def k_major(m):
        return m.reshape(-1, P, m.shape[-1]).transpose(1, 0, 2)

    chan = np.concatenate([xbc, um], axis=1).reshape(KD, P, NCT, P).transpose(2, 1, 0, 3)
    tok = np.concatenate([z, vm, om], axis=1).reshape(KD, P, 6, 512).transpose(2, 1, 0, 3)
    row = np.zeros((D, P), w.dtype)
    row[:, 0:NH], row[:, 32:32 + MH], row[:, 64:64 + MH] = dtw, iw, fw
    gate_b = np.zeros((16, 4), w.dtype)
    gate_b[0:NH, 0], gate_b[0:MH, 1], gate_b[0:MH, 2], gate_b[0:NH, 3] = dt_bias[0], b_igate[0], b_fgate[0], a_log[0]
    conv_w = np.concatenate([np.concatenate([conv_ssd_w[0], conv_m_w[0]], axis=1),
                             np.concatenate([conv_ssd_b[0], conv_m_b[0]])[None]], axis=0)
    conv_s = np.concatenate([state_ssd_conv[0], state_mlstm_conv[0]], axis=2)
    wq = np.asarray(peer_wq[0]).reshape(D, NHC, P)
    arrays = {
        "x_tok": x,
        "x_t": k_major(np.asarray(x).T),
        "w_ch": chan, "w_tok": tok, "w_row": k_major(row), "gate_b": gate_b,
        "conv_w": conv_w.T.reshape(NCT, P, TAPS + 1),
        "conv_s": conv_s.transpose(2, 1, 0).reshape(NCT, P, 3, NSMP),
        "m_state": np.asarray(state_mlstm_m[0]).T,
        "n_state": np.asarray(state_mlstm_n[0]).reshape(NSMP, MH * KT, P).transpose(2, 1, 0),
        "ssd_state": np.asarray(state_ssd[0]).reshape(NSMP, NH * HD, NST),
        "c_state": np.asarray(state_mlstm_c[0]).reshape(NSMP, MH * DK, DK),
        "d_skip": np.asarray(d_skip[0]),
        "d_skip_ch": np.repeat(np.asarray(d_skip[0]), HD).reshape(8, P).T,
        "ssd_g": np.asarray(ssd_norm_g[0]), "mlstm_g": np.asarray(mlstm_norm_g[0]).reshape(-1),
        "w_mq": np.asarray(w_mq[0]).reshape(MH, KT, P, DK).transpose(2, 0, 1, 3),
        "w_mk": np.asarray(w_mk[0]).reshape(MH, KT, P, DK).transpose(2, 0, 1, 3),
        "w_out": k_major(np.asarray(w_out[0])),
        "ln1_g": np.asarray(ln1_g[0]), "ln1_b": np.asarray(ln1_b[0]),
        "ln2_g": np.asarray(ln2_g[0]), "ln2_b": np.asarray(ln2_b[0]),
        "wq_t": wq.transpose(1, 2, 0),
        "keys_t": np.asarray(peer_keys[0]).reshape(NHC, NK, P).transpose(0, 2, 1),
        "peer_u": np.asarray(peer_u[0]), "peer_v": np.asarray(peer_v[0]),
    }
    outs = {"y": (NTOK, D), "conv_p": (NCT, P, 3), "conv_s": (NCT, P, 3, NSMP), "p_ssd": (P, D),
            "p_c": (P, MH * KT, DK), "p_n": (P, MH * KT), "p_m": (MH, 1), "s_ssd": (NSMP, NH * HD, NST),
            "s_c": (NSMP, MH * DK, DK), "s_n": (P, MH * KT, NSMP), "s_m": (MH, NSMP)}
    nc = bacc.Bacc("TRN2", target_bir_lowering=False, num_devices=1)
    given, a, o = {}, {}, {}
    for name, v in arrays.items():
        v = np.ascontiguousarray(v)
        given["in_" + name] = v
        a[name] = nc.dram_tensor("in_" + name, v.shape, mybir.dt.from_np(v.dtype), kind="ExternalInput").ap()
    for name, shape in outs.items():
        o[name] = nc.dram_tensor("out_" + name, shape, mybir.dt.float32, kind="ExternalOutput").ap()
    build(nc, a, o)
    got = run_bass_kernel_spmd(nc, [given], core_ids=[0]).results[0]
    r = {name: got["out_" + name] for name in outs}
    conv_p = r["conv_p"].reshape(NCT * P, 3).T
    conv_q = r["conv_s"].reshape(NCT * P, 3, NSMP).transpose(2, 1, 0)
    nx = D + 2 * NG * NST
    return (
        r["y"][None, 0:SEQ], r["y"][SEQ:NTOK, None],
        r["p_ssd"].T.reshape(1, 1, NH, HD, NST), conv_p[None, None, :, 0:nx],
        r["p_c"].transpose(1, 0, 2).reshape(1, 1, MH, DK, DK), r["p_n"].T.reshape(1, 1, MH, DK),
        r["p_m"].reshape(1, 1, MH), conv_p[None, None, :, nx:],
        r["s_ssd"].reshape(1, NSMP, NH, HD, NST), conv_q[None, :, :, 0:nx],
        r["s_c"].reshape(1, NSMP, MH, DK, DK), r["s_n"].transpose(2, 1, 0).reshape(1, NSMP, MH, DK),
        r["s_m"].T.reshape(1, NSMP, MH), conv_q[None, :, :, nx:],
    )
```

```python
import concourse.bass as bass
from concourse import mybir
from concourse.alu_op_type import AluOpType as ALU
from contextlib import ExitStack
import numpy as np

P = 128
D = 1024
KD = D // P
SEQ = 1024
CH = 128
NCH = SEQ // CH
NSMP = 8
NTOK = SEQ + NSMP
NPAD = SEQ + CH
NH, HD, NST, NG = 16, 64, 128, 2
MH, DK = 4, 256
KT = DK // P
NCT = 20
BT0, CT0, UT0 = 8, 10, 12
PH, NK, TOPK = 8, 128, 16
NE = NK * NK
NHC = 2 * PH
TAPS = 4
ALPHA = 2.0 ** 0.25
EPS = 1e-5
BIG = 1e30
NEG = -3e38
R_NACS, R_M, R_WLOG, R_DT, R_G, R_MT, NROW = 0, 16, 20, 24, 40, 44, 48
NB = 4


class Chain:

    def __init__(self, eng, sem, base=0, plain=None):
        self.eng, self.sem, self.base, self.plain, self.n = eng, sem, base, plain, 0

    def link(self, ins):
        ins.then_inc(self.sem, 1)
        self.n += 1
        self.eng.wait_ge(self.sem, self.base + self.n)

    def link_plain(self, ins):
        self.link(ins)
        self.eng.sem_inc(self.plain, 1)


def steps(eng, n):
    yield 0
    with eng.Fori(1, n) as i:
        yield i


def inner(eng, outer, n):
    if isinstance(outer, int):
        yield from steps(eng, n)
    else:
        with eng.Fori(0, n) as i:
            yield i


def free(eng, sem, value):
    if not isinstance(value, int) or value > 0:
        eng.wait_ge(sem, value)


def build(nc, a, o):
    f32, u32 = mybir.dt.float32, mybir.dt.uint32
    ACT = mybir.ActivationFunctionType
    X = mybir.AxisListType.X

    def dram(name, shape, dt=f32):
        return nc.dram_tensor(name, shape, dt).ap()

    cht_d = dram("cht_d", (NCT, P, NTOK))
    tok_d = dram("tok_d", (6, NTOK, 512))
    rows_d = dram("rows_d", (NROW, SEQ))
    rows_s_d = dram("rows_s_d", (NROW, NSMP))
    wp_d = dram("wp_d", (NHC, P, KD, NK))
    mixt_d = dram("mixt_d", (16, P, NPAD))
    x1_d = dram("x1_d", (NSMP, D))
    bc_d = dram("bc_d", (NSMP, 4, P))

    top = ExitStack()
    with top:
        phase_sems = []

        def sem(name):
            phase_sems.append(nc.alloc_semaphore(name=name))
            return phase_sems[-1]

        def end_phase():
            nc.clear_and_free_semaphores(phase_sems)
            nc.all_engine_barrier()
            phase_sems.clear()

        PB = top.enter_context(nc.psum_tensor("PB", [P, 8, 512], f32))
        ident = top.enter_context(nc.sbuf_tensor("ident", [P, P], f32))

        def two(b):
            return PB[:, b:b + 2, :].rearrange("p a n -> p (a n)")

        with ExitStack() as ctx:
            def sb(name, shape, dt=f32):
                return ctx.enter_context(nc.sbuf_tensor(name, shape, dt))

            xT = sb("xT", [P, KD, NTOK])
            wch = [sb(f"wch{i}", [P, KD, P]) for i in range(2)]
            wtk = [sb(f"wtk{i}", [P, KD, 512]) for i in range(2)]
            wrow = sb("wrow", [P, KD, P])
            cw = [sb(f"cw{i}", [P, TAPS + 1]) for i in range(2)]
            xp = [sb(f"xp{i}", [P, TAPS - 1 + SEQ]) for i in range(2)]
            xps = [sb(f"xps{i}", [P, TAPS, NSMP]) for i in range(2)]
            cv = [sb(f"cv{i}", [P, NTOK]) for i in range(2)]
            so = [sb(f"so{i}", [P, NTOK]) for i in range(2)]
            stg = [sb(f"stg{i}", [P, 512]) for i in range(6)]
            gb = sb("gb", [16, 4])
            dtr = sb("dtr", [NH, NTOK])
            ir = sb("ir", [MH, NTOK])
            fr = sb("fr", [MH, NTOK])
            t1 = sb("t1", [NH, NTOK])
            t2 = sb("t2", [NH, NTOK])
            t3 = sb("t3", [MH, NTOK])
            nacs = sb("nacs", [NH, NTOK])
            bcs = sb("bcs", [MH, NTOK])
            mrun = sb("mrun", [MH, NTOK])
            wlog = sb("wlog", [MH, NTOK])
            mt = sb("mt", [MH, NTOK])
            ones = sb("ones", [16, CH])
            zros = sb("zros", [16, CH])
            mcar = sb("mcar", [MH, NCH + 1])
            m0s = sb("m0s", [MH, NSMP])
            ea = sb("ea", [NH, 1])
            kk_ = [sb(f"wqt{i}", [P, D]) for i in range(2)]
            kyt = [sb(f"kyt{i}", [P, NK]) for i in range(2)]
            wps = [sb(f"wps{i}", [P, KD, NK]) for i in range(2)]

            s_x, s_wr, s_gb = sem("x_loaded"), sem("wrow_loaded"), sem("gate_bias_loaded")
            s_w = [sem(f"chan_weights_loaded{i}") for i in range(2)]
            s_cw = [sem(f"conv_taps_loaded{i}") for i in range(2)]
            s_mm = [sem(f"chan_product{i}") for i in range(2)]
            s_ev = [sem(f"chan_evacuated{i}") for i in range(2)]
            s_cv = [sem(f"convolved{i}") for i in range(2)]
            s_si = [sem(f"silu_done{i}") for i in range(2)]
            s_st = [sem(f"chan_stored{i}") for i in range(2)]
            s_cs = [sem(f"conv_state_stored{i}") for i in range(2)]
            s_rw, s_re, s_z0 = sem("row_product"), sem("row_evacuated"), sem("zeroed")
            s_tw = [sem(f"tok_weights_loaded{i}") for i in range(2)]
            s_tm = [sem(f"tok_product{i}") for i in range(6)]
            s_te = [sem(f"tok_evacuated{i}") for i in range(6)]
            s_ts = [sem(f"tok_stored{i}") for i in range(6)]
            s_pw = [sem(f"wq_loaded{i}") for i in range(2)]
            s_pm = [sem(f"wp_product{i}") for i in range(2)]
            s_pe = [sem(f"wp_evacuated{i}") for i in range(2)]
            s_ps = [sem(f"wp_stored{i}") for i in range(2)]
            s_e1, s_l1, s_rs, s_abs = sem("gate_exp"), sem("gate_log"), sem("rows_stored"), sem("gate_abs")
            s_rr = sem("rows_ready")
            c_d, c_a = sem("dve_chain_a"), sem("act_chain_a")
            s_id0, s_id = sem("ident_zeroed"), sem("ident_ready")

            with nc.Block() as block:
                @block.sync
                def _(sp):
                    sp.dma_start(wrow[:, :, :], a["w_row"]).then_inc(s_wr, 16)
                    for k in range(KD):
                        sp.dma_start(xT[:, k, :], a["x_t"][:, k, :]).then_inc(s_x, 16)
                    sp.dma_start(gb[:, :], a["gate_b"]).then_inc(s_gb, 16)
                    sp.dma_start(m0s[:, :], a["m_state"]).then_inc(s_gb, 16)
                    for i in steps(sp, NCT // 2):
                        for q in range(2):
                            j = 2 * i + q
                            sp.wait_ge(s_mm[q], i)
                            sp.dma_start(wch[q][:, :, :], a["w_ch"][j, :, :, :]).then_inc(s_w[q], 16)
                            sp.wait_ge(s_cv[q], i)
                            sp.dma_start(cw[q][:, :], a["conv_w"][j, :, :]).then_inc(s_cw[q], 16)
                            sp.wait_ge(s_cs[q], 32 * i)
                            sp.dma_start(xps[q][:, 0:3, :], a["conv_s"][j, :, :, :]).then_inc(s_cw[q], 16)
                    for i in steps(sp, 3):
                        for q in range(2):
                            sp.wait_ge(s_tm[(2, 5)[q]], 3 * i)
                            sp.dma_start(wtk[q][:, :, :], a["w_tok"][2 * i + q, :, :, :]).then_inc(s_tw[q], 16)
                    for i in steps(sp, NHC // 2):
                        for q in range(2):
                            j = 2 * i + q
                            sp.wait_ge(s_pm[q], i)
                            sp.dma_start(kk_[q][:, :], a["wq_t"][j, :, :]).then_inc(s_pw[q], 16)
                            sp.dma_start(kyt[q][:, :], a["keys_t"][j, :, :]).then_inc(s_pw[q], 16)

                @block.tensor
                def _(pe):
                    pe.wait_ge(s_x, 16 * KD)
                    pe.wait_ge(s_wr, 16)
                    for out, lo, n in ((PB[:, 6, :], 0, 512), (PB[:, 7, :], 512, 512),
                                       (PB[:, 5, 256:256 + NSMP], SEQ, NSMP)):
                        for k in range(KD):
                            last = nc.tensor.matmul(out, wrow[:, k, :], xT[:, k, lo:lo + n],
                                                    start=k == 0, stop=k == KD - 1)
                    last.then_inc(s_rw, 1)
                    pe.wait_ge(s_re, 1)
                    for i in steps(pe, NCT // 2):
                        for q in range(2):
                            pe.wait_ge(s_w[q], 16 * (i + 1))
                            pe.wait_ge(s_ev[q], i)
                            for out, lo, n in ((PB[:, 3 * q, :], 0, 512), (PB[:, 3 * q + 1, :], 512, 512),
                                               (PB[:, 3 * q + 2, 0:NSMP], SEQ, NSMP)):
                                for k in range(KD):
                                    last = nc.tensor.matmul(out, wch[q][:, k, :], xT[:, k, lo:lo + n],
                                                            start=k == 0, stop=k == KD - 1)
                            last.then_inc(s_mm[q], 1)
                    for q in range(2):
                        pe.wait_ge(s_ev[q], NCT // 2)
                    for i in steps(pe, 3):
                        for u in range(18):
                            q, t, b = u // 9, u % 9, u % 6
                            n = CH if t < NCH else NSMP
                            if t == 0:
                                pe.wait_ge(s_tw[q], 16 * (i + 1))
                            pe.wait_ge(s_te[b], 3 * i + u // 6)
                            for k in range(KD):
                                last = nc.tensor.matmul(PB[0:n, b, :], xT[:, k, t * CH:t * CH + n],
                                                        wtk[q][:, k, :], start=k == 0, stop=k == KD - 1)
                            last.then_inc(s_tm[b], 1)
                    for b in range(6):
                        pe.wait_ge(s_te[b], 9)
                    for i in steps(pe, NHC // 2):
                        for q in range(2):
                            pe.wait_ge(s_pw[q], 32 * (i + 1))
                            pe.wait_ge(s_pe[q], i)
                            for k in range(KD):
                                last = nc.tensor.matmul(two(4 * q)[:, k * NK:(k + 1) * NK],
                                                        kk_[q][:, k * P:(k + 1) * P], kyt[q][:, :],
                                                        start=True, stop=True)
                            last.then_inc(s_pm[q], 1)

                @block.scalar
                def _(act):
                    act.wait_ge(s_rw, 1)
                    for lo, n, src in ((0, 512, PB[:, 6, :]), (512, 512, PB[:, 7, :]),
                                       (SEQ, NSMP, PB[:, 5, 256:256 + NSMP])):
                        nc.scalar.copy(dtr[:, lo:lo + n], src[0:16, :])
                        nc.scalar.copy(ir[:, lo:lo + n], src[32:36, :])
                        last = nc.scalar.copy(fr[:, lo:lo + n], src[64:68, :])
                    last.then_inc(s_re, 1)
                    act.wait_ge(s_abs, 1)
                    ch = Chain(act, c_a)
                    nc.scalar.activation(t1[:, :], t1[:, :], ACT.Exp, scale=-1.0)
                    nc.scalar.activation(ea[:, :], gb[0:NH, 3:4], ACT.Exp)
                    ch.link(nc.scalar.activation(t3[:, :], t3[:, :], ACT.Exp, scale=-1.0))
                    nc.scalar.activation(t1[:, :], t1[:, :], ACT.Ln, bias=1.0)
                    nc.scalar.activation(t3[:, :], t3[:, :], ACT.Ln, bias=1.0).then_inc(s_l1, 1)
                    act.wait_ge(s_z0, 1)
                    for i in steps(act, NCT // 2):
                        for q in range(2):
                            act.wait_ge(s_mm[q], i + 1)
                            act.wait_ge(s_cv[q], i)
                            act.wait_ge(s_cs[q], 32 * i)
                            nc.scalar.copy(xp[q][:, 3:3 + SEQ], two(3 * q))
                            nc.scalar.copy(xps[q][:, 3, :], PB[:, 3 * q + 2, 0:NSMP]).then_inc(s_ev[q], 1)
                            act.wait_ge(s_ev[q], i + 1)
                            act.wait_ge(s_cw[q], 32 * (i + 1))
                            act.dma_start(o["conv_p"][2 * i + q, :, :], xp[q][:, SEQ:SEQ + 3]).then_inc(s_cs[q], 16)
                            act.dma_start(o["conv_s"][2 * i + q, :, :, :], xps[q][:, 1:4, :]).then_inc(s_cs[q], 16)
                            act.wait_ge(s_cv[q], i + 1)
                            act.wait_ge(s_st[q], 16 * i)
                            nc.scalar.activation(so[q][:, :], cv[q][:, :], ACT.Silu).then_inc(s_si[q], 1)
                            act.wait_ge(s_si[q], i + 1)
                            act.dma_start(cht_d[2 * i + q, :, :], so[q][:, :]).then_inc(s_st[q], 16)
                    for i in steps(act, 3):
                        for u in range(18):
                            q, t, b = u // 9, u % 9, u % 6
                            n = CH if t < NCH else NSMP
                            act.wait_ge(s_tm[b], 3 * i + u // 6 + 1)
                            act.wait_ge(s_ts[b], 16 * (3 * i + u // 6))
                            nc.scalar.copy(stg[b][0:n, :], PB[0:n, b, :]).then_inc(s_te[b], 1)
                            act.wait_ge(s_te[b], 3 * i + u // 6 + 1)
                            act.dma_start(tok_d[2 * i + q, t * CH:t * CH + n, :], stg[b][0:n, :]).then_inc(s_ts[b], 16)
                    for i in steps(act, NHC // 2):
                        for q in range(2):
                            act.wait_ge(s_pm[q], i + 1)
                            act.wait_ge(s_ps[q], 16 * i)
                            nc.scalar.copy(wps[q][:, :, :].rearrange("p k n -> p (k n)"), two(4 * q)).then_inc(s_pe[q], 1)
                            act.wait_ge(s_pe[q], i + 1)
                            act.dma_start(wp_d[2 * i + q, :, :, :], wps[q][:, :, :]).then_inc(s_ps[q], 16)
                    act.wait_ge(s_rr, 1)
                    for src, r, n in ((nacs, R_NACS, NH), (mrun, R_M, MH), (wlog, R_WLOG, MH),
                                      (dtr, R_DT, NH), (ir, R_G, MH), (mt, R_MT, MH)):
                        act.dma_start(rows_d[r:r + n, :], src[0:n, 0:SEQ]).then_inc(s_rs, 16)
                        act.dma_start(rows_s_d[r:r + n, :], src[0:n, SEQ:NTOK]).then_inc(s_rs, 16)
                    act.dma_start(o["p_m"], mcar[:, NCH:NCH + 1]).then_inc(s_rs, 16)
                    act.dma_start(o["s_m"], mt[:, SEQ:NTOK]).then_inc(s_rs, 16)
                    act.wait_ge(s_rs, 16 * 14)
                    for q in range(2):
                        act.wait_ge(s_st[q], 16 * NCT // 2)
                        act.wait_ge(s_cs[q], 32 * NCT // 2)
                        act.wait_ge(s_ps[q], 16 * NHC // 2)
                    for b in range(6):
                        act.wait_ge(s_ts[b], 16 * 9)

                @block.gpsimd
                def _(pool):
                    nc.gpsimd.memset(ident[:, :], 0.0).then_inc(s_id0, 1)
                    pool.wait_ge(s_id0, 1)
                    nc.gpsimd.affine_select(out=ident[:, :], in_=ident[:, :], compare_op=ALU.not_equal, fill=1.0,
                                            base=0, pattern=[[-1, P]], channel_multiplier=1).then_inc(s_id, 1)
                    pool.wait_ge(s_id, 1)

                @block.vector
                def _(dve):
                    ch = Chain(dve, c_d)
                    for q in range(2):
                        nc.vector.memset(xp[q][:, 0:3], 0.0)
                    nc.vector.memset(mcar[:, 0:1], 0.0)
                    nc.vector.memset(ones[:, :], 1.0)
                    nc.vector.memset(zros[:, :], 0.0).then_inc(s_z0, 1)
                    dve.wait_ge(s_z0, 1)
                    dve.wait_ge(s_re, 1)
                    dve.wait_ge(s_gb, 32)
                    nc.vector.tensor_scalar(dtr[:, :], dtr[:, :], gb[0:NH, 0:1], None, ALU.add)
                    nc.vector.tensor_scalar(ir[:, :], ir[:, :], gb[0:MH, 1:2], None, ALU.add)
                    ch.link(nc.vector.tensor_scalar(fr[:, :], fr[:, :], gb[0:MH, 2:3], None, ALU.add))
                    nc.vector.scalar_tensor_tensor(t1[:, :], dtr[:, :], -1.0, dtr[:, :], ALU.mult, ALU.max)
                    nc.vector.scalar_tensor_tensor(t3[:, :], fr[:, :], -1.0, fr[:, :], ALU.mult, ALU.max).then_inc(s_abs, 1)
                    dve.wait_ge(s_l1, 1)
                    nc.vector.scalar_tensor_tensor(dtr[:, :], dtr[:, :], 0.0, t1[:, :], ALU.max, ALU.add)
                    ch.link(nc.vector.scalar_tensor_tensor(fr[:, :], fr[:, :], 0.0, t3[:, :], ALU.min, ALU.subtract))
                    ch.link(nc.vector.tensor_scalar(t2[:, :], dtr[:, :], ea[:, :], None, ALU.mult))
                    for c in range(NCH):
                        s = slice(c * CH, (c + 1) * CH)
                        nc.vector.tensor_tensor_scan(nacs[:, s], ones[0:NH, :], t2[:, s], 0.0, ALU.mult, ALU.add)
                        nc.vector.tensor_tensor_scan(bcs[:, s], ones[0:MH, :], fr[:, s], 0.0, ALU.mult, ALU.add)
                    nc.vector.tensor_copy(nacs[:, SEQ:NTOK], t2[:, SEQ:NTOK])
                    ch.link(nc.vector.tensor_copy(bcs[:, SEQ:NTOK], fr[:, SEQ:NTOK]))
                    ch.link(nc.vector.tensor_tensor(ir[:, :], ir[:, :], bcs[:, :], ALU.subtract))
                    for c in range(NCH):
                        s, e = slice(c * CH, (c + 1) * CH), (c + 1) * CH - 1
                        ch.link(nc.vector.tensor_tensor_scan(mrun[:, s], zros[0:MH, :], ir[:, s], mcar[:, c:c + 1],
                                                             ALU.add, ALU.max))
                        nc.vector.tensor_scalar(wlog[:, s], mrun[:, s], -1.0, mcar[:, c:c + 1], ALU.mult, ALU.add)
                        ch.link(nc.vector.tensor_tensor(mcar[:, c + 1:c + 2], mrun[:, e:e + 1], bcs[:, e:e + 1], ALU.add))
                    s = slice(SEQ, NTOK)
                    ch.link(nc.vector.tensor_tensor(mrun[:, s], m0s[:, :], ir[:, s], ALU.max))
                    nc.vector.tensor_tensor(wlog[:, s], m0s[:, :], mrun[:, s], ALU.subtract)
                    nc.vector.tensor_tensor(mt[:, :], mrun[:, :], bcs[:, :], ALU.add).then_inc(s_rr, 1)
                    for i in steps(dve, NCT // 2):
                        cc = Chain(dve, s_e1, 6 * i)
                        for q in range(2):
                            dve.wait_ge(s_ev[q], i + 1)
                            dve.wait_ge(s_cw[q], 32 * (i + 1))
                            dve.wait_ge(s_si[q], i)
                            for tap in range(TAPS):
                                w = cw[q][:, tap:tap + 1]
                                for out, src in ((cv[q][:, 0:SEQ], xp[q][:, tap:tap + SEQ]),
                                                 (cv[q][:, SEQ:NTOK], xps[q][:, tap, :])):
                                    if tap == 0:
                                        last = nc.vector.tensor_scalar(out, src, w, cw[q][:, 4:5], ALU.mult, ALU.add)
                                    else:
                                        last = nc.vector.scalar_tensor_tensor(out, src, w, out, ALU.mult, ALU.add)
                                if tap < TAPS - 1:
                                    cc.link(last)
                            last.then_inc(s_cv[q], 1)

        end_phase()

        with ExitStack() as ctx:
            def sb(name, shape, dt=f32):
                return ctx.enter_context(nc.sbuf_tensor(name, shape, dt))

            wmq = sb("wmq", [P, MH, KT, DK])
            wmk = sb("wmk", [P, MH, KT, DK])
            cht = sb("cht", [P, NCT, CH])
            zvo = sb("zvo", [P, 6, 512])
            rows = sb("rows", [NROW, CH])
            rb = sb("rb", [P, R_DT, CH])
            L = sb("L", [P, NH + MH, CH])
            maskp = sb("maskp", [P, CH])
            onec = sb("onec", [P, 1])
            cols = sb("cols", [P, NROW])
            btok = sb("btok", [P, NG * NST])
            xtok = sb("xtok", [P, D])
            xdt = sb("xdt", [P, D])
            xdec = sb("xdec", [P, D])
            qT = sb("qT", [P, MH * KT, CH])
            kT = sb("kT", [P, MH * KT, CH])
            kw = sb("kw", [P, D])
            hT = sb("hT", [P, D])
            cst = sb("cst", [P, MH * KT, DK])
            nst = sb("nst", [P, MH * KT])
            sm = sb("sm", [P, 64])
            e_ea, e_wi, e_em = sm[:, 0:16], sm[:, 16:20], sm[:, 20:24]
            e_hd, e_wo = sb("e_hd", [P, NH]), sb("e_wo", [P, MH])
            e_de, e_ws = sb("e_de", [P, NH]), sb("e_ws", [P, MH])
            ysb = sb("ysb", [P, D])
            tmp = sb("tmp", [P, D])
            ez = sb("ez", [P, 2 * D])
            nx = sb("nx", [P, D])
            den = sb("den", [P, 8])
            num = sb("num", [P, D])
            stt = sb("stt", [P, MH, 6])
            mv = sb("mv", [P, MH, 2])
            var = sb("var", [P, 5])
            mix = sb("mix", [P, 2 * D])
            mixT = sb("mixT", [P, 16, CH])
            gs = sb("gs", [P, D])
            gm = sb("gm", [P, D])
            dsk = sb("dsk", [P, NH])
            epst = sb("epst", [P, 1])

            names = ("w ch tok rows rb pe_a pe_b pe_kk pe_st pe_ys pe_hn pe_y pe_ni pe_nx pe_c1 pe_c2 pe_tr "
                     "act_xt act_small act_qk act_l act_l2 act_ez act_nx act_sq act_mt stored "
                     "dve_arg dve_d dve_xdec dve_h dve_mm dve_kw dve_att dve_ys dve_y dve_c1 dve_c2 "
                     "dve_num dve_var dve_mix dve_end setup mask0 outs passed pad")
            s = {n: sem("scan_" + n) for n in names.split()}
            c_d, c_a = sem("dve_chain_s"), sem("act_chain_s")
            DVE_LINKS, ACT_LINKS = 19, 0

            def heads(ap, n):
                return ap.rearrange("p (h n) -> p h n", n=n)

            def scan_vector(dve, i):
                ch = Chain(dve, c_d, DVE_LINKS * i, s["passed"])
                V = nc.vector
                dve.wait_ge(s["act_xt"], i + 1)
                dve.wait_ge(s["rb"], 16 * (i + 1))
                dve.wait_ge(s["act_small"], i)
                V.tensor_tensor(e_de[:, :], cols[:, R_NACS:R_NACS + NH], rb[:, R_NACS:R_NACS + NH, CH - 1], ALU.subtract)
                V.tensor_tensor(e_ws[:, :], cols[:, R_G:R_G + MH], rb[:, R_M:R_M + MH, CH - 1], ALU.subtract).then_inc(s["dve_arg"], 1)
                dve.wait_ge(s["pe_ni"], i)
                V.tensor_tensor(L[:, :, :], rb[:, 0:NH + MH, :], maskp[:, :].unsqueeze(1).to_broadcast([P, NH + MH, CH]), ALU.add).then_inc(s["dve_d"], 1)
                dve.wait_ge(s["pe_y"], i)
                ch.link(V.tensor_tensor(heads(xdt[:, :], HD), heads(xtok[:, :], HD),
                                        cols[:, R_DT:R_DT + NH].unsqueeze(2).to_broadcast([P, NH, HD]), ALU.mult))
                dve.wait_ge(s["act_small"], i + 1)
                V.tensor_tensor(heads(xdec[:, :], HD), heads(xdt[:, :], HD),
                                e_de[:, :].unsqueeze(2).to_broadcast([P, NH, HD]), ALU.mult).then_inc(s["dve_xdec"], 1)
                dve.wait_ge(s["pe_kk"], i + 1)
                V.scalar_tensor_tensor(heads(kw[:, :], DK), heads(two(0), DK), DK ** -0.5,
                                       e_ws[:, :].unsqueeze(2).to_broadcast([P, MH, DK]), ALU.mult, ALU.mult).then_inc(s["dve_kw"], 1)
                dve.wait_ge(s["act_l"], i + 1)
                for g in range(NG):
                    last = V.tensor_tensor(L[:, g * 8:g * 8 + 8, :], L[:, g * 8:g * 8 + 8, :],
                                           PB[:, 3, g * CH:(g + 1) * CH].unsqueeze(1).to_broadcast([P, 8, CH]), ALU.mult)
                last.then_inc(s["dve_mm"], 1)
                dve.wait_ge(s["pe_st"], i + 1)
                dve.wait_ge(s["act_l2"], i + 1)
                V.tensor_tensor(L[:, NH:NH + MH, :], L[:, NH:NH + MH, :], heads(PB[:, 2, :], CH), ALU.mult).then_inc(s["dve_att"], 1)
                dve.wait_ge(s["pe_ys"], i + 1)
                V.tensor_tensor(heads(ysb[:, :], HD), heads(two(4), HD),
                                e_ea.unsqueeze(2).to_broadcast([P, NH, HD]), ALU.mult).then_inc(s["dve_ys"], 1)
                dve.wait_ge(s["dve_ys"], i + 1)
                V.tensor_tensor(heads(tmp[:, :], HD), heads(xtok[:, :], HD),
                                dsk[:, :].unsqueeze(2).to_broadcast([P, NH, HD]), ALU.mult)
                ch.link(V.tensor_tensor(heads(hT[:, :], HD), heads(hT[:, :], HD),
                                        e_hd[:, :].unsqueeze(2).to_broadcast([P, NH, HD]), ALU.mult))
                dve.wait_ge(s["pe_hn"], i + 1)
                V.tensor_tensor(hT[:, :], hT[:, :], two(6), ALU.add).then_inc(s["dve_h"], 1)
                ch.link(V.tensor_tensor(ysb[:, :], ysb[:, :], tmp[:, :], ALU.add))
                dve.wait_ge(s["pe_y"], i + 1)
                V.tensor_tensor(ysb[:, :], ysb[:, :], two(0), ALU.add).then_inc(s["dve_y"], 1)
                dve.wait_ge(s["dve_y"], i + 1)
                dve.wait_ge(s["act_ez"], i + 1)
                gate_z(dve, ch, P)
                dve.wait_ge(s["pe_ni"], i + 1)
                dve.wait_ge(s["act_nx"], i + 1)
                V.tensor_tensor(num[:, :], two(4), nx[:, :], ALU.add).then_inc(s["dve_num"], 1)
                ch.link(V.tensor_tensor(den[:, 0:4], PB[:, 3, 4:8], e_wi, ALU.mult))
                ch.link(V.tensor_tensor(den[:, 0:4], den[:, 0:4], PB[:, 3, 0:4], ALU.add))
                V.tensor_tensor(cst[:, :, :].rearrange("p (h k) v -> p h (k v)", h=MH),
                                cst[:, :, :].rearrange("p (h k) v -> p h (k v)", h=MH),
                                e_wo[:, :].unsqueeze(2).to_broadcast([P, MH, KT * DK]), ALU.mult)
                ch.link(V.tensor_tensor(heads(nst[:, :], KT), heads(nst[:, :], KT),
                                        e_wo[:, :].unsqueeze(2).to_broadcast([P, MH, KT]), ALU.mult))
                dve.wait_ge(s["pe_c1"], i + 1)
                V.tensor_tensor(nst[:, :], nst[:, :], PB[:, 2, 0:8], ALU.add)
                V.tensor_tensor(cst[:, 0:4, :].rearrange("p a v -> p (a v)"), cst[:, 0:4, :].rearrange("p a v -> p (a v)"),
                                two(0), ALU.add).then_inc(s["dve_c1"], 1)
                dve.wait_ge(s["pe_c2"], i + 1)
                V.tensor_tensor(cst[:, 4:8, :].rearrange("p a v -> p (a v)"), cst[:, 4:8, :].rearrange("p a v -> p (a v)"),
                                two(4), ALU.add).then_inc(s["dve_c2"], 1)
                head_out(dve, ch, P, i)
                assert ch.n == DVE_LINKS, ch.n

            def gate_z(dve, ch, r):
                V = nc.vector
                ch.link(V.tensor_scalar(ez[0:r, :], ez[0:r, :], 1.0, None, ALU.add))
                ch.link(V.reciprocal(ez[0:r, :], ez[0:r, :]))
                z = zvo[0:r, 0:2, :].rearrange("p a n -> p (a n)")
                ch.link(V.tensor_tensor(tmp[0:r, :], ez[0:r, 0:D], z, ALU.mult))
                ch.link(V.tensor_tensor(ysb[0:r, :], ysb[0:r, :], tmp[0:r, :], ALU.mult))
                V.tensor_tensor_reduce(out=tmp[0:r, :], in0=ysb[0:r, :], in1=ysb[0:r, :], scale=1.0 / D, scalar=EPS,
                                       op0=ALU.mult, op1=ALU.add, accum_out=var[0:r, 0:1])

            def head_out(dve, ch, r, i):
                V = nc.vector
                ch.link(V.scalar_tensor_tensor(den[0:r, 4:8], den[0:r, 0:4], -1.0, den[0:r, 0:4], ALU.mult, ALU.max))
                ch.link(V.tensor_tensor(den[0:r, 4:8], den[0:r, 4:8], e_em[0:r, :], ALU.max))
                ch.link(V.reciprocal(den[0:r, 4:8], den[0:r, 4:8]))
                ch.link(V.tensor_tensor(heads(num[0:r, :], DK), heads(num[0:r, :], DK),
                                        den[0:r, 4:8].unsqueeze(2).to_broadcast([r, MH, DK]), ALU.mult))
                for h in range(MH):
                    last = V.bn_stats(stt[0:r, h, :], num[0:r, h * DK:(h + 1) * DK])
                ch.link_plain(last)
                for h in range(MH):
                    last = V.bn_aggr(mv[0:r, h, :], stt[0:r, h, :])
                ch.link(last)
                V.tensor_scalar(var[0:r, 1:5], mv[0:r, :, 1], EPS, None, ALU.add).then_inc(s["dve_var"], 1)
                dve.wait_ge(s["act_sq"], i + 1)
                ch.link(V.reciprocal(var[0:r, :], var[0:r, :]))
                dve.wait_ge(s["pe_tr"], i)
                V.scalar_tensor_tensor(mix[0:r, 0:D], ysb[0:r, :], var[0:r, 0:1], gs[0:r, :], ALU.mult, ALU.mult)
                for h in range(MH):
                    last = V.tensor_scalar(num[0:r, h * DK:(h + 1) * DK], num[0:r, h * DK:(h + 1) * DK],
                                           mv[0:r, h, 0:1], var[0:r, 1 + h:2 + h], ALU.subtract, ALU.mult)
                ch.link(last)
                ch.link(V.tensor_tensor(num[0:r, :], num[0:r, :], gm[0:r, :], ALU.mult))
                V.tensor_tensor(mix[0:r, D:2 * D], num[0:r, :], ez[0:r, D:2 * D], ALU.mult).then_inc(s["dve_mix"], 1)

            def sqrt_step(act, r, i):
                act.wait_ge(s["dve_var"], i + 1)
                nc.scalar.activation(var[0:r, :], var[0:r, :], ACT.Sqrt).then_inc(s["act_sq"], 1)

            def mix_transposes(pe, r, i):
                pe.wait_ge(s["dve_mix"], i + 1)
                for j in range(16):
                    b = (0, 1, 6, 7)[j // 4]
                    last = nc.tensor.transpose(PB[:, b, (j % 4) * CH:(j % 4) * CH + r], mix[0:r, j * P:(j + 1) * P], ident[0:r, 0:r])
                last.then_inc(s["pe_tr"], 1)

            def mix_store(act, r, i, lo):
                act.wait_ge(s["pe_tr"], i + 1)
                act.wait_ge(s["stored"], 16 * i)
                if r < CH:
                    act.wait_ge(s["pad"], 1)
                for b, j in ((0, 0), (1, 4), (6, 8), (7, 12)):
                    last = nc.scalar.copy(mixT[:, j:j + 4, 0:r], PB[:, b, :].rearrange("p (a n) -> p a n", n=CH)[:, :, 0:r])
                last.then_inc(s["act_mt"], 1)
                act.wait_ge(s["act_mt"], i + 1)
                act.dma_start(mixt_d[:, :, bass.ds(lo, CH)].rearrange("j p t -> p j t"), mixT[:, :, :]).then_inc(s["stored"], 16)

            with nc.Block() as block:
                @block.sync
                def _(sp):
                    sp.dma_start(wmq[:, :, :, :], a["w_mq"]).then_inc(s["w"], 16)
                    sp.dma_start(wmk[:, :, :, :], a["w_mk"]).then_inc(s["w"], 16)
                    sp.dma_start(gs[:, :], a["ssd_g"].partition_broadcast(P)).then_inc(s["w"], 16)
                    sp.dma_start(gm[:, :], a["mlstm_g"].partition_broadcast(P)).then_inc(s["w"], 16)
                    sp.dma_start(dsk[:, :], a["d_skip"].partition_broadcast(P)).then_inc(s["w"], 16)
                    for i in steps(sp, NCH):
                        sp.wait_ge(s["pe_a"], i)
                        sp.dma_start(rows[:, :], rows_d[:, bass.ds(i * CH, CH)]).then_inc(s["rows"], 16)
                        sp.wait_ge(s["pe_ys"], i)
                        sp.dma_start(cht[:, :, :], cht_d[:, :, bass.ds(i * CH, CH)].rearrange("j p t -> p j t")).then_inc(s["ch"], 16)
                        sp.wait_ge(s["dve_d"], i)
                        sp.wait_ge(s["act_small"], i)
                        sp.dma_start(rb[:, :, :], rows_d[0:R_DT, bass.ds(i * CH, CH)].partition_broadcast(P)).then_inc(s["rb"], 16)
                        sp.wait_ge(s["pe_c2"], i)
                        sp.wait_ge(s["dve_mix"], i)
                        sp.dma_start(zvo[:, :, :], tok_d[:, bass.ds(i * CH, CH), :].rearrange("j t n -> t j n")).then_inc(s["tok"], 16)

                @block.tensor
                def _(pe):
                    pe.wait_ge(s["w"], 80)
                    pe.wait_ge(s["setup"], 1)
                    T = nc.tensor
                    for i in steps(pe, NCH):
                        v = zvo[:, 2:4, :].rearrange("p a n -> p (a n)")
                        pe.wait_ge(s["act_mt"], i)
                        pe.wait_ge(s["dve_mix"], i)
                        pe.wait_ge(s["rows"], 16 * (i + 1))
                        pe.sem_inc(s["passed"], 1)
                        T.transpose(PB[:, 2, 256:256 + NROW], rows[:, :], ident[0:NROW, 0:NROW])
                        pe.wait_ge(s["ch"], 16 * (i + 1))
                        for g in range(NG):
                            T.transpose(PB[:, 2, g * NST:(g + 1) * NST], cht[:, BT0 + g, :], ident[:, :])
                        for j in range(8):
                            T.transpose(two(0)[:, j * P:(j + 1) * P], cht[:, j, :], ident[:, :])
                        for g in range(NG):
                            last = T.matmul(PB[:, 3, g * CH:(g + 1) * CH], cht[:, BT0 + g, :], cht[:, CT0 + g, :], start=True, stop=True)
                        last.then_inc(s["pe_a"], 1)
                        for w, b in ((wmq, 4), (wmk, 6)):
                            for h in range(MH):
                                for e in range(KT):
                                    for k in range(KT):
                                        last = T.matmul(two(b)[:, (h * KT + e) * CH:(h * KT + e + 1) * CH],
                                                        w[:, h, k, e * P:(e + 1) * P], cht[:, UT0 + h * KT + k, :],
                                                        start=k == 0, stop=k == KT - 1)
                        last.then_inc(s["pe_b"], 1)
                        pe.wait_ge(s["act_xt"], i + 1)
                        for h in range(MH):
                            for k in range(KT):
                                last = T.matmul(two(0)[:, h * DK:(h + 1) * DK], cht[:, UT0 + h * KT + k, :], wmk[:, h, k, :],
                                                start=k == 0, stop=k == KT - 1)
                        last.then_inc(s["pe_kk"], 1)
                        pe.wait_ge(s["act_qk"], i + 1)
                        for h in range(MH):
                            for k in range(KT):
                                last = T.matmul(PB[:, 2, h * CH:(h + 1) * CH], kT[:, h * KT + k, :], qT[:, h * KT + k, :],
                                                start=k == 0, stop=k == KT - 1)
                        last.then_inc(s["pe_st"], 1)
                        for g in range(NG):
                            last = T.matmul(PB[:, 4 + g, :], cht[:, CT0 + g, :], hT[:, g * 512:(g + 1) * 512], start=True, stop=True)
                        last.then_inc(s["pe_ys"], 1)
                        pe.wait_ge(s["dve_xdec"], i + 1)
                        for g in range(NG):
                            last = T.matmul(PB[:, 6 + g, :], btok[:, g * NST:(g + 1) * NST], xdec[:, g * 512:(g + 1) * 512], start=True, stop=True)
                        last.then_inc(s["pe_hn"], 1)
                        pe.wait_ge(s["dve_mm"], i + 1)
                        pe.wait_ge(s["dve_kw"], i + 1)
                        for h in range(NH):
                            last = T.matmul(two(0)[:, h * HD:(h + 1) * HD], L[:, h, :], xdt[:, h * HD:(h + 1) * HD], start=True, stop=True)
                        last.then_inc(s["pe_y"], 1)
                        pe.wait_ge(s["dve_h"], i + 1)
                        pe.wait_ge(s["tok"], 16 * (i + 1))
                        for h in range(MH):
                            for k in range(KT):
                                last = T.matmul(two(6)[:, h * DK:(h + 1) * DK], qT[:, h * KT + k, :], cst[:, h * KT + k, :],
                                                start=k == 0, stop=k == KT - 1)
                        for h in range(MH):
                            for k in range(KT):
                                last = T.matmul(PB[:, 3, 4 + h:5 + h], qT[:, h * KT + k, :], nst[:, h * KT + k:h * KT + k + 1],
                                                start=k == 0, stop=k == KT - 1)
                        last.then_inc(s["pe_nx"], 1)
                        pe.wait_ge(s["dve_att"], i + 1)
                        pe.wait_ge(s["dve_ys"], i + 1)
                        for h in range(MH):
                            last = T.matmul(two(4)[:, h * DK:(h + 1) * DK], L[:, NH + h, :], v[:, h * DK:(h + 1) * DK], start=True, stop=True)
                        for h in range(MH):
                            last = T.matmul(PB[:, 3, h:h + 1], L[:, NH + h, :], onec[:, :], start=True, stop=True)
                        last.then_inc(s["pe_ni"], 1)
                        pe.wait_ge(s["dve_y"], i + 1)
                        for h in range(MH):
                            for k in range(KT):
                                j = h * KT + k
                                T.matmul(PB[:, 2, j:j + 1], kw[:, j * P:(j + 1) * P], onec[:, :], start=True, stop=True)
                        for j in range(4):
                            h = j // KT
                            last = T.matmul(two(0)[:, j * DK:(j + 1) * DK], kw[:, j * P:(j + 1) * P], v[:, h * DK:(h + 1) * DK], start=True, stop=True)
                        last.then_inc(s["pe_c1"], 1)
                        pe.wait_ge(s["dve_num"], i + 1)
                        for j in range(4, 8):
                            h = j // KT
                            last = T.matmul(two(4)[:, (j - 4) * DK:(j - 3) * DK], kw[:, j * P:(j + 1) * P], v[:, h * DK:(h + 1) * DK], start=True, stop=True)
                        last.then_inc(s["pe_c2"], 1)
                        pe.wait_ge(s["dve_c1"], i + 1)
                        mix_transposes(pe, P, i)

                @block.scalar
                def _(act):
                    S = nc.scalar
                    act.wait_ge(s["setup"], 1)
                    for i in steps(act, NCH):
                        ch = Chain(act, c_a, ACT_LINKS * i)
                        act.wait_ge(s["pe_a"], i + 1)
                        act.wait_ge(s["dve_mix"], i)
                        act.wait_ge(s["pe_hn"], i)
                        S.copy(cols[:, :], PB[:, 2, 256:256 + NROW])
                        S.copy(btok[:, :], PB[:, 2, 0:256])
                        S.copy(xtok[:, :], two(0)).then_inc(s["act_xt"], 1)
                        act.wait_ge(s["act_xt"], i + 1)
                        act.wait_ge(s["pe_b"], i + 1)
                        S.copy(qT[:, :, :].rearrange("p a n -> p (a n)"), two(4))
                        S.activation(kT[:, :, :].rearrange("p a n -> p (a n)"), two(6), ACT.Copy, scale=DK ** -0.5).then_inc(s["act_qk"], 1)
                        act.wait_ge(s["rb"], 16 * (i + 1))
                        S.activation(e_ea, cols[:, R_NACS:R_NACS + NH], ACT.Exp, scale=-1.0)
                        S.activation(e_wi, cols[:, R_WLOG:R_WLOG + MH], ACT.Exp)
                        S.activation(e_em, cols[:, R_MT:R_MT + MH], ACT.Exp, scale=-1.0)
                        S.activation(e_hd[:, :], rb[:, R_NACS:R_NACS + NH, CH - 1], ACT.Exp, scale=-1.0)
                        S.activation(e_wo[:, :], rb[:, R_WLOG:R_WLOG + MH, CH - 1], ACT.Exp)
                        act.wait_ge(s["dve_arg"], i + 1)
                        S.activation(e_de[:, :], e_de[:, :], ACT.Exp)
                        S.activation(e_ws[:, :], e_ws[:, :], ACT.Exp).then_inc(s["act_small"], 1)
                        act.wait_ge(s["dve_d"], i + 1)
                        for h in range(NH):
                            last = S.activation(L[:, h, :], L[:, h, :], ACT.Exp, scale=-1.0, bias=cols[:, R_NACS + h:R_NACS + h + 1])
                        last.then_inc(s["act_l"], 1)
                        for h in range(MH):
                            last = S.activation(L[:, NH + h, :], L[:, NH + h, :], ACT.Exp, scale=-1.0, bias=cols[:, R_G + h:R_G + h + 1])
                        last.then_inc(s["act_l2"], 1)
                        act.wait_ge(s["tok"], 16 * (i + 1))
                        S.activation(ez[:, 0:D], zvo[:, 0:2, :].rearrange("p a n -> p (a n)"), ACT.Exp, scale=-1.0)
                        S.activation(ez[:, D:2 * D], zvo[:, 4:6, :].rearrange("p a n -> p (a n)"), ACT.Exp, scale=-1.0).then_inc(s["act_ez"], 1)
                        act.wait_ge(s["pe_nx"], i + 1)
                        for h in range(MH):
                            last = S.activation(nx[:, h * DK:(h + 1) * DK], two(6)[:, h * DK:(h + 1) * DK], ACT.Copy, scale=e_wi[:, h:h + 1])
                        last.then_inc(s["act_nx"], 1)
                        sqrt_step(act, P, i)
                        mix_store(act, P, i, i * CH)
                    act.wait_ge(s["dve_c2"], NCH)
                    act.dma_start(o["p_ssd"], hT[:, :]).then_inc(s["outs"], 16)
                    act.dma_start(o["p_c"], cst[:, :, :]).then_inc(s["outs"], 16)
                    act.dma_start(o["p_n"], nst[:, :]).then_inc(s["outs"], 16)
                    act.wait_ge(s["outs"], 48)
                    act.wait_ge(s["stored"], 16 * NCH)

                @block.gpsimd
                def _(pool):
                    nc.gpsimd.memset(maskp[:, :], 0.0).then_inc(s["mask0"], 1)
                    pool.wait_ge(s["mask0"], 1)
                    nc.gpsimd.affine_select(out=maskp[:, :], in_=maskp[:, :], compare_op=ALU.is_ge, fill=BIG,
                                            base=0, pattern=[[1, CH]], channel_multiplier=-1).then_inc(s["mask0"], 1)
                    pool.wait_ge(s["mask0"], 2)

                @block.vector
                def _(dve):
                    nc.vector.memset(onec[:, :], 1.0)
                    nc.vector.memset(hT[:, :], 0.0)
                    nc.vector.memset(cst[:, :, :], 0.0)
                    nc.vector.memset(nst[:, :], 0.0).then_inc(s["setup"], 1)
                    dve.wait_ge(s["setup"], 1)
                    dve.wait_ge(s["mask0"], 2)
                    dve.wait_ge(s["w"], 80)
                    for i in steps(dve, NCH):
                        scan_vector(dve, i)
            build_sample(nc, a, o, locals())
        end_phase()
        build_peer(nc, a, o, locals())


def build_sample(nc, a, o, L_):
    f32 = mybir.dt.float32
    ACT = mybir.ActivationFunctionType
    ctx, PB, ident, two, heads, s, sem = (L_[k] for k in ("ctx", "PB", "ident", "two", "heads", "s", "sem"))
    zvo, den, num, ysb, ez, e_em, wmq, wmk, onec = (L_[k] for k in ("zvo", "den", "num", "ysb", "ez", "e_em", "wmq", "wmk", "onec"))
    cht_d, tok_d, rows_s_d, bc_d = (L_[k] for k in ("cht_d", "tok_d", "rows_s_d", "bc_d"))
    mixT = L_["mixT"]
    gate_z, head_out, sqrt_step, mix_transposes, mix_store = (
        L_[k] for k in ("gate_z", "head_out", "sqrt_step", "mix_transposes", "mix_store"))
    B = NSMP
    i = NCH

    def sb(name, shape, dt=f32):
        return ctx.enter_context(nc.sbuf_tensor(name, shape, dt))

    chs = sb("chs", [P, NCT, B])
    rsb = sb("rsb", [P, NROW, B])
    nas = sb("nas", [P, 8, B])
    dts = sb("dts", [P, 8, B])
    dxt = sb("dxt", [P, 8, B])
    wos, wss = sb("wos", [P, MH, B]), sb("wss", [P, MH, B])
    bcsb = sb("bcsb", [B, 4 * P])
    bb = [sb(f"bb{q}", [P, 4 * P]) for q in range(2)]
    st = [sb(f"st{q}", [P, 8, NST]) for q in range(2)]
    cs = [sb(f"cs{q}", [P, MH * KT, DK]) for q in range(2)]
    vb = [sb(f"vb{q}", [P, D]) for q in range(2)]
    tt = L_["tmp"]
    tc_ = L_["mix"]
    qs, ks = sb("qs", [P, 8, B]), sb("ks", [P, 8, B])
    ns = sb("ns", [P, 8, B])
    pr, pr2 = sb("pr", [P, 8, B]), sb("pr2", [P, 8, B])
    qd = sb("qd", [P, 8, B, B])
    ysc = sb("ysc", [P, 8, B])
    dsc = sb("dsc", [P, 8])
    ss = {n: sem("smp_" + n) for n in ("ld ld2 bct bcc bcd qk qkc exp arg ea1 kws qdz nn nst yt ytc "
                                       "st_new c_new num num_c num_e den_c").split()}
    s_in = [sem(f"smp_states_loaded{q}") for q in range(2)]
    s_out = [sem(f"smp_states_stored{q}") for q in range(2)]
    c_d = sem("dve_chain_smp")

    with nc.Block() as block:
        @block.sync
        def _(sp):
            sp.dma_start(chs[:, :, :], cht_d[:, :, SEQ:NTOK].rearrange("j p t -> p j t")).then_inc(ss["ld"], 16)
            sp.dma_start(rsb[:, :, :], rows_s_d.partition_broadcast(P)).then_inc(ss["ld"], 16)
            for half in range(2):
                sp.dma_start(nas[half * HD:(half + 1) * HD, :, :],
                             rows_s_d[R_NACS:R_NACS + NH, :].rearrange("(j two) b -> two j b", two=2)[half].partition_broadcast(HD)).then_inc(ss["ld"], 16)
                sp.dma_start(dts[half * HD:(half + 1) * HD, :, :],
                             rows_s_d[R_DT:R_DT + NH, :].rearrange("(j two) b -> two j b", two=2)[half].partition_broadcast(HD)).then_inc(ss["ld"], 16)
            sp.dma_start(ns[:, :, :], a["n_state"]).then_inc(ss["ld"], 16)
            sp.dma_start(dsc[:, :], a["d_skip_ch"]).then_inc(ss["ld"], 16)
            sp.dma_start(e_em[0:B, :], rows_s_d[R_MT:R_MT + MH, :].rearrange("h b -> b h"),
                         allow_slow_non_contiguous=True).then_inc(ss["ld"], 16)
            sp.dma_start(zvo[0:B, :, :], tok_d[:, SEQ:NTOK, :].rearrange("j t n -> t j n")).then_inc(ss["ld2"], 16)
            sp.wait_ge(ss["bcd"], 16)
            for b in range(B):
                q, n = b % 2, b // 2
                sp.wait_ge(s_out[q], 32 * n)
                sp.dma_start(st[q][:, :, :], a["ssd_state"][b].rearrange("(j p) n -> p j n", p=P)).then_inc(s_in[q], 16)
                sp.dma_start(cs[q][:, :, :], a["c_state"][b].rearrange("(j p) v -> p j v", p=P)).then_inc(s_in[q], 16)
                sp.dma_start(vb[q][:, :].rearrange("p (j n) -> p j n", j=2),
                             tok_d[2:4, SEQ + b, :].partition_broadcast(P)).then_inc(s_in[q], 16)
                sp.dma_start(bb[q][:, :], bc_d[b].rearrange("a n -> (a n)").partition_broadcast(P)).then_inc(s_in[q], 16)

        @block.tensor
        def _(pe):
            T = nc.tensor
            pe.wait_ge(ss["ld"], 16 * 9)
            for g in range(4):
                last = T.transpose(PB[0:B, 2, g * P:(g + 1) * P], chs[:, BT0 + g, :], ident[:, :])
            last.then_inc(ss["bct"], 1)
            for w, bank in ((wmq, 4), (wmk, 5)):
                for h in range(MH):
                    for e in range(KT):
                        for k in range(KT):
                            last = T.matmul(PB[:, bank, (h * KT + e) * B:(h * KT + e + 1) * B], w[:, h, k, e * P:(e + 1) * P],
                                            chs[:, UT0 + h * KT + k, :], start=k == 0, stop=k == KT - 1)
            last.then_inc(ss["qk"], 1)
            pe.wait_ge(ss["qdz"], 1)
            for b in range(B):
                pe.wait_ge(ss["c_new"], b + 1)
                for h in range(MH):
                    for k in range(KT):
                        j = h * KT + k
                        last = T.matmul(PB[0:B, (0, 1, 6, 7)[h], 0:DK],
                                        qd[:, j, b, :], cs[b % 2][:, j, :],
                                        start=b == 0 and k == 0, stop=b == B - 1 and k == KT - 1)
                last.then_inc(ss["num"], 1)
            pe.wait_ge(ss["nn"], 1)
            for h in range(MH):
                for k in range(KT):
                    last = T.matmul(PB[0:B, 3, h:h + 1], pr[:, h * KT + k, :], onec[:, :], start=k == 0, stop=k == KT - 1)
            pe.wait_ge(ss["yt"], 1)
            for j in range(8):
                last = T.transpose(two(4)[0:B, j * P:(j + 1) * P], ysc[:, j, :], ident[:, :])
            last.then_inc(ss["ytc"], 1)
            pe.wait_ge(ss["num_e"], 1)
            mix_transposes(pe, B, i)

        @block.scalar
        def _(act):
            S = nc.scalar
            act.wait_ge(ss["ld"], 16 * 9)
            S.activation(nas[:, :, :], nas[:, :, :], ACT.Exp, scale=-1.0)
            S.activation(wos[:, :, :], rsb[:, R_WLOG:R_WLOG + MH, :], ACT.Exp)
            S.activation(e_em[0:B, :], e_em[0:B, :], ACT.Exp, scale=-1.0)
            act.wait_ge(ss["arg"], 1)
            S.activation(wss[:, :, :], wss[:, :, :], ACT.Exp).then_inc(ss["exp"], 1)
            act.wait_ge(ss["bct"], 1)
            S.copy(bcsb[:, :], PB[0:B, 2, :]).then_inc(ss["bcc"], 1)
            act.wait_ge(ss["bcc"], 1)
            act.dma_start(bc_d.rearrange("b a n -> b (a n)"), bcsb[:, :]).then_inc(ss["bcd"], 16)
            act.wait_ge(ss["qk"], 1)
            S.copy(qs[:, :, :].rearrange("p a b -> p (a b)"), PB[:, 4, 0:64])
            S.activation(ks[:, :, :].rearrange("p a b -> p (a b)"), PB[:, 5, 0:64], ACT.Copy, scale=DK ** -0.5).then_inc(ss["qkc"], 1)
            act.wait_ge(ss["ld2"], 16)
            S.activation(ez[0:B, 0:D], zvo[0:B, 0:2, :].rearrange("p a n -> p (a n)"), ACT.Exp, scale=-1.0)
            S.activation(ez[0:B, D:2 * D], zvo[0:B, 4:6, :].rearrange("p a n -> p (a n)"), ACT.Exp, scale=-1.0).then_inc(ss["ea1"], 1)
            for b in range(B):
                act.wait_ge(ss["st_new"], b + 1)
                act.dma_start(o["s_ssd"][b].rearrange("(j p) n -> p j n", p=P), st[b % 2][:, :, :]).then_inc(s_out[b % 2], 16)
                act.wait_ge(ss["c_new"], b + 1)
                act.wait_ge(ss["num"], b + 1)
                act.dma_start(o["s_c"][b].rearrange("(j p) v -> p j v", p=P), cs[b % 2][:, :, :]).then_inc(s_out[b % 2], 16)
            act.wait_ge(ss["nn"], 1)
            act.dma_start(o["s_n"], ns[:, :, :]).then_inc(ss["nst"], 16)
            sqrt_step(act, B, i)
            mix_store(act, B, i, SEQ)
            act.wait_ge(ss["nst"], 16)
            for q in range(2):
                act.wait_ge(s_out[q], 16 * B)
            act.wait_ge(s["stored"], 16 * (NCH + 1))

        @block.vector
        def _(dve):
            V = nc.vector
            ch = Chain(dve, c_d, 0, s["passed"])
            dve.wait_ge(s["stored"], 16 * NCH)
            V.memset(mixT[:, :, :], 0.0).then_inc(s["pad"], 1)
            ch.link(V.memset(qd[:, :, :, :], 0.0))
            dve.wait_ge(ss["ld"], 16 * 9)
            V.tensor_tensor(wss[:, :, :], rsb[:, R_G:R_G + MH, :], rsb[:, R_M:R_M + MH, :], ALU.subtract).then_inc(ss["arg"], 1)
            V.tensor_tensor(dxt[:, :, :], dts[:, :, :], chs[:, 0:8, :], ALU.mult)
            ch.link(V.tensor_tensor(ysc[:, :, :], chs[:, 0:8, :], dsc[:, :].unsqueeze(2).to_broadcast([P, 8, B]), ALU.mult))
            dve.wait_ge(ss["qkc"], 1)
            dve.wait_ge(ss["exp"], 1)
            V.tensor_copy(qd[:, :, :, :].rearrange("p a b c -> p a (b c)")[:, :, ::B + 1], qs[:, :, :]).then_inc(ss["qdz"], 1)

            def by_head(ap):
                return ap[:, :, :].rearrange("p (h k) b -> p h k b", k=KT)

            ch.link(V.tensor_tensor(by_head(ks), by_head(ks), wss[:, :, :].unsqueeze(2).to_broadcast([P, MH, KT, B]), ALU.mult))
            ch.link(V.tensor_tensor(by_head(ns), by_head(ns), wos[:, :, :].unsqueeze(2).to_broadcast([P, MH, KT, B]), ALU.mult))
            ch.link(V.tensor_tensor(ns[:, :, :], ns[:, :, :], ks[:, :, :], ALU.add))
            V.tensor_tensor(pr[:, :, :], ns[:, :, :], qs[:, :, :], ALU.mult).then_inc(ss["nn"], 1)
            for b in range(B):
                q = b % 2
                dve.wait_ge(s_in[q], 64 * (b // 2 + 1))
                x3 = [P, 8, NST]

                def group(col):
                    return bb[q][:, col * P:(col + 2) * P].rearrange("p (g n) -> p g n", g=2).unsqueeze(2).to_broadcast([P, 2, 4, NST])

                t3 = tt[:, :].rearrange("p (j n) -> p j n", j=8)
                V.tensor_tensor(st[q][:, :, :], st[q][:, :, :], nas[:, :, b:b + 1].to_broadcast(x3), ALU.mult)
                ch.link(V.tensor_tensor(t3.rearrange("p (g r) n -> p g r n", g=2), group(0),
                                        dxt[:, :, b:b + 1].rearrange("p (g r) n -> p g r n", g=2).to_broadcast([P, 2, 4, NST]), ALU.mult))
                V.tensor_tensor(st[q][:, :, :], st[q][:, :, :], t3, ALU.add).then_inc(ss["st_new"], 1)
                dve.wait_ge(ss["st_new"], b + 1)
                ch.link(V.tensor_tensor(t3.rearrange("p (g r) n -> p g r n", g=2), st[q][:, :, :].rearrange("p (g r) n -> p g r n", g=2), group(2), ALU.mult))
                ch.link(V.tensor_reduce(pr2[:, :, b], t3, mybir.AxisListType.X, ALU.add))
                c4 = cs[q][:, :, :].rearrange("p (h k) v -> p h (k v)", k=KT)
                V.tensor_tensor(c4, c4, wos[:, :, b:b + 1].to_broadcast([P, MH, KT * DK]), ALU.mult)
                t4 = tc_[:, :].rearrange("p (h k v) -> p h k v", h=MH, k=KT)
                ch.link(V.tensor_tensor(t4, vb[q][:, :].rearrange("p (h v) -> p h v", h=MH).unsqueeze(2).to_broadcast([P, MH, KT, DK]),
                                        ks[:, :, b:b + 1].rearrange("p (h k) b -> p h k b", k=KT).to_broadcast([P, MH, KT, DK]), ALU.mult))
                V.tensor_tensor(cs[q][:, :, :].rearrange("p a v -> p (a v)"), cs[q][:, :, :].rearrange("p a v -> p (a v)"), tc_[:, :], ALU.add).then_inc(ss["c_new"], 1)
                dve.wait_ge(ss["c_new"], b + 1)
            V.tensor_tensor(ysc[:, :, :], ysc[:, :, :], pr2[:, :, :], ALU.add).then_inc(ss["yt"], 1)
            dve.wait_ge(ss["ytc"], 1)
            V.tensor_copy(ysb[0:B, :], two(4)[0:B, :])
            for h in range(MH):
                V.tensor_copy(num[0:B, h * DK:(h + 1) * DK], PB[0:B, (0, 1, 6, 7)[h], 0:DK])
            ch.link(V.tensor_copy(den[0:B, 0:4], PB[0:B, 3, 0:4]))
            V.engine_nop().then_inc(ss["num_e"], 1)
            dve.wait_ge(ss["ea1"], 1)
            gate_z(dve, ch, B)
            head_out(dve, ch, B, i)


def build_peer(nc, a, o, L_):
    f32, u32 = mybir.dt.float32, mybir.dt.uint32
    ACT = mybir.ActivationFunctionType
    X = mybir.AxisListType.X
    PB, ident, two, sem = (L_[k] for k in ("PB", "ident", "two", "sem"))
    mixt_d, wp_d, x1_d = (L_[k] for k in ("mixt_d", "wp_d", "x1_d"))
    V = nc.vector
    T = nc.tensor

    with ExitStack() as ctx:
        def sb(name, shape, dt=f32):
            return ctx.enter_context(nc.sbuf_tensor(name, shape, dt))

        wo = sb("wo", [P, 16, D])
        wp = sb("wp", [P, NHC, KD, NK])
        work = sb("work", [P, 2 * D])
        mt = work[:, :].rearrange("p (j t) -> p j t", j=16)
        x1T = work[:, 0:D].rearrange("p (k t) -> p k t", k=KD)
        sc = work[:, :].rearrange("p (j n) -> p j n", j=NHC)
        cand = work[:, :].rearrange("p (h n) -> p h n", h=PH)
        eq = work[:, :].rearrange("p (g k) -> p g k", k=TOPK)
        x1 = sb("x1", [P, D])
        g1, b1, g2, b2 = (sb(n, [P, D]) for n in ("g1", "b1", "g2", "b2"))
        vals = sb("vals", [P, NHC, TOPK])
        idx = sb("idx", [P, NHC, TOPK], u32)
        idf = idx[:, :, :].bitcast(f32)
        topv = sb("topv", [P, PH, TOPK])
        pos = sb("pos", [P, PH, TOPK], u32)
        pa = sb("pa", [P, 2, PH, TOPK], u32)
        paf = pa[:, :, :, :].bitcast(f32)
        io = sb("io", [P, TOPK])
        iou = sb("iou", [P, TOPK], mybir.dt.int32)
        e2 = sb("e2", [P, 2, PH, TOPK])
        ef = e2[:, 0, :, :]
        eo = sb("eo", [P, PH, TOPK], u32)
        gt = sb("gt", [P, PH, TOPK])
        sg = sb("sg", [P, PH])
        st6, mv = sb("st6", [P, 2, 6]), sb("mv1", [P, 2])
        ub, vbf = sb("ub", [P, NB, D]), sb("vbf", [P, NB, D])
        ixg = sb("ixg", [P, PH, TOPK], u32)
        gg = sb("gg", [P, PH, TOPK])
        hid, wg = sb("hid", [P, 2, TOPK]), sb("wg", [P, 2, TOPK])
        dg = sb("dg", [P, 2, P])
        x1g, acc = sb("x1g", [P, D]), sb("acc", [P, D])
        st7, mv7 = sb("st7", [P, 2, 6]), sb("mv7", [P, 2])
        x1s, us = wo[:, 0:NSMP, :], wo[:, NSMP:2 * NSMP, :]
        vs = wp[:, :, :, :].rearrange("p a b c -> p (a b c)").rearrange("p (b n) -> p b n", n=D)
        ixs = sb("ixs", [P, NSMP], u32)
        ggs, hids, wgs = sb("ggs", [P, NSMP]), sb("hids", [P, NSMP]), sb("wgs", [P, NSMP, NSMP])

        s = {n: sem("pk_" + n) for n in (
            "w mt xr mix var sq x1 x1t x1tc sco scc top exp out iota iou passed ix_lo ix_hi x1g "
            "dot gelu gate diag pv ysum yvar ysq y stored ident x1st smp dots gates gz go tr trc").split()}
        s_u = [sem(f"u_rows{n}") for n in range(NB)]
        s_v = [sem(f"v_rows{n}") for n in range(NB)]
        s_us = [sem(f"smp_u{n}") for n in range(NSMP)]
        s_vs = [sem(f"smp_v{n}") for n in range(NSMP)]
        c_p, c_y, c_s = sem("dve_chain_pick"), sem("dve_chain_norm"), sem("dve_chain_last")
        PICK_LINKS, NORM_LINKS = 123, 4

        def pe_pick(pe, t, h, k):
            if h < 2:
                if (h, k) == (0, 0):
                    pe.wait_ge(s["mt"], 16 * (t + 1))
                    free(pe, s["scc"], t)
                last = T.matmul(PB[:, 4 + h, :], mt[:, k, :], wo[:, k, h * 512:(h + 1) * 512], start=k == 0, stop=k == 15)
                if (h, k) == (1, 15):
                    last.then_inc(s["mix"], 1)
            elif h == 2 and k >= 12:
                if k == 12:
                    pe.wait_ge(s["x1"], t + 1)
                    pe.sem_inc(s["passed"], 1)
                for j in (2 * (k - 12), 2 * (k - 12) + 1):
                    last = T.transpose(PB[:, 6 + j // 4, (j % 4) * CH:(j % 4 + 1) * CH], x1[:, j * P:(j + 1) * P], ident[:, :])
                if k == 15:
                    last.then_inc(s["x1t"], 1)
            elif h in (3, 4):
                if (h, k) == (3, 0):
                    pe.wait_ge(s["x1tc"], t + 1)
                n, kk = 2 * (h - 3) + k // 8, k % 8
                last = T.matmul(PB[:, 4 + n, :].rearrange("p (h n) -> p h n", h=4), x1T[:, kk, :], wp[:, 4 * n:4 * n + 4, kk, :],
                                start=kk == 0, stop=kk == KD - 1)
                if (h, k) == (4, 15):
                    last.then_inc(s["sco"], 1)

        def act_pick(act, t, h, k):
            if (h, k) == (2, 4):
                act.wait_ge(s["var"], t + 1)
                nc.scalar.activation(mv[:, 1:2], mv[:, 1:2], ACT.Sqrt).then_inc(s["sq"], 1)
            elif (h, k) == (2, 15):
                act.wait_ge(s["x1t"], t + 1)
                nc.scalar.copy(work[:, 0:D], two(6)).then_inc(s["x1tc"], 1)
            elif (h, k) == (5, 0):
                act.wait_ge(s["sco"], t + 1)
                nc.scalar.copy(work[:, 0:D], two(4))
                nc.scalar.copy(work[:, D:2 * D], two(6)).then_inc(s["scc"], 1)
            elif (h, k) == (7, 2):
                act.wait_ge(s["top"], t + 1)
                nc.scalar.activation(gt[:, :, :], gt[:, :, :], ACT.Exp).then_inc(s["exp"], 1)

        def top16(ch, src, val, ind):
            ch.link_plain(V.max(val[:, 0:8], src))
            V.max_index(ind[:, 0:8], val[:, 0:8], src)
            ch.link_plain(V.match_replace(src, val[:, 0:8], src, NEG))
            ch.link_plain(V.max(val[:, 8:16], src))
            ch.link(V.max_index(ind[:, 8:16], val[:, 8:16], src))

        def dve_pick(dve, ch, t, h, k):
            if (h, k) == (2, 0):
                dve.wait_ge(s["mix"], t + 1)
                dve.wait_ge(s["xr"], 16 * (t + 1))
                ch.link(V.scalar_tensor_tensor(x1[:, :], x1[:, :], ALPHA, two(4), ALU.mult, ALU.add))
            elif (h, k) == (2, 1):
                V.bn_stats(st6[:, 0, :], x1[:, 0:512])
                ch.link_plain(V.bn_stats(st6[:, 1, :], x1[:, 512:D]))
            elif (h, k) == (2, 2):
                ch.link(V.bn_aggr(mv[:, :], st6[:, :, :]))
                V.tensor_scalar(mv[:, 1:2], mv[:, 1:2], EPS, None, ALU.add).then_inc(s["var"], 1)
            elif (h, k) == (2, 5):
                dve.wait_ge(s["sq"], t + 1)
                ch.link(V.reciprocal(mv[:, 1:2], mv[:, 1:2]))
                ch.link(V.tensor_scalar(x1[:, :], x1[:, :], mv[:, 0:1], mv[:, 1:2], ALU.subtract, ALU.mult))
            elif (h, k) == (2, 7):
                ch.link(V.tensor_tensor(x1[:, :], x1[:, :], g1[:, :], ALU.mult))
            elif (h, k) == (2, 9):
                V.tensor_tensor(x1[:, :], x1[:, :], b1[:, :], ALU.add).then_inc(s["x1"], 1)
            elif h == 5:
                if k == 0:
                    dve.wait_ge(s["scc"], t + 1)
                    dve.sem_inc(s["passed"], 1)
                top16(ch, sc[:, k, :], vals[:, k, :], idx[:, k, :])
            elif h == 6 and k % 2 == 0:
                j = k // 2
                if j == 0:
                    ch.link(V.tensor_copy(idf, idx[:, :, :]))
                ch.link_plain(V.tensor_tensor(cand[:, j, :].rearrange("p (x y) -> p x y", x=TOPK),
                                              vals[:, 2 * j, :].unsqueeze(2).to_broadcast([P, TOPK, TOPK]),
                                              vals[:, 2 * j + 1, :].unsqueeze(1).to_broadcast([P, TOPK, TOPK]), ALU.add))
                top16(ch, cand[:, j, :], topv[:, j, :], pos[:, j, :])
            elif (h, k) == (7, 0):
                V.tensor_tensor(gt[:, :, :], topv[:, :, :], topv[:, :, 0:1].to_broadcast([P, PH, TOPK]), ALU.subtract).then_inc(s["top"], 1)
                V.tensor_scalar(pa[:, 0, :, :], pos[:, :, :], 4, None, ALU.logical_shift_right)
                ch.link(V.tensor_scalar(pa[:, 1, :, :], pos[:, :, :], TOPK - 1, None, ALU.bitwise_and))
                ch.link(V.tensor_copy(paf, pa[:, :, :, :]))
            elif h == 7 and 1 <= k <= 6:
                c = (k - 1) // 3
                if k % 3 == 1:
                    ch.link(V.tensor_tensor(eq, paf[:, c, :, :].rearrange("p h k -> p (h k)").unsqueeze(2).to_broadcast([P, P, TOPK]),
                                            io[:, :].unsqueeze(1).to_broadcast([P, P, TOPK]), ALU.is_equal))
                elif k % 3 == 2:
                    q4 = eq.rearrange("p (h k) x -> p h k x", h=PH)
                    ch.link(V.tensor_tensor(q4, q4, idf.rearrange("p (h c) k -> p h c k", c=2)[:, :, c, :].unsqueeze(2).to_broadcast([P, PH, TOPK, TOPK]), ALU.mult))
                else:
                    ch.link(V.tensor_reduce(e2[:, c, :, :].rearrange("p h k -> p (h k)"), eq, X, ALU.add))
            elif (h, k) == (7, 7):
                ch.link(V.scalar_tensor_tensor(ef, ef, float(NK), e2[:, 1, :, :], ALU.mult, ALU.add))
            elif (h, k) == (7, 8):
                dve.wait_ge(s["exp"], t + 1)
                ch.link(V.tensor_reduce(sg[:, :], gt[:, :, :], X, ALU.add))
                ch.link(V.reciprocal(sg[:, :], sg[:, :]))
                ch.link(V.tensor_tensor(gt[:, :, :], gt[:, :, :], sg[:, :].unsqueeze(2).to_broadcast([P, PH, TOPK]), ALU.mult))
            elif (h, k) == (7, 9):
                V.tensor_copy(ixg[:, 0:4, :], ef[:, 0:4, :]).then_inc(s["ix_lo"], 1)

        def pe_expert(pe, c, h, k):
            if isinstance(c, int) and c == 0 and h == 0:
                return
            hh = PH * c + h - 1
            pe.wait_ge(s["diag"], TOPK * hh + k + 1)
            pe.wait_ge(s_v[k % NB], 16 * (4 * hh + k // NB + 1))
            if (h, k) == (1, 0):
                free(pe, s["ysum"], c)
            for n in range(2):
                last = T.matmul(PB[:, n, :], dg[:, k % 2, :], vbf[:, k % NB, n * 512:(n + 1) * 512],
                                start=(h, k) == (1, 0), stop=(h, k) == (0, 15))
            last.then_inc(s["pv"], 1)

        def act_expert(act, c, h, k):
            if not (isinstance(c, int) and c == 0 and h == 0):
                hh = PH * c + h - 1
                if k == 0:
                    act.wait_ge(s["gate"], hh + 1)
                free(act, s["pv"], TOPK * hh + k - 1)
                nc.scalar.activation(dg[:, k % 2, :], ident[:, :], ACT.Copy, scale=wg[:, (h - 1) % 2, k:k + 1]).then_inc(s["diag"], 1)

        def act_gelu(act, c, h):
            act.wait_ge(s["dot"], TOPK * (PH * c + h + 1))
            nc.scalar.activation(hid[:, h % 2, :], hid[:, h % 2, :], ACT.Gelu).then_inc(s["gelu"], 1)

        def act_norm(act, c, k):
            if k == 7:
                act.wait_ge(s["yvar"], c)
                nc.scalar.activation(mv7[:, 1:2], mv7[:, 1:2], ACT.Sqrt).then_inc(s["ysq"], 1)
            elif k == 15:
                act.wait_ge(s["y"], c)
                act.dma_start(o["y"][bass.ds((c - 1) * CH, CH), :], acc[:, :]).then_inc(s["stored"], 16)

        def dve_norm(dve, ch, c, k):
            if k == 2:
                dve.wait_ge(s["pv"], TOPK * PH * c)
                V.tensor_tensor(acc[:, :], acc[:, :], two(0), ALU.add).then_inc(s["ysum"], 1)
                dve.wait_ge(s["ysum"], c)
            elif k == 3:
                V.bn_stats(st7[:, 0, :], acc[:, 0:512])
                ch.link_plain(V.bn_stats(st7[:, 1, :], acc[:, 512:D]))
            elif k == 4:
                ch.link(V.bn_aggr(mv7[:, :], st7[:, :, :]))
                V.tensor_scalar(mv7[:, 1:2], mv7[:, 1:2], EPS, None, ALU.add).then_inc(s["yvar"], 1)
            elif k == 8:
                dve.wait_ge(s["ysq"], c)
                ch.link(V.reciprocal(mv7[:, 1:2], mv7[:, 1:2]))
            elif k == 9:
                ch.link(V.tensor_scalar(acc[:, :], acc[:, :], mv7[:, 0:1], mv7[:, 1:2], ALU.subtract, ALU.mult))
            elif k == 11:
                V.tensor_tensor(acc[:, :], acc[:, :], g2[:, :], ALU.mult).then_inc(s["ymul"], 1)
                dve.wait_ge(s["ymul"], c)
            elif k == 13:
                V.tensor_tensor(acc[:, :], acc[:, :], b2[:, :], ALU.add).then_inc(s["y"], 1)

        s["ymul"] = sem("pk_ymul")


        def dve_start(dve, c):
            if not (isinstance(c, int) and c == 0):
                if not (isinstance(c, int) and c == 1):
                    free(dve, s["stored"], 16 * (c - 1))
                V.tensor_scalar(acc[:, :], x1g[:, :], ALPHA, None, ALU.mult).then_inc(s["acc0"], 1)
                dve.wait_ge(s["acc0"], c)
            V.tensor_copy(gg[:, :, :], gt[:, :, :])
            V.tensor_copy(x1g[:, :], x1[:, :]).then_inc(s["x1g"], 1)
            dve.wait_ge(s["x1g"], c + 1)

        s["acc0"] = sem("pk_acc0")

        with nc.Block() as block:
            @block.sync
            def _(sp):
                sp.dma_start(wo[:, :, :], a["w_out"]).then_inc(s["w"], 16)
                for j in range(NHC):
                    sp.dma_start(wp[:, j, :, :], wp_d[j]).then_inc(s["w"], 16)
                for dst, name in ((g1, "ln1_g"), (b1, "ln1_b"), (g2, "ln2_g"), (b2, "ln2_b")):
                    sp.dma_start(dst[:, :], a[name].partition_broadcast(P)).then_inc(s["w"], 16)

                def load(t):
                    free(sp, s["ix_lo"], t)
                    sp.dma_start(work[:, :].rearrange("p (j t) -> p j t", j=16),
                                 mixt_d[:, :, bass.ds(t * CH, CH)].rearrange("j p t -> p j t")).then_inc(s["mt"], 16)
                    free(sp, s["x1g"], t)
                    sp.dma_start(x1[:, :], a["x_tok"][bass.ds(t * CH, CH), :]).then_inc(s["xr"], 16)

                load(0)
                for c in steps(sp, NCH):
                    load(c + 1)
                sp.wait_ge(s["x1st"], 16)
                sp.dma_start(x1s, x1_d.partition_broadcast(P)).then_inc(s["smp"], 16)

            @block.gpsimd
            def _(pool):
                nc.gpsimd.iota(iou[:, :], [[1, TOPK]], 0, 0).then_inc(s["iou"], 1)
                pool.wait_ge(s["iou"], 1)

                def gather(buf, table, index, done):
                    pool.indirect_dma_start(out=buf, out_offset=None, in_=a[table],
                                            in_offset=bass.IndirectOffsetOnAxis(ap=index, axis=0)).then_inc(done, 16)

                def gathers(c, h, k):
                    hh = PH * c + h
                    u_now = not (isinstance(c, int) and c == NCH)
                    v_now = not (isinstance(c, int) and c == 0 and h == 0)
                    if (h, k) == (0, 0) and u_now:
                        pool.wait_ge(s["ix_lo"], c + 1)
                    if (h, k) == (4, 0):
                        pool.wait_ge(s["ix_hi"], c + 1)
                    if u_now:
                        free(pool, s["dot"], TOPK * hh + k + 1 - NB)
                    if v_now:
                        free(pool, s["pv"], TOPK * (hh - 1) + k + 1 - NB)
                    pool.sem_inc(s["passed"], 1)
                    if u_now:
                        gather(ub[:, k % NB, :], "peer_u", ixg[:, h, k:k + 1], s_u[k % NB])
                    if v_now:
                        gather(vbf[:, k % NB, :], "peer_v", ixg[:, (h - 1) % PH, k:k + 1], s_v[k % NB])

                for c in steps(pool, NCH):
                    for h in range(PH):
                        for k in range(TOPK):
                            gathers(c, h, k)
                for k in range(TOPK):
                    gathers(NCH, 0, k)
                pool.wait_ge(s["trc"], 1)
                for b in range(NSMP):
                    gather(us[:, b, :], "peer_u", ixs[:, b:b + 1], s_us[b])
                    gather(vs[:, b, :], "peer_v", ixs[:, b:b + 1], s_vs[b])

            @block.vector
            def _(dve):
                V.memset(wgs[:, :, :], 0.0)
                dve.wait_ge(s["iou"], 1)
                V.tensor_copy(io[:, :], iou[:, :]).then_inc(s["iota"], 1)
                dve.wait_ge(s["iota"], 1)
                dve.wait_ge(s["w"], 16 * (NHC + 5))
                ch = Chain(dve, c_p, 0, s["passed"])
                for h in range(PH):
                    for k in range(TOPK):
                        dve_pick(dve, ch, 0, h, k)
                assert ch.n == PICK_LINKS, ch.n
                for c in steps(dve, NCH):
                    ch = Chain(dve, c_p, PICK_LINKS * (c + 1), s["passed"])
                    cy = Chain(dve, c_y, NORM_LINKS * (c - 1), s["passed"])
                    first = isinstance(c, int) and c == 0
                    dve_start(dve, c)
                    for h in range(PH):
                        hh = PH * c + h
                        for k in range(TOPK):
                            dve.wait_ge(s_u[k % NB], 16 * (4 * hh + k // NB + 1))
                            V.tensor_tensor_reduce(out=ub[:, k % NB, :], in0=ub[:, k % NB, :], in1=x1g[:, :], scale=1.0, scalar=0.0,
                                                   op0=ALU.mult, op1=ALU.add, accum_out=hid[:, h % 2, k:k + 1]).then_inc(s["dot"], 1)
                            if h == 1 and not first:
                                dve_norm(dve, cy, c, k)
                            if (h, k) == (1, 5):
                                V.tensor_copy(ixg[:, 4:8, :], ef[:, 4:8, :]).then_inc(s["ix_hi"], 1)
                            dve_pick(dve, ch, c + 1, h, k)
                        dve.wait_ge(s["gelu"], hh + 1)
                        if not (first and h < 2):
                            dve.wait_ge(s["pv"], TOPK * (hh - 1))
                        V.tensor_tensor(wg[:, h % 2, :], hid[:, h % 2, :], gg[:, h, :], ALU.mult).then_inc(s["gate"], 1)
                        dve.wait_ge(s["gate"], hh + 1)
                    assert first or cy.n == NORM_LINKS, cy.n
                c, r = NCH, NSMP
                cy = Chain(dve, c_y, NORM_LINKS * (c - 1), s["passed"])
                dve.wait_ge(s["stored"], 16 * (c - 1))
                V.tensor_scalar(acc[:, :], x1g[:, :], ALPHA, None, ALU.mult).then_inc(s["acc0"], 1)
                dve.wait_ge(s["acc0"], c)
                dve.wait_ge(s["tr"], 1)
                V.tensor_copy(ixs[:, :], PB[:, 4, 0:r])
                V.tensor_copy(ggs[:, :], PB[:, 4, r:2 * r]).then_inc(s["trc"], 1)
                dve.wait_ge(s["smp"], 16)
                for b in range(r):
                    dve.wait_ge(s_us[b], 16)
                    last = V.tensor_tensor_reduce(out=us[:, b, :], in0=us[:, b, :], in1=x1s[:, b, :], scale=1.0, scalar=0.0,
                                                  op0=ALU.mult, op1=ALU.add, accum_out=hids[:, b:b + 1])
                last.then_inc(s["dots"], 1)
                for k in range(TOPK):
                    dve_norm(dve, cy, c, k)
                dve.wait_ge(s["gates"], 1)
                V.tensor_tensor(wgs[:, :, :].rearrange("p a b -> p (a b)")[:, ::r + 1], hids[:, :], ggs[:, :], ALU.mult).then_inc(s["gz"], 1)
                dve.wait_ge(s["go"], 1)
                ch = Chain(dve, c_s, 0, s["passed"])
                ch.link(V.scalar_tensor_tensor(x1[0:r, :], x1[0:r, :], ALPHA, two(6)[0:r, :], ALU.mult, ALU.add))
                for n in range(2):
                    last = V.bn_stats(st6[0:r, n, :], x1[0:r, n * 512:(n + 1) * 512])
                ch.link(last)
                ch.link(V.bn_aggr(mv[0:r, :], st6[0:r, :, :]))
                V.tensor_scalar(mv[0:r, 1:2], mv[0:r, 1:2], EPS, None, ALU.add).then_inc(s["var"], 1)
                dve.wait_ge(s["sq"], NCH + 2)
                ch.link(V.reciprocal(mv[0:r, 1:2], mv[0:r, 1:2]))
                ch.link(V.tensor_scalar(x1[0:r, :], x1[0:r, :], mv[0:r, 0:1], mv[0:r, 1:2], ALU.subtract, ALU.mult))
                ch.link(V.tensor_tensor(x1[0:r, :], x1[0:r, :], g2[0:r, :], ALU.mult))
                V.tensor_tensor(x1[0:r, :], x1[0:r, :], b2[0:r, :], ALU.add).then_inc(s["x1"], 1)

            @block.scalar
            def _(act):
                for h in range(PH):
                    for k in range(TOPK):
                        act_pick(act, 0, h, k)
                for c in steps(act, NCH):
                    for h in range(PH):
                        for k in range(TOPK):
                            act_expert(act, c, h, k)
                            if h == 1 and not (isinstance(c, int) and c == 0):
                                act_norm(act, c, k)
                            act_pick(act, c + 1, h, k)
                        act_gelu(act, c, h)
                act.wait_ge(s["x1"], NCH + 1)
                act.dma_start(x1_d, x1[0:NSMP, :]).then_inc(s["x1st"], 16)
                for k in range(TOPK):
                    act_expert(act, NCH, 0, k)
                act.wait_ge(s["dots"], 1)
                nc.scalar.activation(hids[:, :], hids[:, :], ACT.Gelu).then_inc(s["gates"], 1)
                for k in range(TOPK):
                    act_norm(act, NCH, k)
                act.wait_ge(s["var"], NCH + 2)
                nc.scalar.activation(mv[0:NSMP, 1:2], mv[0:NSMP, 1:2], ACT.Sqrt).then_inc(s["sq"], 1)
                act.wait_ge(s["x1"], NCH + 2)
                act.dma_start(o["y"][SEQ:NTOK, :], x1[0:NSMP, :]).then_inc(s["stored"], 16)
                act.wait_ge(s["stored"], 16 * (NCH + 1))

            @block.tensor
            def _(pe):
                pe.wait_ge(s["w"], 16 * (NHC + 5))
                for h in range(PH):
                    for k in range(TOPK):
                        pe_pick(pe, 0, h, k)
                for c in steps(pe, NCH):
                    for h in range(PH):
                        for k in range(TOPK):
                            pe_expert(pe, c, h, k)
                            pe_pick(pe, c + 1, h, k)
                pe.wait_ge(s["ix_lo"], NCH + 1)
                T.transpose(PB[:, 4, 0:NSMP], e2[0:NSMP, 0, :, :].rearrange("p h k -> p (h k)"), ident[0:NSMP, 0:NSMP])
                T.transpose(PB[:, 4, NSMP:2 * NSMP], gt[0:NSMP, :, :].rearrange("p h k -> p (h k)"), ident[0:NSMP, 0:NSMP]).then_inc(s["tr"], 1)
                for k in range(TOPK):
                    pe_expert(pe, NCH, 0, k)
                pe.wait_ge(s["gz"], 1)
                for b in range(NSMP):
                    pe.wait_ge(s_vs[b], 16)
                    for n in range(2):
                        last = T.matmul(PB[0:NSMP, 6 + n, :], wgs[:, b, :], vs[:, b, n * 512:(n + 1) * 512],
                                        start=b == 0, stop=b == NSMP - 1)
                last.then_inc(s["go"], 1)


def kernel(x_prompt, x_sample, state_ssd, state_ssd_conv, state_mlstm_c, state_mlstm_n, state_mlstm_m,
           state_mlstm_conv, w_in, conv_ssd_w, conv_ssd_b, dt_bias, a_log, d_skip, ssd_norm_g, conv_m_w, conv_m_b,
           w_mq, w_mk, b_igate, b_fgate, mlstm_norm_g, w_out, ln1_g, ln1_b, peer_wq, peer_keys, peer_u, peer_v,
           ln2_g, ln2_b):
    import concourse.bacc as bacc
    from concourse.bass_utils import run_bass_kernel_spmd

    x = np.concatenate([x_prompt[0], x_sample[:, 0]], axis=0)
    w = np.asarray(w_in[0])
    cols = np.cumsum((D, D + 2 * NG * NST, NH, D, D, D, MH, MH))
    z, xbc, dtw, um, vm, om, iw, fw = np.split(w, cols[:-1], axis=1)

    def k_major(m):
        return m.reshape(-1, P, m.shape[-1]).transpose(1, 0, 2)

    chan = np.concatenate([xbc, um], axis=1).reshape(KD, P, NCT, P).transpose(2, 1, 0, 3)
    tok = np.concatenate([z, vm, om], axis=1).reshape(KD, P, 6, 512).transpose(2, 1, 0, 3)
    row = np.zeros((D, P), w.dtype)
    row[:, 0:NH], row[:, 32:32 + MH], row[:, 64:64 + MH] = dtw, iw, fw
    gate_b = np.zeros((16, 4), w.dtype)
    gate_b[0:NH, 0], gate_b[0:MH, 1], gate_b[0:MH, 2], gate_b[0:NH, 3] = dt_bias[0], b_igate[0], b_fgate[0], a_log[0]
    conv_w = np.concatenate([np.concatenate([conv_ssd_w[0], conv_m_w[0]], axis=1),
                             np.concatenate([conv_ssd_b[0], conv_m_b[0]])[None]], axis=0)
    conv_s = np.concatenate([state_ssd_conv[0], state_mlstm_conv[0]], axis=2)
    wq = np.asarray(peer_wq[0]).reshape(D, NHC, P)
    arrays = {
        "x_tok": np.concatenate([x, np.zeros((NPAD - NTOK, D), x.dtype)], axis=0),
        "x_t": k_major(np.asarray(x).T),
        "w_ch": chan, "w_tok": tok, "w_row": k_major(row), "gate_b": gate_b,
        "conv_w": conv_w.T.reshape(NCT, P, TAPS + 1),
        "conv_s": conv_s.transpose(2, 1, 0).reshape(NCT, P, 3, NSMP),
        "m_state": np.asarray(state_mlstm_m[0]).T,
        "n_state": np.asarray(state_mlstm_n[0]).reshape(NSMP, MH * KT, P).transpose(2, 1, 0),
        "ssd_state": np.asarray(state_ssd[0]).reshape(NSMP, NH * HD, NST),
        "c_state": np.asarray(state_mlstm_c[0]).reshape(NSMP, MH * DK, DK),
        "d_skip": np.asarray(d_skip[0]),
        "d_skip_ch": np.repeat(np.asarray(d_skip[0]), HD).reshape(8, P).T,
        "ssd_g": np.asarray(ssd_norm_g[0]), "mlstm_g": np.asarray(mlstm_norm_g[0]).reshape(-1),
        "w_mq": np.asarray(w_mq[0]).reshape(MH, KT, P, DK).transpose(2, 0, 1, 3),
        "w_mk": np.asarray(w_mk[0]).reshape(MH, KT, P, DK).transpose(2, 0, 1, 3),
        "w_out": k_major(np.asarray(w_out[0])),
        "ln1_g": np.asarray(ln1_g[0]), "ln1_b": np.asarray(ln1_b[0]),
        "ln2_g": np.asarray(ln2_g[0]), "ln2_b": np.asarray(ln2_b[0]),
        "wq_t": wq.transpose(1, 2, 0),
        "keys_t": np.asarray(peer_keys[0]).reshape(NHC, NK, P).transpose(0, 2, 1),
        "peer_u": np.asarray(peer_u[0]), "peer_v": np.asarray(peer_v[0]),
    }
    outs = {"y": (NTOK, D), "conv_p": (NCT, P, 3), "conv_s": (NCT, P, 3, NSMP), "p_ssd": (P, D),
            "p_c": (P, MH * KT, DK), "p_n": (P, MH * KT), "p_m": (MH, 1), "s_ssd": (NSMP, NH * HD, NST),
            "s_c": (NSMP, MH * DK, DK), "s_n": (P, MH * KT, NSMP), "s_m": (MH, NSMP)}
    nc = bacc.Bacc("TRN2", target_bir_lowering=False, num_devices=1)
    given, a, o = {}, {}, {}
    for name, v in arrays.items():
        v = np.ascontiguousarray(v)
        given["in_" + name] = v
        a[name] = nc.dram_tensor("in_" + name, v.shape, mybir.dt.from_np(v.dtype), kind="ExternalInput").ap()
    for name, shape in outs.items():
        o[name] = nc.dram_tensor("out_" + name, shape, mybir.dt.float32, kind="ExternalOutput").ap()
    build(nc, a, o)
    got = run_bass_kernel_spmd(nc, [given], core_ids=[0]).results[0]
    r = {name: got["out_" + name] for name in outs}
    conv_p = r["conv_p"].reshape(NCT * P, 3).T
    conv_q = r["conv_s"].reshape(NCT * P, 3, NSMP).transpose(2, 1, 0)
    nx = D + 2 * NG * NST
    return (
        r["y"][None, 0:SEQ], r["y"][SEQ:NTOK, None],
        r["p_ssd"].T.reshape(1, 1, NH, HD, NST), conv_p[None, None, :, 0:nx],
        r["p_c"].transpose(1, 0, 2).reshape(1, 1, MH, DK, DK), r["p_n"].T.reshape(1, 1, MH, DK),
        r["p_m"].reshape(1, 1, MH), conv_p[None, None, :, nx:],
        r["s_ssd"].reshape(1, NSMP, NH, HD, NST), conv_q[None, :, :, 0:nx],
        r["s_c"].reshape(1, NSMP, MH, DK, DK), r["s_n"].transpose(2, 1, 0).reshape(1, NSMP, MH, DK),
        r["s_m"].T.reshape(1, NSMP, MH), conv_q[None, :, :, nx:],
    )
```

```python
import concourse.bass as bass
from concourse import mybir
from concourse.alu_op_type import AluOpType as ALU
from contextlib import ExitStack
import numpy as np

P = 128
D = 1024
KD = D // P
SEQ = 1024
CH = 128
NCH = SEQ // CH
NSMP = 8
NTOK = SEQ + NSMP
NPAD = SEQ + CH
NH, HD, NST, NG = 16, 64, 128, 2
MH, DK = 4, 256
KT = DK // P
NCT = 20
BT0, CT0, UT0 = 8, 10, 12
PH, NK, TOPK = 8, 128, 16
NE = NK * NK
NHC = 2 * PH
TAPS = 4
TW = 256
NTB = 3 * D // TW
TN = NTOK // 3
ALPHA = 2.0 ** 0.25
EPS = 1e-5
BIG = 1e30
NEG = -3e38
R_NACS, R_M, R_WLOG, R_DT, R_G, R_MT, NROW = 0, 16, 20, 24, 40, 44, 48
NB = 4


class Chain:

    def __init__(self, eng, sem, base=0, plain=None):
        self.eng, self.sem, self.base, self.plain, self.n = eng, sem, base, plain, 0

    def link(self, ins):
        ins.then_inc(self.sem, 1)
        self.n += 1
        self.eng.wait_ge(self.sem, self.base + self.n)

    def link_plain(self, ins):
        self.link(ins)
        self.eng.sem_inc(self.plain, 1)


def steps(eng, n, first=0):
    if first == 0:
        yield 0
    with eng.Fori(max(first, 1), n) as i:
        yield i


def inner(eng, outer, n):
    if isinstance(outer, int):
        yield from steps(eng, n)
    else:
        with eng.Fori(0, n) as i:
            yield i


def free(eng, sem, value):
    if not isinstance(value, int) or value > 0:
        eng.wait_ge(sem, value)


def build(nc, a, o):
    f32, f32r = mybir.dt.float32, mybir.dt.float32r
    ACT = mybir.ActivationFunctionType

    def dram(name, shape, dt=f32):
        return nc.dram_tensor(name, shape, dt).ap()

    cht_d = dram("cht_d", (NCT, P, NTOK))
    tok_d = dram("tok_d", (6, NTOK, 512))
    rows_d = dram("rows_d", (NROW, SEQ))
    rows_s_d = dram("rows_s_d", (NROW, NSMP))
    wp_d = dram("wp_d", (NHC, P, KD, NK))
    mixt_d = dram("mixt_d", (16, P, NPAD))
    x1_d = dram("x1_d", (NSMP, D))
    bc_d = dram("bc_d", (NSMP, 4, P))

    top = ExitStack()
    with top:
        phase_sems = []

        def sem(name):
            phase_sems.append(nc.alloc_semaphore(name=name))
            return phase_sems[-1]

        def end_phase():
            nc.clear_and_free_semaphores(phase_sems)
            nc.all_engine_barrier()
            phase_sems.clear()

        PB = top.enter_context(nc.psum_tensor("PB", [P, 8, 512], f32))
        ident = top.enter_context(nc.sbuf_tensor("ident", [P, P], f32))

        def two(b):
            return PB[:, b:b + 2, :].rearrange("p a n -> p (a n)")

        with ExitStack() as ctx:
            def sb(name, shape, dt=f32):
                return ctx.enter_context(nc.sbuf_tensor(name, shape, dt))

            xh, xl = (sb(n, [P, KD, NTOK], f32r) for n in ("xh", "xl"))
            wch = [[sb(f"wch{part}{i}", [P, KD, P], f32r) for part in "hl"] for i in range(2)]
            wtk = [[sb(f"wtk{part}{i}", [P, KD, TW], f32r) for part in "hl"] for i in range(2)]
            wcr = [sb(f"wcr{i}", [P, KD, P]) for i in range(2)]
            wtr = [sb(f"wtr{i}", [P, KD, TW]) for i in range(2)]
            cw = [sb(f"cw{i}", [P, TAPS + 1]) for i in range(2)]
            xp = [sb(f"xp{i}", [P, TAPS - 1 + SEQ]) for i in range(2)]
            xps = [sb(f"xps{i}", [P, TAPS, NSMP]) for i in range(2)]
            cv = [sb(f"cv{i}", [P, NTOK]) for i in range(2)]
            stg = [sb(f"stg{i}", [P, TW]) for i in range(6)]
            gb = sb("gb", [16, 4])
            dtr = sb("dtr", [NH, NTOK])
            ir = sb("ir", [MH, NTOK])
            fr = sb("fr", [MH, NTOK])
            t1 = sb("t1", [NH, NTOK])
            t2 = sb("t2", [NH, NTOK])
            t3 = sb("t3", [MH, NTOK])
            mrun = sb("mrun", [MH, NTOK])
            nacs, bcs, wlog, mt = t1, t3, fr, t2[0:MH, :]
            ones = sb("ones", [16, CH])
            zros = sb("zros", [16, CH])
            mcar = sb("mcar", [MH, NCH + 1])
            m0s = sb("m0s", [MH, NSMP])
            ea = sb("ea", [NH, 1])
            wqt = [sb(f"wqt{i}", [P, D]) for i in range(2)]
            kyt = [sb(f"kyt{i}", [P, NK]) for i in range(2)]
            xst = [w[:, :, :].rearrange("p k n -> p (k n)")[:, 0:NTOK] for w in wtr] + [c[:, :] for c in cv]
            wrp = [w[:, :, 0:P] for w in wtk[0]]
            wrow = wqt[0][:, :].rearrange("p (k n) -> p k n", k=KD)
            wps = [c[:, 0:KD * NK] for c in cv]

            s_x = [sem(f"x_loaded{i}") for i in range(4)]
            s_xh, s_xl = sem("x_high_part"), sem("x_split")
            s_wr, s_gb = sem("wrow_loaded"), sem("gate_bias_loaded")
            s_go = sem("split_go")
            s_rh, s_rp = sem("wrow_high_part"), sem("wrow_split")
            s_ch, s_cp = ([sem(f"chan_weights_{what}{i}") for i in range(2)] for what in ("high_part", "split"))
            s_th, s_tp = ([sem(f"tok_weights_{what}{i}") for i in range(2)] for what in ("high_part", "split"))
            s_w = [sem(f"chan_weights_loaded{i}") for i in range(2)]
            s_cw = [sem(f"conv_taps_loaded{i}") for i in range(2)]
            s_mm = [sem(f"chan_product{i}") for i in range(2)]
            s_ev = [sem(f"chan_evacuated{i}") for i in range(2)]
            s_cv = [sem(f"convolved{i}") for i in range(2)]
            s_si = [sem(f"silu_done{i}") for i in range(2)]
            s_st = [sem(f"chan_stored{i}") for i in range(2)]
            s_cs = [sem(f"conv_state_stored{i}") for i in range(2)]
            s_rw, s_re, s_z0 = sem("row_product"), sem("row_evacuated"), sem("zeroed")
            s_tw = [sem(f"tok_weights_loaded{i}") for i in range(2)]
            s_tm = [sem(f"tok_product{i}") for i in range(6)]
            s_te = [sem(f"tok_evacuated{i}") for i in range(6)]
            s_ts = [sem(f"tok_stored{i}") for i in range(6)]
            s_pw = [sem(f"wq_loaded{i}") for i in range(2)]
            s_pm = [sem(f"wp_product{i}") for i in range(2)]
            s_pe = [sem(f"wp_evacuated{i}") for i in range(2)]
            s_ps = [sem(f"wp_stored{i}") for i in range(2)]
            s_cc, s_l1, s_rs, s_abs = sem("conv_chain"), sem("gate_log"), sem("rows_stored"), sem("gate_abs")
            s_rr = sem("rows_ready")
            c_d, c_a = sem("dve_chain_a"), sem("act_chain_a")
            s_id0, s_id = sem("ident_zeroed"), sem("ident_ready")

            with nc.Block() as block:
                @block.sync
                def _(sp):
                    sp.dma_start(wrow, a["w_row"]).then_inc(s_wr, 16)
                    for q in range(2):
                        sp.dma_start(wcr[q][:, :, :], a["w_ch"][q, :, :, :]).then_inc(s_w[q], 16)
                    for k in range(KD):
                        free(sp, s_xl, k - 3)
                        sp.dma_start(xst[k % 4], a["x_t"][:, k, :]).then_inc(s_x[k % 4], 16)
                    sp.dma_start(gb[:, :], a["gate_b"]).then_inc(s_gb, 16)
                    sp.dma_start(m0s[:, :], a["m_state"]).then_inc(s_gb, 16)
                    for i in steps(sp, NCT // 2):
                        for q in range(2):
                            j = 2 * i + q
                            if not isinstance(i, int):
                                sp.wait_ge(s_cp[q], i)
                                sp.dma_start(wcr[q][:, :, :], a["w_ch"][j, :, :, :]).then_inc(s_w[q], 16)
                            free(sp, s_cv[q], i)
                            sp.dma_start(cw[q][:, :], a["conv_w"][j, :, :]).then_inc(s_cw[q], 16)
                            free(sp, s_cs[q], 32 * i)
                            sp.dma_start(xps[q][:, 0:3, :], a["conv_s"][j, :, :, :]).then_inc(s_cw[q], 16)
                    sp.wait_ge(s_xl, KD)
                    def w_load(i, q):
                        if isinstance(i, int) and (i, q) == (0, 0):
                            sp.wait_ge(s_rp, 1)
                        free(sp, s_pm[q], i)
                        sp.dma_start(wqt[q][:, :], a["wq_t"][2 * i + q, :, :]).then_inc(s_pw[q], 16)
                        sp.dma_start(kyt[q][:, :], a["keys_t"][2 * i + q, :, :]).then_inc(s_pw[q], 16)

                    for i in steps(sp, NTB // 2):
                        for q in range(2):
                            free(sp, s_tp[q], i)
                            sp.dma_start(wtr[q][:, :, :], a["w_tok"][2 * i + q, :, :, :]).then_inc(s_tw[q], 16)
                            w_load(i, q)
                    for i in steps(sp, NHC // 2, NTB // 2):
                        for q in range(2):
                            w_load(i, q)

                @block.tensor
                def _(pe):
                    def terms(xs, ws):
                        return (xs[0], ws[0]), (xs[0], ws[1]), (xs[1], ws[0])

                    pe.wait_ge(s_rp, 1)
                    for k in range(KD):
                        pe.wait_ge(s_xl, k + 1)
                        for part in range(3):
                            for u, (x, w) in enumerate(terms((xh, xl), wrp)):
                                last = nc.tensor.matmul(PB[:, 5 + part, 0:TN], w[:, k, :], x[:, k, part * TN:(part + 1) * TN],
                                                        start=k == 0 and u == 0, stop=k == KD - 1 and u == 2)
                    last.then_inc(s_rw, 1)
                    for i in steps(pe, NCT // 2):
                        for q in range(2):
                            if isinstance(i, int) and q == 1:
                                pe.wait_ge(s_re, 1)
                            pe.wait_ge(s_cp[q], i + 1)
                            free(pe, s_ev[q], i)
                            for part in range(3):
                                for k in range(KD):
                                    for u, (x, w) in enumerate(terms((xh, xl), wch[q])):
                                        last = nc.tensor.matmul(PB[:, 3 * q + part, 0:TN], w[:, k, :], x[:, k, part * TN:(part + 1) * TN],
                                                                start=k == 0 and u == 0, stop=k == KD - 1 and u == 2)
                            last.then_inc(s_mm[q], 1)
                    for q in range(2):
                        pe.wait_ge(s_ev[q], NCT // 2)

                    def w_product(i, q):
                        pe.wait_ge(s_pw[q], 32 * (i + 1))
                        free(pe, s_pe[1 - q], i + q)
                        for k in range(KD):
                            last = nc.tensor.matmul(two(6)[:, k * NK:(k + 1) * NK], wqt[q][:, k * P:(k + 1) * P],
                                                    kyt[q][:, :], start=True, stop=True)
                        last.then_inc(s_pm[q], 1)

                    for i in steps(pe, NTB // 2):
                        for u in range(18):
                            q, t, b = u // 9, u % 9, u % 6
                            n = CH if t < NCH else NSMP
                            if t == 0:
                                pe.wait_ge(s_tp[q], i + 1)
                            free(pe, s_te[b], 3 * i + u // 6)
                            for k in range(KD):
                                for v, (x, w) in enumerate(terms((xh, xl), wtk[q])):
                                    last = nc.tensor.matmul(PB[0:n, b, 0:TW], x[:, k, t * CH:t * CH + n], w[:, k, :],
                                                            start=k == 0 and v == 0, stop=k == KD - 1 and v == 2)
                            last.then_inc(s_tm[b], 1)
                            if t == NCH:
                                w_product(i, q)
                    for i in steps(pe, NHC // 2, NTB // 2):
                        for q in range(2):
                            w_product(i, q)

                @block.scalar
                def _(act):
                    for k in range(KD):
                        act.wait_ge(s_x[k % 4], 16 * (k // 4 + 1))
                        nc.scalar.copy(xh[:, k, :], xst[k % 4]).then_inc(s_xh, 1)
                    act.wait_ge(s_rw, 1)
                    for dst, lo in ((dtr, 0), (ir, 32), (fr, 64)):
                        last = nc.scalar.copy(dst[:, :].rearrange("p (a n) -> p a n", a=3), PB[lo:lo + dst.shape[0], 5:8, 0:TN])
                    last.then_inc(s_re, 1)
                    act.wait_ge(s_abs, 1)
                    ch = Chain(act, c_a)
                    nc.scalar.activation(t1[:, :], t1[:, :], ACT.Exp, scale=-1.0)
                    nc.scalar.activation(ea[:, :], gb[0:NH, 3:4], ACT.Exp)
                    ch.link(nc.scalar.activation(t3[:, :], t3[:, :], ACT.Exp, scale=-1.0))
                    nc.scalar.activation(t1[:, :], t1[:, :], ACT.Ln, bias=1.0)
                    nc.scalar.activation(t3[:, :], t3[:, :], ACT.Ln, bias=1.0).then_inc(s_l1, 1)
                    act.wait_ge(s_z0, 1)
                    for i in steps(act, NCT // 2):
                        for q in range(2):
                            act.wait_ge(s_mm[q], i + 1)
                            act.wait_ge(s_cv[q], i)
                            act.wait_ge(s_cs[q], 32 * i)
                            nc.scalar.copy(xp[q][:, 3:3 + 2 * TN].rearrange("p (a n) -> p a n", a=2), PB[:, 3 * q:3 * q + 2, 0:TN])
                            nc.scalar.copy(xp[q][:, 3 + 2 * TN:3 + SEQ], PB[:, 3 * q + 2, 0:SEQ - 2 * TN])
                            nc.scalar.copy(xps[q][:, 3, :], PB[:, 3 * q + 2, SEQ - 2 * TN:TN]).then_inc(s_ev[q], 1)
                            act.wait_ge(s_ev[q], i + 1)
                            act.wait_ge(s_cw[q], 32 * (i + 1))
                            act.dma_start(o["conv_p"][2 * i + q, :, :], xp[q][:, SEQ:SEQ + 3]).then_inc(s_cs[q], 16)
                            act.dma_start(o["conv_s"][2 * i + q, :, :, :], xps[q][:, 1:4, :]).then_inc(s_cs[q], 16)
                            act.wait_ge(s_cv[q], i + 1)
                            nc.scalar.activation(cv[q][:, :], cv[q][:, :], ACT.Silu).then_inc(s_si[q], 1)
                            act.wait_ge(s_si[q], i + 1)
                            act.dma_start(cht_d[2 * i + q, :, :], cv[q][:, :]).then_inc(s_st[q], 16)
                    act.wait_ge(s_rr, 1)
                    for src, r, n in ((nacs, R_NACS, NH), (mrun, R_M, MH), (wlog, R_WLOG, MH),
                                      (dtr, R_DT, NH), (ir, R_G, MH), (mt, R_MT, MH)):
                        act.dma_start(rows_d[r:r + n, :], src[0:n, 0:SEQ]).then_inc(s_rs, 16)
                        act.dma_start(rows_s_d[r:r + n, :], src[0:n, SEQ:NTOK]).then_inc(s_rs, 16)
                    act.dma_start(o["p_m"], mcar[:, NCH:NCH + 1]).then_inc(s_rs, 16)
                    act.dma_start(o["s_m"], mt[:, SEQ:NTOK]).then_inc(s_rs, 16)
                    def w_store(i, q):
                        act.wait_ge(s_pm[q], i + 1)
                        if isinstance(i, int) and i == 0:
                            act.wait_ge(s_st[q], 16 * NCT // 2)
                        free(act, s_ps[q], 16 * i)
                        nc.scalar.copy(wps[q], two(6)).then_inc(s_pe[q], 1)
                        act.wait_ge(s_pe[q], i + 1)
                        act.dma_start(wp_d[bass.ds(2 * i + q, 1), :, :, :].rearrange("a p k n -> p (a k) n"),
                                      wps[q].rearrange("p (k n) -> p k n", k=KD)).then_inc(s_ps[q], 16)

                    for third, func in enumerate((ACT.Silu, ACT.Copy, ACT.Sigmoid)):
                        for i in steps(act, (third + 1) * NTB // 6, third * NTB // 6):
                            for u in range(18):
                                q, t, b = u // 9, u % 9, u % 6
                                n = CH if t < NCH else NSMP
                                act.wait_ge(s_tm[b], 3 * i + u // 6 + 1)
                                free(act, s_ts[b], 16 * (3 * i + u // 6))
                                nc.scalar.activation(stg[b][0:n, :], PB[0:n, b, 0:TW], func).then_inc(s_te[b], 1)
                                act.wait_ge(s_te[b], 3 * i + u // 6 + 1)
                                act.dma_start(tok_d[bass.ds(i, 1), t * CH:t * CH + n, q * TW:(q + 1) * TW].rearrange("a t n -> t (a n)"),
                                              stg[b][0:n, :]).then_inc(s_ts[b], 16)
                                if t == NCH:
                                    w_store(i, q)
                    for i in steps(act, NHC // 2, NTB // 2):
                        for q in range(2):
                            w_store(i, q)
                    act.wait_ge(s_rs, 16 * 14)
                    for q in range(2):
                        act.wait_ge(s_st[q], 16 * NCT // 2)
                        act.wait_ge(s_cs[q], 32 * NCT // 2)
                        act.wait_ge(s_ps[q], 16 * NHC // 2)
                    for b in range(6):
                        act.wait_ge(s_ts[b], 16 * 3 * NTB // 2)

                @block.gpsimd
                def _(pool):
                    nc.gpsimd.memset(ident[:, :], 0.0).then_inc(s_id0, 1)
                    pool.wait_ge(s_id0, 1)
                    nc.gpsimd.affine_select(out=ident[:, :], in_=ident[:, :], compare_op=ALU.not_equal, fill=1.0,
                                            base=0, pattern=[[-1, P]], channel_multiplier=1).then_inc(s_id, 1)
                    pool.wait_ge(s_id, 1)

                    def split(parts, src, half, done, n):
                        pool.sem_inc(s_go, 1)
                        nc.gpsimd.tensor_copy(parts[0][:, :, :], src).then_inc(half, 1)
                        pool.wait_ge(half, n)
                        nc.gpsimd.tensor_tensor(parts[1][:, :, :], src, parts[0][:, :, :].bitcast(f32), ALU.subtract).then_inc(done, 1)

                    pool.wait_ge(s_wr, 16)
                    split(wrp, wrow, s_rh, s_rp, 1)
                    for i in steps(pool, NCT // 2):
                        for q in range(2):
                            pool.wait_ge(s_w[q], 16 * (i + 1))
                            free(pool, s_mm[q], i)
                            split(wch[q], wcr[q][:, :, :], s_ch[q], s_cp[q], i + 1)
                    for i in steps(pool, NTB // 2):
                        for q in range(2):
                            pool.wait_ge(s_tw[q], 16 * (i + 1))
                            free(pool, s_tm[(2, 5)[q]], 3 * i - 1 + q)
                            split(wtk[q], wtr[q][:, :, :], s_th[q], s_tp[q], i + 1)

                @block.vector
                def _(dve):
                    ch = Chain(dve, c_d)
                    for q in range(2):
                        nc.vector.memset(xp[q][:, 0:3], 0.0)
                    nc.vector.memset(mcar[:, 0:1], 0.0)
                    nc.vector.memset(ones[:, :], 1.0)
                    nc.vector.memset(zros[:, :], 0.0).then_inc(s_z0, 1)
                    dve.wait_ge(s_z0, 1)
                    for k in range(KD):
                        dve.wait_ge(s_xh, k + 1)
                        nc.vector.tensor_tensor(xl[:, k, :], xst[k % 4], xh[:, k, :].bitcast(f32), ALU.subtract).then_inc(s_xl, 1)
                    dve.wait_ge(s_re, 1)
                    dve.wait_ge(s_gb, 32)
                    nc.vector.tensor_scalar(dtr[:, :], dtr[:, :], gb[0:NH, 0:1], None, ALU.add)
                    nc.vector.tensor_scalar(ir[:, :], ir[:, :], gb[0:MH, 1:2], None, ALU.add)
                    ch.link(nc.vector.tensor_scalar(fr[:, :], fr[:, :], gb[0:MH, 2:3], None, ALU.add))
                    nc.vector.scalar_tensor_tensor(t1[:, :], dtr[:, :], -1.0, dtr[:, :], ALU.mult, ALU.max)
                    nc.vector.scalar_tensor_tensor(t3[:, :], fr[:, :], -1.0, fr[:, :], ALU.mult, ALU.max).then_inc(s_abs, 1)
                    dve.wait_ge(s_l1, 1)
                    nc.vector.scalar_tensor_tensor(dtr[:, :], dtr[:, :], 0.0, t1[:, :], ALU.max, ALU.add)
                    ch.link(nc.vector.scalar_tensor_tensor(fr[:, :], fr[:, :], 0.0, t3[:, :], ALU.min, ALU.subtract))
                    ch.link(nc.vector.tensor_scalar(t2[:, :], dtr[:, :], ea[:, :], None, ALU.mult))
                    for c in range(NCH):
                        s = slice(c * CH, (c + 1) * CH)
                        nc.vector.tensor_tensor_scan(nacs[:, s], ones[0:NH, :], t2[:, s], 0.0, ALU.mult, ALU.add)
                        nc.vector.tensor_tensor_scan(bcs[:, s], ones[0:MH, :], fr[:, s], 0.0, ALU.mult, ALU.add)
                    nc.vector.tensor_copy(nacs[:, SEQ:NTOK], t2[:, SEQ:NTOK])
                    ch.link(nc.vector.tensor_copy(bcs[:, SEQ:NTOK], fr[:, SEQ:NTOK]))
                    ch.link(nc.vector.tensor_tensor(ir[:, :], ir[:, :], bcs[:, :], ALU.subtract))
                    for c in range(NCH):
                        s, e = slice(c * CH, (c + 1) * CH), (c + 1) * CH - 1
                        ch.link(nc.vector.tensor_tensor_scan(mrun[:, s], zros[0:MH, :], ir[:, s], mcar[:, c:c + 1],
                                                             ALU.add, ALU.max))
                        nc.vector.tensor_scalar(wlog[:, s], mrun[:, s], -1.0, mcar[:, c:c + 1], ALU.mult, ALU.add)
                        ch.link(nc.vector.tensor_tensor(mcar[:, c + 1:c + 2], mrun[:, e:e + 1], bcs[:, e:e + 1], ALU.add))
                    s = slice(SEQ, NTOK)
                    ch.link(nc.vector.tensor_tensor(mrun[:, s], m0s[:, :], ir[:, s], ALU.max))
                    nc.vector.tensor_tensor(wlog[:, s], m0s[:, :], mrun[:, s], ALU.subtract)
                    nc.vector.tensor_tensor(mt[:, :], mrun[:, :], bcs[:, :], ALU.add).then_inc(s_rr, 1)
                    for i in steps(dve, NCT // 2):
                        cc = Chain(dve, s_cc, 6 * i)
                        for q in range(2):
                            dve.wait_ge(s_ev[q], i + 1)
                            dve.wait_ge(s_cw[q], 32 * (i + 1))
                            free(dve, s_st[q], 16 * i)
                            for tap in range(TAPS):
                                w = cw[q][:, tap:tap + 1]
                                for out, src in ((cv[q][:, 0:SEQ], xp[q][:, tap:tap + SEQ]),
                                                 (cv[q][:, SEQ:NTOK], xps[q][:, tap, :])):
                                    if tap == 0:
                                        last = nc.vector.tensor_scalar(out, src, w, cw[q][:, 4:5], ALU.mult, ALU.add)
                                    else:
                                        last = nc.vector.scalar_tensor_tensor(out, src, w, out, ALU.mult, ALU.add)
                                if tap < TAPS - 1:
                                    cc.link(last)
                            last.then_inc(s_cv[q], 1)

        end_phase()

        with ExitStack() as ctx:
            build_scan(nc, a, o, ctx, sem, PB, ident, two, cht_d, tok_d, rows_d, rows_s_d, bc_d, mixt_d)
        end_phase()
        build_peer(nc, a, o, sem, PB, ident, two, mixt_d, wp_d, x1_d)


def pairs(eng):
    for i in steps(eng, NCH // 2):
        for q in range(2):
            yield 2 * i + q, q


def build_scan(nc, a, o, ctx, sem, PB, ident, two, cht_d, tok_d, rows_d, rows_s_d, bc_d, mixt_d):
    f32 = mybir.dt.float32
    ACT = mybir.ActivationFunctionType
    AX = mybir.AxisListType.X
    V, S, G, T = nc.vector, nc.scalar, nc.gpsimd, nc.tensor
    B = NSMP

    def sb(name, shape, dt=f32):
        return ctx.enter_context(nc.sbuf_tensor(name, shape, dt))

    def sb2(name, shape):
        return [sb(f"{name}{q}", shape) for q in range(2)]

    def heads(ap, n):
        return ap.rearrange("p (h n) -> p h n", n=n)

    def wide(ap, n):
        return ap.unsqueeze(2).to_broadcast([ap.shape[0], ap.shape[1], n])

    wmq, wmk = sb("wmq", [P, MH, KT, DK]), sb("wmk", [P, MH, KT, DK])
    gs, gm, dsk = sb("gs", [P, D]), sb("gm", [P, D]), sb("dsk", [P, NH])
    maskp, onec = sb("maskp", [P, CH]), sb("onec", [P, 1])
    cht = sb("cht", [P, NCT, CH])
    zvo = sb("zvo", [P, 6, 512])
    rows = sb("rows", [NROW, CH])
    rb = sb("rb", [P, R_DT, CH])
    L = sb("L", [P, NH + MH, CH])
    cols = sb2("cols", [P, NROW])
    e_ea, e_wi, e_em = sb2("e_ea", [P, NH]), sb2("e_wi", [P, MH]), sb2("e_em", [P, MH])
    e_hd, e_wo = sb2("e_hd", [P, NH]), sb2("e_wo", [P, MH])
    e_de, e_ws = sb2("e_de", [P, NH]), sb2("e_ws", [P, MH])
    btok = sb("btok", [P, NG * NST])
    xtok, xdt, xdec, dx = (sb(n, [P, D]) for n in ("xtok", "xdt", "xdec", "dx"))
    qT, kT = sb("qT", [P, MH * KT, CH]), sb("kT", [P, MH * KT, CH])
    kw = sb("kw", [P, D])
    hT, cst, nst = sb("hT", [P, D]), sb("cst", [P, MH * KT, DK]), sb("nst", [P, MH * KT])
    ysb, yst, sq, nx, num, og = (sb(n, [P, D]) for n in ("ysb", "yst", "sq", "nx", "num", "og"))
    den = sb("den", [P, 8])
    stt, mv, rs = sb("stt", [P, MH, 6]), sb("mv", [P, MH, 2]), sb("rs", [P, 5])
    mix, mixT = sb("mix", [P, 2 * D]), sb("mixT", [P, 16, CH])
    chs = sb("chs", [P, NCT, B])
    rsb = sb("rsb", [P, NROW, B])
    dts, dsc = sb("dts", [P, 8, B]), sb("dsc", [P, 8])
    scl = sb("scl", [P, 36, B])
    nas, wos, ks, dxt, qs = (scl[:, lo:hi, :] for lo, hi in ((0, 8), (8, 12), (12, 20), (20, 28), (28, 36)))
    cur = sb2("cur", [P, 36])
    wss = sb("wss", [P, MH, B])
    bcsb = sb("bcsb", [B, 4 * P])
    bb = sb2("bb", [P, 4 * P])
    st, cs, vb = sb2("st", [P, 8, NST]), sb2("cs", [P, MH * KT, DK]), sb2("vb", [P, D])
    t3, t4 = sb("t3s", [P, 8, NST]), sb("t4s", [P, MH * KT, DK])
    ns, pr, red = sb("ns", [P, 8, B]), sb("pr", [P, 8, B]), sb("red", [P, 8])
    ysc, ych, numc = sb("ysc", [P, 8, B]), sb("ych", [P, 8, B]), sb("numc", [P, 8, B])
    e_ems, den_s = sb("e_ems", [B, MH]), sb("den_s", [B, 8])
    z_s, o_s, y_s, num_s = dx[0:B, :], xdt[0:B, :], xtok[0:B, :], yst[0:B, :]

    s = {n: sem("scan_" + n) for n in (
        "w wqk setup mask rows ch rb v zo pe_a pe_b pe_kk pe_st pe_tr pe_y pe_ys pe_hn pe_ni pe_nx pe_c1 pe_c2 "
        "act_xt act_small act_l act_qk act_l2 act_mt act_nx pool_l pool_arg pool_xdec pool_dx pool_hs pool_og "
        "dve_xdt dve_kw dve_mm dve_att dve_y dve_ys dve_h dve_num dve_var act_ln act_rs dve_den dve_c1 dve_c2 dve_mix "
        "outs stored passed pad").split()}
    ss = {n: sem("smp_" + n) for n in (
        "ld zo bct bcc bcd qk qkc exp arg pre nst cur decay cscale outer st_new red c_new num numc den yt end").split()}
    s_in = [sem(f"smp_states_loaded{q}") for q in range(2)]
    s_out = [sem(f"smp_states_stored{q}") for q in range(2)]
    c_d, c_p = sem("dve_chain_scan"), sem("dve_chain_smp")
    DVE_LINKS = 12

    def gate_y(ch, r, z, y):
        ch.link(V.tensor_tensor(y, y, z, ALU.mult))
        V.tensor_tensor_reduce(out=sq[0:r, :], in0=y, in1=y, scale=1.0 / D, scalar=EPS,
                               op0=ALU.mult, op1=ALU.add, accum_out=rs[0:r, 0:1])

    def head_out(dve, ch, r, em, n, y, num, den, og):
        for h in range(MH):
            V.bn_stats(stt[0:r, h, :], num[:, h * DK:(h + 1) * DK])
        ch.link_plain(V.scalar_tensor_tensor(den[:, 4:8], den[:, 0:4], -1.0, den[:, 0:4], ALU.mult, ALU.max))
        for h in range(MH):
            V.bn_aggr(mv[0:r, h, :], stt[0:r, h, :])
        ch.link(V.tensor_tensor(den[:, 4:8], den[:, 4:8], em, ALU.max))
        ch.link(V.reciprocal(den[:, 4:8], den[:, 4:8]))
        ch.link(V.tensor_tensor(den[:, 0:4], den[:, 4:8], den[:, 4:8], ALU.mult))
        ch.link(V.tensor_tensor(rs[0:r, 1:5], mv[0:r, :, 1], den[:, 0:4], ALU.mult))
        V.tensor_scalar(rs[0:r, 1:5], rs[0:r, 1:5], EPS, None, ALU.add).then_inc(s["dve_var"], 1)
        dve.wait_ge(s["act_rs"], n + 1)
        ch.link(V.tensor_tensor(rs[0:r, 1:5], rs[0:r, 1:5], den[:, 4:8], ALU.mult))
        free(dve, s["pe_tr"], n)
        for h in range(MH):
            last = V.tensor_scalar(num[:, h * DK:(h + 1) * DK], num[:, h * DK:(h + 1) * DK],
                                   mv[0:r, h, 0:1], rs[0:r, 1 + h:2 + h], ALU.subtract, ALU.mult)
        ch.link(last)
        V.scalar_tensor_tensor(mix[0:r, 0:D], y, rs[0:r, 0:1], gs[0:r, :], ALU.mult, ALU.mult)
        dve.wait_ge(s["pool_og"], n + 1)
        V.tensor_tensor(mix[0:r, D:2 * D], num, og, ALU.mult).then_inc(s["dve_mix"], 1)

    def root(act, r, n):
        act.wait_ge(s["dve_var"], n + 1)
        S.activation(rs[0:r, :], rs[0:r, :], ACT.Ln).then_inc(s["act_ln"], 1)
        act.wait_ge(s["act_ln"], n + 1)
        S.activation(rs[0:r, :], rs[0:r, :], ACT.Exp, scale=-0.5).then_inc(s["act_rs"], 1)

    def mix_transposes(pe, r, n):
        pe.wait_ge(s["dve_mix"], n + 1)
        for j in range(16):
            last = T.transpose(PB[:, 4 + j // 4, (j % 4) * CH:(j % 4) * CH + r], mix[0:r, j * P:(j + 1) * P], ident[0:r, 0:r])
        last.then_inc(s["pe_tr"], 1)

    def mix_store(act, r, n, lo):
        act.wait_ge(s["pe_tr"], n + 1)
        free(act, s["stored"], 16 * n)
        if r < CH:
            act.wait_ge(s["pad"], 1)
        for j in range(4):
            last = S.copy(mixT[:, 4 * j:4 * j + 4, 0:r], PB[:, 4 + j, :].rearrange("p (a n) -> p a n", n=CH)[:, :, 0:r])
        last.then_inc(s["act_mt"], 1)
        act.wait_ge(s["act_mt"], n + 1)
        act.dma_start(mixt_d[:, :, bass.ds(lo, CH)].rearrange("j p t -> p j t"), mixT[:, :, :]).then_inc(s["stored"], 16)

    def by_head(ap):
        return ap.rearrange("p (h k) b -> p h k b", k=KT)

    def groups(ap):
        return ap.rearrange("p (g r) n -> p g r n", g=NG)

    with nc.Block() as block:
        @block.sync
        def _(sp):
            for i, q in pairs(sp):
                free(sp, s["pe_a"], i)
                sp.dma_start(rows[:, :], rows_d[:, bass.ds(i * CH, CH)]).then_inc(s["rows"], 16)
                free(sp, s["pool_arg"], i)
                free(sp, s["pool_l"], i)
                free(sp, s["act_small"], i)
                sp.dma_start(rb[:, :, :], rows_d[0:R_DT, bass.ds(i * CH, CH)].partition_broadcast(P)).then_inc(s["rb"], 16)
                free(sp, s["pe_ys"], i)
                sp.dma_start(cht[:, :, :], cht_d[:, :, bass.ds(i * CH, CH)].rearrange("j p t -> p j t")).then_inc(s["ch"], 16)
                if isinstance(i, int) and i == 0:
                    sp.dma_start(wmq[:, :, :, :], a["w_mq"]).then_inc(s["wqk"], 16)
                    sp.dma_start(wmk[:, :, :, :], a["w_mk"]).then_inc(s["wqk"], 16)
                    sp.dma_start(gs[:, :], a["ssd_g"].partition_broadcast(P)).then_inc(s["w"], 16)
                    sp.dma_start(gm[:, :], a["mlstm_g"].partition_broadcast(P)).then_inc(s["w"], 16)
                    sp.dma_start(dsk[:, :], a["d_skip"].partition_broadcast(P)).then_inc(s["w"], 16)
                free(sp, s["pe_c2"], i)
                sp.dma_start(zvo[:, 2:4, :], tok_d[2:4, bass.ds(i * CH, CH), :].rearrange("j t n -> t j n")).then_inc(s["v"], 16)
                free(sp, s["dve_mix"], i)
                sp.sem_inc(s["passed"], 1)
                for j in (0, 4):
                    sp.dma_start(zvo[:, j:j + 2, :], tok_d[j:j + 2, bass.ds(i * CH, CH), :].rearrange("j t n -> t j n")).then_inc(s["zo"], 16)
                if isinstance(i, int) and i == 0:
                    sp.wait_ge(ss["bcd"], 16)
                free(sp, s_out[q], 16 * (i - q))
                sp.dma_start(st[q][:, :, :], a["ssd_state"][bass.ds(i, 1)].rearrange("b (j p) n -> p (b j) n", p=P)).then_inc(s_in[q], 16)
                sp.dma_start(bb[q][:, :], bc_d[bass.ds(i, 1)].rearrange("b a n -> (b a n)").partition_broadcast(P)).then_inc(s_in[q], 16)
                sp.dma_start(cs[q][:, :, :], a["c_state"][bass.ds(i, 1)].rearrange("b (j p) v -> p (b j) v", p=P)).then_inc(s_in[q], 16)
                sp.dma_start(vb[q][:, :].rearrange("p (j n) -> p j n", j=2),
                             tok_d[2:4, bass.ds(i + SEQ, 1), :].rearrange("j b n -> (j b) n").partition_broadcast(P)).then_inc(s_in[q], 16)
            sp.wait_ge(s["dve_y"], NCH)
            sp.wait_ge(s["pe_y"], NCH)
            sp.wait_ge(s["pool_xdec"], NCH)
            for dst, j in ((z_s, 0), (o_s, 4)):
                sp.dma_start(dst.rearrange("p (j n) -> p j n", j=2),
                             tok_d[j:j + 2, SEQ:NTOK, :].rearrange("j t n -> t j n")).then_inc(ss["zo"], 16)

        @block.tensor
        def _(pe):
            def sample_start():
                pe.wait_ge(ss["ld"], 16 * 9)
                for g in range(4):
                    last = T.transpose(PB[0:B, 6, g * P:(g + 1) * P], chs[:, BT0 + g, :], ident[:, :])
                last.then_inc(ss["bct"], 1)
                for w, bank in ((wmq, 4), (wmk, 5)):
                    for h in range(MH):
                        for e in range(KT):
                            for k in range(KT):
                                last = T.matmul(PB[:, bank, (h * KT + e) * B:(h * KT + e + 1) * B], w[:, h, k, e * P:(e + 1) * P],
                                                chs[:, UT0 + h * KT + k, :], start=k == 0, stop=k == KT - 1)
                last.then_inc(ss["qk"], 1)
                pe.wait_ge(ss["qkc"], 1)

            pe.wait_ge(s["setup"], 1)
            v = zvo[:, 2:4, :].rearrange("p a n -> p (a n)")
            for i, q in pairs(pe):
                free(pe, s["act_nx"], i)
                free(pe, s["dve_den"], i)
                free(pe, s["dve_c1"], i)
                pe.wait_ge(s["rows"], 16 * (i + 1))
                pe.sem_inc(s["passed"], 1)
                T.transpose(PB[:, 2, 256:256 + NROW], rows[:, :], ident[0:NROW, 0:NROW])
                pe.wait_ge(s["ch"], 16 * (i + 1))
                for g in range(NG):
                    T.transpose(PB[:, 2, g * NST:(g + 1) * NST], cht[:, BT0 + g, :], ident[:, :])
                for g in range(NG):
                    T.matmul(PB[:, 3, g * CH:(g + 1) * CH], cht[:, BT0 + g, :], cht[:, CT0 + g, :], start=True, stop=True)
                free(pe, ss["numc"], i)
                for j in range(8):
                    last = T.transpose(two(0)[:, j * P:(j + 1) * P], cht[:, j, :], ident[:, :])
                last.then_inc(s["pe_a"], 1)
                free(pe, s["dve_c2"], i)
                if isinstance(i, int) and i == 0:
                    pe.wait_ge(s["wqk"], 32)
                for w, b in ((wmq, 4), (wmk, 6)):
                    for h in range(MH):
                        for e in range(KT):
                            for k in range(KT):
                                last = T.matmul(two(b)[:, (h * KT + e) * CH:(h * KT + e + 1) * CH],
                                                w[:, h, k, e * P:(e + 1) * P], cht[:, UT0 + h * KT + k, :],
                                                start=k == 0, stop=k == KT - 1)
                last.then_inc(s["pe_b"], 1)
                pe.wait_ge(s["act_xt"], i + 1)
                for h in range(MH):
                    for k in range(KT):
                        last = T.matmul(two(0)[:, h * DK:(h + 1) * DK], cht[:, UT0 + h * KT + k, :], wmk[:, h, k, :],
                                        start=k == 0, stop=k == KT - 1)
                last.then_inc(s["pe_kk"], 1)
                pe.wait_ge(s["act_qk"], i + 1)
                for h in range(MH):
                    for k in range(KT):
                        last = T.matmul(PB[:, 2, h * CH:(h + 1) * CH], kT[:, h * KT + k, :], qT[:, h * KT + k, :],
                                        start=k == 0, stop=k == KT - 1)
                last.then_inc(s["pe_st"], 1)
                if isinstance(i, int) and i == 0:
                    sample_start()
                else:
                    mix_transposes(pe, P, i - 1)
                pe.wait_ge(s["dve_mm"], i + 1)
                pe.wait_ge(s["dve_kw"], i + 1)
                for h in range(NH):
                    last = T.matmul(two(0)[:, h * HD:(h + 1) * HD], L[:, h, :], xdt[:, h * HD:(h + 1) * HD], start=True, stop=True)
                last.then_inc(s["pe_y"], 1)
                free(pe, s["act_mt"], i)
                free(pe, s["dve_h"], i)
                for g in range(NG):
                    last = T.matmul(PB[:, 4 + g, :], cht[:, CT0 + g, :], hT[:, g * 512:(g + 1) * 512], start=True, stop=True)
                last.then_inc(s["pe_ys"], 1)
                pe.wait_ge(s["pool_xdec"], i + 1)
                for g in range(NG):
                    last = T.matmul(PB[:, 6 + g, :], btok[:, g * NST:(g + 1) * NST], xdec[:, g * 512:(g + 1) * 512], start=True, stop=True)
                last.then_inc(s["pe_hn"], 1)
                pe.wait_ge(s["dve_y"], i + 1)
                for h in range(MH):
                    for k in range(KT):
                        last = T.matmul(two(0)[:, h * DK:(h + 1) * DK], qT[:, h * KT + k, :], cst[:, h * KT + k, :],
                                        start=k == 0, stop=k == KT - 1)
                for h in range(MH):
                    for k in range(KT):
                        last = T.matmul(PB[:, 3, 4 + h:5 + h], qT[:, h * KT + k, :], nst[:, h * KT + k:h * KT + k + 1],
                                        start=k == 0, stop=k == KT - 1)
                last.then_inc(s["pe_nx"], 1)
                pe.wait_ge(s["dve_att"], i + 1)
                pe.wait_ge(s["dve_ys"], i + 1)
                pe.wait_ge(s["v"], 16 * (i + 1))
                for h in range(MH):
                    last = T.matmul(two(4)[:, h * DK:(h + 1) * DK], L[:, NH + h, :], v[:, h * DK:(h + 1) * DK], start=True, stop=True)
                for h in range(MH):
                    last = T.matmul(PB[:, 3, h:h + 1], L[:, NH + h, :], onec[:, :], start=True, stop=True)
                last.then_inc(s["pe_ni"], 1)
                pe.wait_ge(s["dve_h"], i + 1)
                for j in range(4):
                    h = j // KT
                    last = T.matmul(two(6)[:, j * DK:(j + 1) * DK], kw[:, j * P:(j + 1) * P], v[:, h * DK:(h + 1) * DK], start=True, stop=True)
                for h in range(MH):
                    for k in range(KT):
                        j = h * KT + k
                        last = T.matmul(PB[:, 2, j:j + 1], kw[:, j * P:(j + 1) * P], onec[:, :], start=True, stop=True)
                last.then_inc(s["pe_c1"], 1)
                pe.wait_ge(s["dve_num"], i + 1)
                for j in range(4, 8):
                    h = j // KT
                    last = T.matmul(two(4)[:, (j - 4) * DK:(j - 3) * DK], kw[:, j * P:(j + 1) * P], v[:, h * DK:(h + 1) * DK], start=True, stop=True)
                last.then_inc(s["pe_c2"], 1)
                pe.wait_ge(ss["c_new"], i + 1)
                pe.wait_ge(s["act_nx"], i + 1)
                for j in range(8):
                    h, e = j // KT, j % KT
                    for k in range(KT):
                        last = T.matmul(PB[:, 1, j:j + 1], cs[q][:, h * KT + k, e * P:(e + 1) * P],
                                        cur[q][:, 28 + h * KT + k:29 + h * KT + k], start=k == 0, stop=k == KT - 1)
                last.then_inc(ss["num"], 1)
            pe.wait_ge(ss["numc"], NCH)
            pe.wait_ge(s["dve_c2"], NCH)
            for j in range(8):
                T.transpose(two(2)[0:B, j * P:(j + 1) * P], numc[:, j, :], ident[:, :])
            for h in range(MH):
                for k in range(KT):
                    T.matmul(PB[0:B, 4, h:h + 1], pr[:, h * KT + k, :], onec[:, :], start=k == 0, stop=k == KT - 1)
            for j in range(8):
                T.matmul(two(0)[0:B, j * P:(j + 1) * P], ysc[:, j, :], ident[:, :], start=True, stop=False)
                last = T.matmul(two(0)[0:B, j * P:(j + 1) * P], ych[:, j, :], ident[:, :], start=False, stop=True)
            last.then_inc(ss["den"], 1)
            pe.wait_ge(ss["end"], 1)
            mix_transposes(pe, P, NCH - 1)
            pe.wait_ge(s["act_mt"], NCH)
            mix_transposes(pe, B, NCH)

        @block.scalar
        def _(act):
            act.dma_start(chs[:, :, :], cht_d[:, :, SEQ:NTOK].rearrange("j p t -> p j t")).then_inc(ss["ld"], 16)
            act.dma_start(rsb[:, :, :], rows_s_d.partition_broadcast(P)).then_inc(ss["ld"], 16)
            for half in range(2):
                for dst, r in ((nas, R_NACS), (dts[:, :, :], R_DT)):
                    act.dma_start(dst[half * HD:(half + 1) * HD, :, :],
                                  rows_s_d[r:r + NH, :].rearrange("(j two) b -> two j b", two=2)[half].partition_broadcast(HD)).then_inc(ss["ld"], 16)
            act.dma_start(ns[:, :, :], a["n_state"]).then_inc(ss["ld"], 16)
            act.dma_start(dsc[:, :], a["d_skip_ch"]).then_inc(ss["ld"], 16)
            act.dma_start(e_ems[:, :], rows_s_d[R_MT:R_MT + MH, :].rearrange("h b -> b h"),
                          allow_slow_non_contiguous=True).then_inc(ss["ld"], 16)

            def sample_start():
                act.wait_ge(ss["ld"], 16 * 9)
                act.wait_ge(ss["bct"], 1)
                S.copy(bcsb[:, :], PB[0:B, 6, :]).then_inc(ss["bcc"], 1)
                act.wait_ge(ss["bcc"], 1)
                act.dma_start(bc_d.rearrange("b a n -> b (a n)"), bcsb[:, :]).then_inc(ss["bcd"], 16)
                S.activation(nas, nas, ACT.Exp, scale=-1.0)
                S.activation(wos, rsb[:, R_WLOG:R_WLOG + MH, :], ACT.Exp)
                S.activation(e_ems[:, :], e_ems[:, :], ACT.Exp, scale=-1.0)
                act.wait_ge(ss["arg"], 1)
                S.activation(wss[:, :, :], wss[:, :, :], ACT.Exp).then_inc(ss["exp"], 1)
                act.wait_ge(ss["qk"], 1)
                S.copy(qs.rearrange("p a b -> p (a b)"), PB[:, 4, 0:64])
                S.activation(ks.rearrange("p a b -> p (a b)"), PB[:, 5, 0:64], ACT.Copy, scale=DK ** -0.5).then_inc(ss["qkc"], 1)

            act.wait_ge(s["setup"], 1)
            for i, q in pairs(act):
                act.wait_ge(s["pe_a"], i + 1)
                free(act, s["pe_hn"], i)
                free(act, s["pool_dx"], i)
                free(act, s["dve_xdt"], i)
                S.copy(cols[q][:, :], PB[:, 2, 256:256 + NROW])
                S.copy(btok[:, :], PB[:, 2, 0:256])
                S.copy(xtok[:, :], two(0)).then_inc(s["act_xt"], 1)
                act.wait_ge(s["act_xt"], i + 1)
                act.wait_ge(s["rb"], 16 * (i + 1))
                S.activation(e_ea[q][:, :], cols[q][:, R_NACS:R_NACS + NH], ACT.Exp, scale=-1.0)
                S.activation(e_wi[q][:, :], cols[q][:, R_WLOG:R_WLOG + MH], ACT.Exp)
                S.activation(e_em[q][:, :], cols[q][:, R_MT:R_MT + MH], ACT.Exp, scale=-1.0)
                S.activation(e_hd[q][:, :], rb[:, R_NACS:R_NACS + NH, CH - 1], ACT.Exp, scale=-1.0)
                S.activation(e_wo[q][:, :], rb[:, R_WLOG:R_WLOG + MH, CH - 1], ACT.Exp)
                act.wait_ge(s["pool_arg"], i + 1)
                S.activation(e_de[q][:, :], e_de[q][:, :], ACT.Exp)
                S.activation(e_ws[q][:, :], e_ws[q][:, :], ACT.Exp).then_inc(s["act_small"], 1)
                if not (isinstance(i, int) and i == 0):
                    root(act, P, i - 1)
                act.wait_ge(s["pool_l"], i + 1)
                for h in range(NH):
                    last = S.activation(L[:, h, :], L[:, h, :], ACT.Exp, scale=-1.0, bias=cols[q][:, R_NACS + h:R_NACS + h + 1])
                last.then_inc(s["act_l"], 1)
                act.wait_ge(s["pe_b"], i + 1)
                free(act, s["pe_nx"], i)
                S.copy(qT[:, :, :].rearrange("p a n -> p (a n)"), two(4))
                S.activation(kT[:, :, :].rearrange("p a n -> p (a n)"), two(6), ACT.Copy, scale=DK ** -0.5).then_inc(s["act_qk"], 1)
                for h in range(MH):
                    last = S.activation(L[:, NH + h, :], L[:, NH + h, :], ACT.Exp, scale=-1.0, bias=cols[q][:, R_G + h:R_G + h + 1])
                last.then_inc(s["act_l2"], 1)
                if isinstance(i, int) and i == 0:
                    sample_start()
                else:
                    mix_store(act, P, i - 1, (i - 1) * CH)
                act.wait_ge(ss["cur"], i + 1)
                act.wait_ge(s_in[q], 64 * ((i - q) // 2 + 1) if isinstance(i, int) else 32 * (i - q) + 64)
                for j in range(8):
                    last = S.activation(st[q][:, j, :], st[q][:, j, :], ACT.Copy, scale=cur[q][:, j:j + 1])
                last.then_inc(ss["decay"], 1)
                free(act, ss["c_new"], i)
                for h in range(MH):
                    S.activation(cs[q][:, 2 * h:2 * h + 2, :], cs[q][:, 2 * h:2 * h + 2, :], ACT.Copy, scale=cur[q][:, 8 + h:9 + h])
                    for k in range(KT):
                        j = h * KT + k
                        last = S.activation(t4[:, j, :], vb[q][:, h * DK:(h + 1) * DK], ACT.Copy, scale=cur[q][:, 12 + j:13 + j])
                last.then_inc(ss["outer"], 1)
                act.wait_ge(s["pe_nx"], i + 1)
                free(act, s["dve_num"], i)
                for h in range(MH):
                    last = S.activation(nx[:, h * DK:(h + 1) * DK], two(0)[:, h * DK:(h + 1) * DK], ACT.Copy, scale=e_wi[q][:, h:h + 1])
                last.then_inc(s["act_nx"], 1)
                act.wait_ge(ss["st_new"], i + 1)
                act.dma_start(o["s_ssd"][bass.ds(i, 1)].rearrange("b (j p) n -> p (b j) n", p=P), st[q][:, :, :]).then_inc(s_out[q], 16)
                act.wait_ge(ss["num"], i + 1)
                S.copy(numc[:, :, bass.ds(i, 1)], PB[:, 1, 0:8].unsqueeze(2)).then_inc(ss["numc"], 1)
                act.dma_start(o["s_c"][bass.ds(i, 1)].rearrange("b (j p) v -> p (b j) v", p=P), cs[q][:, :, :]).then_inc(s_out[q], 16)
            act.wait_ge(s["dve_c2"], NCH)
            act.dma_start(o["p_ssd"], hT[:, :]).then_inc(s["outs"], 16)
            act.dma_start(o["p_c"], cst[:, :, :]).then_inc(s["outs"], 16)
            act.dma_start(o["p_n"], nst[:, :]).then_inc(s["outs"], 16)
            act.dma_start(o["s_n"], ns[:, :, :]).then_inc(s["outs"], 16)
            root(act, P, NCH - 1)
            act.wait_ge(ss["den"], 1)
            act.wait_ge(s["dve_num"], NCH)
            act.wait_ge(s["pool_dx"], NCH)
            act.wait_ge(s["dve_xdt"], NCH)
            S.copy(den_s[:, 0:4], PB[0:B, 4, 0:4]).then_inc(ss["end"], 1)
            S.copy(num_s, two(2)[0:B, :])
            S.copy(y_s, two(0)[0:B, :]).then_inc(ss["end"], 1)
            mix_store(act, P, NCH - 1, (NCH - 1) * CH)
            root(act, B, NCH)
            mix_store(act, B, NCH, SEQ)
            act.wait_ge(s["outs"], 64)
            for q in range(2):
                act.wait_ge(s_out[q], 16 * B)
            act.wait_ge(s["stored"], 16 * (NCH + 1))

        @block.gpsimd
        def _(pool):
            G.memset(maskp[:, :], 0.0).then_inc(s["mask"], 1)
            pool.wait_ge(s["mask"], 1)
            G.affine_select(out=maskp[:, :], in_=maskp[:, :], compare_op=ALU.is_ge, fill=BIG,
                            base=0, pattern=[[1, CH]], channel_multiplier=-1).then_inc(s["mask"], 1)
            pool.wait_ge(s["mask"], 2)
            for i, q in pairs(pool):
                pool.wait_ge(s["rb"], 16 * (i + 1))
                free(pool, s["pe_ni"], i)
                G.tensor_tensor(L[:, :, :], rb[:, 0:NH + MH, :],
                                maskp[:, :].unsqueeze(1).to_broadcast([P, NH + MH, CH]), ALU.add).then_inc(s["pool_l"], 1)
                pool.wait_ge(s["act_xt"], i + 1)
                G.tensor_tensor(e_de[q][:, :], cols[q][:, R_NACS:R_NACS + NH], rb[:, R_NACS:R_NACS + NH, CH - 1], ALU.subtract)
                G.tensor_tensor(e_ws[q][:, :], cols[q][:, R_G:R_G + MH], rb[:, R_M:R_M + MH, CH - 1], ALU.subtract).then_inc(s["pool_arg"], 1)
                if isinstance(i, int) and i == 0:
                    pool.wait_ge(s["w"], 48)
                    pool.wait_ge(s["setup"], 1)
                free(pool, s["dve_y"], i)
                G.tensor_tensor(heads(dx[:, :], HD), heads(xtok[:, :], HD), wide(dsk[:, :], HD), ALU.mult).then_inc(s["pool_dx"], 1)
                pool.wait_ge(s["dve_xdt"], i + 1)
                pool.wait_ge(s["act_small"], i + 1)
                free(pool, s["pe_hn"], i)
                G.tensor_tensor(heads(xdec[:, :], HD), heads(xdt[:, :], HD), wide(e_de[q][:, :], HD), ALU.mult).then_inc(s["pool_xdec"], 1)
                pool.wait_ge(s["zo"], 32 * (i + 1))
                free(pool, s["dve_mix"], i)
                G.tensor_tensor(og[:, :], zvo[:, 4:6, :].rearrange("p a n -> p (a n)"), gm[:, :], ALU.mult).then_inc(s["pool_og"], 1)
                pool.wait_ge(s["pe_ys"], i + 1)
                G.tensor_tensor(heads(hT[:, :], HD), heads(hT[:, :], HD), wide(e_hd[q][:, :], HD), ALU.mult).then_inc(s["pool_hs"], 1)
            pool.wait_ge(ss["zo"], 32)
            G.tensor_tensor(o_s, o_s, gm[0:B, :], ALU.mult).then_inc(s["pool_og"], 1)

        @block.vector
        def _(dve):
            V.memset(onec[:, :], 1.0)
            V.memset(hT[:, :], 0.0)
            V.memset(cst[:, :, :], 0.0)
            V.memset(nst[:, :], 0.0).then_inc(s["setup"], 1)
            dve.wait_ge(s["setup"], 1)
            cp = Chain(dve, c_p, 0, s["passed"])

            def sample_start():
                dve.wait_ge(ss["ld"], 16 * 9)
                V.tensor_tensor(wss[:, :, :], rsb[:, R_G:R_G + MH, :], rsb[:, R_M:R_M + MH, :], ALU.subtract).then_inc(ss["arg"], 1)
                V.tensor_tensor(dxt, dts[:, :, :], chs[:, 0:8, :], ALU.mult)
                V.tensor_tensor(ysc[:, :, :], chs[:, 0:8, :], wide(dsc[:, :], B), ALU.mult)
                dve.wait_ge(ss["exp"], 1)
                dve.wait_ge(ss["qkc"], 1)
                cp.link(V.tensor_tensor(by_head(ks), by_head(ks), wss[:, :, :].unsqueeze(2).to_broadcast([P, MH, KT, B]), ALU.mult))
                cp.link(V.tensor_tensor(by_head(ns[:, :, :]), by_head(ns[:, :, :]), wos.unsqueeze(2).to_broadcast([P, MH, KT, B]), ALU.mult))
                cp.link(V.tensor_tensor(ns[:, :, :], ns[:, :, :], ks, ALU.add))
                cp.link(V.tensor_tensor(pr[:, :, :], ns[:, :, :], qs, ALU.mult))

            z = zvo[:, 0:2, :].rearrange("p a n -> p (a n)")
            for i, q in pairs(dve):
                ch = Chain(dve, c_d, DVE_LINKS * i, s["passed"])
                dve.wait_ge(s["act_xt"], i + 1)
                free(dve, s["pe_y"], i)
                free(dve, s["pool_xdec"], i)
                V.tensor_tensor(heads(xdt[:, :], HD), heads(xtok[:, :], HD), wide(cols[q][:, R_DT:R_DT + NH], HD), ALU.mult).then_inc(s["dve_xdt"], 1)
                dve.wait_ge(s["act_small"], i + 1)
                dve.wait_ge(s["pe_kk"], i + 1)
                V.scalar_tensor_tensor(heads(kw[:, :], DK), heads(two(0), DK), DK ** -0.5, wide(e_ws[q][:, :], DK),
                                       ALU.mult, ALU.mult).then_inc(s["dve_kw"], 1)
                dve.wait_ge(s["act_l"], i + 1)
                for g in range(NG):
                    last = V.tensor_tensor(L[:, g * 8:g * 8 + 8, :], L[:, g * 8:g * 8 + 8, :],
                                           PB[:, 3, g * CH:(g + 1) * CH].unsqueeze(1).to_broadcast([P, 8, CH]), ALU.mult)
                last.then_inc(s["dve_mm"], 1)
                dve.wait_ge(s["act_l2"], i + 1)
                dve.wait_ge(s["pe_st"], i + 1)
                V.tensor_tensor(L[:, NH:NH + MH, :], L[:, NH:NH + MH, :], heads(PB[:, 2, :], CH), ALU.mult).then_inc(s["dve_att"], 1)
                if isinstance(i, int) and i == 0:
                    sample_start()
                V.tensor_copy(cur[q][:, :], scl[:, :, bass.ds(i, 1)].rearrange("p a b -> p (a b)")).then_inc(ss["cur"], 1)
                dve.wait_ge(s_in[q], 64 * ((i - q) // 2 + 1) if isinstance(i, int) else 32 * (i - q) + 64)
                bcq = bb[q][:, :].rearrange("p (c g n) -> p c g n", c=2, g=NG)
                over = [P, NG, 4, NST]
                dve.wait_ge(ss["cur"], i + 1)
                ch.link(V.tensor_tensor(groups(t3[:, :, :]), bcq[:, 0].unsqueeze(2).to_broadcast(over),
                                        groups(cur[q][:, 20:28].unsqueeze(2)).to_broadcast(over), ALU.mult))
                dve.wait_ge(s["pe_y"], i + 1)
                dve.wait_ge(s["pool_dx"], i + 1)
                V.tensor_tensor(ysb[:, :], two(0), dx[:, :], ALU.add).then_inc(s["dve_y"], 1)
                dve.wait_ge(s["pe_ys"], i + 1)
                V.tensor_tensor(heads(yst[:, :], HD), heads(two(4), HD), wide(e_ea[q][:, :], HD), ALU.mult).then_inc(s["dve_ys"], 1)
                dve.wait_ge(s["pool_hs"], i + 1)
                dve.wait_ge(s["pe_hn"], i + 1)
                V.tensor_tensor(hT[:, :], hT[:, :], two(6), ALU.add).then_inc(s["dve_h"], 1)
                dve.wait_ge(s["dve_ys"], i + 1)
                ch.link(V.tensor_tensor(ysb[:, :], ysb[:, :], yst[:, :], ALU.add))
                dve.wait_ge(s["zo"], 32 * (i + 1))
                gate_y(ch, P, z, ysb[:, :])
                dve.wait_ge(ss["decay"], i + 1)
                V.tensor_tensor(st[q][:, :, :], st[q][:, :, :], t3[:, :, :], ALU.add).then_inc(ss["st_new"], 1)
                dve.wait_ge(ss["st_new"], i + 1)
                V.tensor_tensor(groups(t3[:, :, :]), groups(st[q][:, :, :]), bcq[:, 1].unsqueeze(2).to_broadcast(over), ALU.mult).then_inc(ss["red"], 1)
                dve.wait_ge(ss["outer"], i + 1)
                V.tensor_tensor(cs[q][:, :, :], cs[q][:, :, :], t4[:, :, :], ALU.add).then_inc(ss["c_new"], 1)
                dve.wait_ge(s["pe_ni"], i + 1)
                dve.wait_ge(s["act_nx"], i + 1)
                V.tensor_tensor(num[:, :], two(4), nx[:, :], ALU.add).then_inc(s["dve_num"], 1)
                ch.link(V.tensor_tensor(den[:, 0:4], PB[:, 3, 4:8], e_wi[q][:, :], ALU.mult))
                V.tensor_tensor(den[:, 0:4], den[:, 0:4], PB[:, 3, 0:4], ALU.add).then_inc(s["dve_den"], 1)
                dve.wait_ge(ss["red"], i + 1)
                V.tensor_reduce(ych[:, :, bass.ds(i, 1)].rearrange("p a b -> p (a b)"), t3[:, :, :], AX, ALU.add)
                ch.link(V.tensor_tensor(heads(nst[:, :], KT), heads(nst[:, :], KT), wide(e_wo[q][:, :], KT), ALU.mult))
                dve.wait_ge(s["pe_c1"], i + 1)
                V.tensor_tensor(nst[:, :], nst[:, :], PB[:, 2, 0:8], ALU.add)
                for half, done in ((0, "c1"), (1, "c2")):
                    dve.wait_ge(s["pe_" + done], i + 1)
                    for h in (2 * half, 2 * half + 1):
                        last = V.scalar_tensor_tensor(cst[:, 2 * h:2 * h + 2, :], cst[:, 2 * h:2 * h + 2, :], e_wo[q][:, h:h + 1],
                                                      two((6, 4)[half])[:, (h % 2) * 512:(h % 2) * 512 + 512].rearrange("p (k v) -> p k v", k=KT),
                                                      ALU.mult, ALU.add)
                    last.then_inc(s["dve_" + done], 1)
                dve.wait_ge(s["dve_den"], i + 1)
                dve.wait_ge(s["dve_num"], i + 1)
                head_out(dve, ch, P, e_em[q][:, :], i, ysb[:, :], num[:, :], den[:, :], og[:, :])
                assert ch.n == DVE_LINKS, ch.n
            dve.wait_ge(s["dve_mix"], NCH)
            dve.wait_ge(ss["end"], 2)
            dve.wait_ge(ss["zo"], 32)
            gate_y(cp, B, z_s, y_s)
            head_out(dve, cp, B, e_ems[:, :], NCH, y_s, num_s, den_s[:, :], o_s)
            dve.wait_ge(s["stored"], 16 * NCH)
            V.memset(mixT[:, :, :], 0.0).then_inc(s["pad"], 1)


def build_peer(nc, a, o, sem, PB, ident, two, mixt_d, wp_d, x1_d):
    f32, u32 = mybir.dt.float32, mybir.dt.uint32
    ACT = mybir.ActivationFunctionType
    X = mybir.AxisListType.X
    V = nc.vector
    T = nc.tensor

    with ExitStack() as ctx:
        def sb(name, shape, dt=f32):
            return ctx.enter_context(nc.sbuf_tensor(name, shape, dt))

        wo = sb("wo", [P, 16, D])
        wp = sb("wp", [P, NHC, KD, NK])
        work = sb("work", [P, 2 * D])
        mt = work[:, :].rearrange("p (j t) -> p j t", j=16)
        x1T = work[:, 0:D].rearrange("p (k t) -> p k t", k=KD)
        sc = work[:, :].rearrange("p (j n) -> p j n", j=NHC)
        cand = work[:, :].rearrange("p (h n) -> p h n", h=PH)
        eq = work[:, :].rearrange("p (g k) -> p g k", k=TOPK)
        x1 = sb("x1", [P, D])
        g1, b1, g2, b2 = (sb(n, [P, D]) for n in ("g1", "b1", "g2", "b2"))
        vals = sb("vals", [P, NHC, TOPK])
        idx = sb("idx", [P, NHC, TOPK], u32)
        idf = idx[:, :, :].bitcast(f32)
        topv = sb("topv", [P, PH, TOPK])
        pos = sb("pos", [P, PH, TOPK], u32)
        pa = sb("pa", [P, 2, PH, TOPK], u32)
        paf = pa[:, :, :, :].bitcast(f32)
        io = sb("io", [P, TOPK])
        iou = sb("iou", [P, TOPK], mybir.dt.int32)
        e2 = sb("e2", [P, 2, PH, TOPK])
        ef = e2[:, 0, :, :]
        eo = sb("eo", [P, PH, TOPK], u32)
        gt = sb("gt", [P, PH, TOPK])
        sg = sb("sg", [P, PH])
        st6, mv = sb("st6", [P, 2, 6]), sb("mv1", [P, 2])
        ub, vbf = sb("ub", [P, NB, D]), sb("vbf", [P, NB, D])
        ixg = sb("ixg", [P, PH, TOPK], u32)
        gg = sb("gg", [P, PH, TOPK])
        hid, wg = sb("hid", [P, 2, TOPK]), sb("wg", [P, 2, TOPK])
        dg = sb("dg", [P, 2, P])
        x1g, acc = sb("x1g", [P, D]), sb("acc", [P, D])
        st7, mv7 = sb("st7", [P, 2, 6]), sb("mv7", [P, 2])
        x1s, us = wo[:, 0:NSMP, :], wo[:, NSMP:2 * NSMP, :]
        vs = wp[:, :, :, :].rearrange("p a b c -> p (a b c)").rearrange("p (b n) -> p b n", n=D)
        ixs = sb("ixs", [P, NSMP], u32)
        ggs, hids, wgs = sb("ggs", [P, NSMP]), sb("hids", [P, NSMP]), sb("wgs", [P, NSMP, NSMP])

        s = {n: sem("pk_" + n) for n in (
            "g1 g2 wp mt xr mix var sq x1 x1t x1tc sco0 scc0 sco scc acc0 ymul top0 exp0 top exp out iota iou passed ix_lo ix_hi x1g "
            "dot gelu gate diag pv ysum yvar ysq y stored ident x1st smp dots gates gz go tr trc").split()}
        s_wo = [sem(f"w_out{n}") for n in range(4)]
        s_u = [sem(f"u_rows{n}") for n in range(NB)]
        s_v = [sem(f"v_rows{n}") for n in range(NB)]
        s_us = [sem(f"smp_u{n}") for n in range(NSMP)]
        s_vs = [sem(f"smp_v{n}") for n in range(NSMP)]
        c_0 = sem("dve_chain_first")
        c_p, c_y, c_s = sem("dve_chain_pick"), sem("dve_chain_norm"), sem("dve_chain_last")
        PICK_LINKS, NORM_LINKS = 123, 4

        def pe_pick(pe, t, h, k):
            if h < 2:
                if (h, k) == (0, 0):
                    pe.wait_ge(s["mt"], 16 * (t + 1))
                    free(pe, s["scc"], t)
                last = T.matmul(PB[:, 4 + h, :], mt[:, k, :], wo[:, k, h * 512:(h + 1) * 512], start=k == 0, stop=k == 15)
                if (h, k) == (1, 15):
                    last.then_inc(s["mix"], 1)
            elif h == 2 and k >= 12:
                if k == 12:
                    pe.wait_ge(s["x1"], t + 1)
                    pe.sem_inc(s["passed"], 1)
                for j in (2 * (k - 12), 2 * (k - 12) + 1):
                    last = T.transpose(PB[:, 6 + j // 4, (j % 4) * CH:(j % 4 + 1) * CH], x1[:, j * P:(j + 1) * P], ident[:, :])
                if k == 15:
                    last.then_inc(s["x1t"], 1)
            elif h in (3, 4):
                if (h, k) == (3, 0):
                    pe.wait_ge(s["x1tc"], t + 1)
                n, kk = 2 * (h - 3) + k // 8, k % 8
                last = T.matmul(PB[:, 4 + n, :].rearrange("p (h n) -> p h n", h=4), x1T[:, kk, :], wp[:, 4 * n:4 * n + 4, kk, :],
                                start=kk == 0, stop=kk == KD - 1)
                if (h, k) == (4, 15):
                    last.then_inc(s["sco"], 1)
                elif kk == KD - 1 and isinstance(t, int) and t == 0:
                    last.then_inc(s["sco0"], 1)

        def act_pick(act, t, h, k):
            if (h, k) == (2, 4):
                act.wait_ge(s["var"], t + 1)
                nc.scalar.activation(mv[:, 1:2], mv[:, 1:2], ACT.Sqrt).then_inc(s["sq"], 1)
            elif (h, k) == (2, 15):
                act.wait_ge(s["x1t"], t + 1)
                nc.scalar.copy(work[:, 0:D], two(6)).then_inc(s["x1tc"], 1)
            elif (h, k) == (5, 0) and isinstance(t, int) and t == 0:
                for n in range(4):
                    act.wait_ge(*((s["sco0"], n + 1) if n < 3 else (s["sco"], 1)))
                    nc.scalar.copy(first_scores[n // 2][:, (n % 2) * 512:(n % 2 + 1) * 512],
                                   PB[:, 4 + n, :]).then_inc(s["scc0"] if n < 3 else s["scc"], 1)
            elif (h, k) == (5, 0):
                act.wait_ge(s["sco"], t + 1)
                nc.scalar.copy(work[:, 0:D], two(4))
                nc.scalar.copy(work[:, D:2 * D], two(6)).then_inc(s["scc"], 1)
            elif (h, k) == (7, 2):
                act.wait_ge(s["top"], t)
                nc.scalar.activation(gt[:, :, :], gt[:, :, :], ACT.Exp).then_inc(s["exp"], 1)

        def top16(ch, src, val, ind):
            ch.link_plain(V.max(val[:, 0:8], src))
            V.max_index(ind[:, 0:8], val[:, 0:8], src)
            ch.link_plain(V.match_replace(src, val[:, 0:8], src, NEG))
            ch.link_plain(V.max(val[:, 8:16], src))
            ch.link(V.max_index(ind[:, 8:16], val[:, 8:16], src))

        def dve_pick(dve, ch, t, h, k):
            if (h, k) == (2, 0):
                dve.wait_ge(s["mix"], t + 1)
                dve.wait_ge(s["xr"], 16 * (t + 1))
                ch.link(V.scalar_tensor_tensor(x1[:, :], x1[:, :], ALPHA, two(4), ALU.mult, ALU.add))
            elif (h, k) == (2, 1):
                V.bn_stats(st6[:, 0, :], x1[:, 0:512])
                ch.link_plain(V.bn_stats(st6[:, 1, :], x1[:, 512:D]))
            elif (h, k) == (2, 2):
                ch.link(V.bn_aggr(mv[:, :], st6[:, :, :]))
                V.tensor_scalar(mv[:, 1:2], mv[:, 1:2], EPS, None, ALU.add).then_inc(s["var"], 1)
            elif (h, k) == (2, 5):
                dve.wait_ge(s["sq"], t + 1)
                ch.link(V.reciprocal(mv[:, 1:2], mv[:, 1:2]))
                ch.link(V.tensor_scalar(x1[:, :], x1[:, :], mv[:, 0:1], mv[:, 1:2], ALU.subtract, ALU.mult))
            elif (h, k) == (2, 7):
                ch.link(V.tensor_tensor(x1[:, :], x1[:, :], g1[:, :], ALU.mult))
            elif (h, k) == (2, 9):
                V.tensor_tensor(x1[:, :], x1[:, :], b1[:, :], ALU.add).then_inc(s["x1"], 1)
            elif h == 5:
                if k == 0:
                    dve.wait_ge(s["scc"], t + 1)
                    dve.sem_inc(s["passed"], 1)
                top16(ch, sc[:, k, :], vals[:, k, :], idx[:, k, :])
            elif h == 6 and k % 2 == 0:
                j = k // 2
                if j == 0:
                    ch.link(V.tensor_copy(idf, idx[:, :, :]))
                ch.link_plain(V.tensor_tensor(cand[:, j, :].rearrange("p (x y) -> p x y", x=TOPK),
                                              vals[:, 2 * j, :].unsqueeze(2).to_broadcast([P, TOPK, TOPK]),
                                              vals[:, 2 * j + 1, :].unsqueeze(1).to_broadcast([P, TOPK, TOPK]), ALU.add))
                top16(ch, cand[:, j, :], topv[:, j, :], pos[:, j, :])
            elif (h, k) == (7, 0):
                V.tensor_tensor(gt[:, :, :], topv[:, :, :], topv[:, :, 0:1].to_broadcast([P, PH, TOPK]), ALU.subtract).then_inc(s["top"], 1)
                V.tensor_scalar(pa[:, 0, :, :], pos[:, :, :], 4, None, ALU.logical_shift_right)
                ch.link(V.tensor_scalar(pa[:, 1, :, :], pos[:, :, :], TOPK - 1, None, ALU.bitwise_and))
                ch.link(V.tensor_copy(paf, pa[:, :, :, :]))
            elif h == 7 and 1 <= k <= 6:
                c = (k - 1) // 3
                if k % 3 == 1:
                    ch.link(V.tensor_tensor(eq, paf[:, c, :, :].rearrange("p h k -> p (h k)").unsqueeze(2).to_broadcast([P, P, TOPK]),
                                            io[:, :].unsqueeze(1).to_broadcast([P, P, TOPK]), ALU.is_equal))
                elif k % 3 == 2:
                    q4 = eq.rearrange("p (h k) x -> p h k x", h=PH)
                    ch.link(V.tensor_tensor(q4, q4, idf.rearrange("p (h c) k -> p h c k", c=2)[:, :, c, :].unsqueeze(2).to_broadcast([P, PH, TOPK, TOPK]), ALU.mult))
                else:
                    ch.link(V.tensor_reduce(e2[:, c, :, :].rearrange("p h k -> p (h k)"), eq, X, ALU.add))
            elif (h, k) == (7, 7):
                ch.link(V.scalar_tensor_tensor(ef, ef, float(NK), e2[:, 1, :, :], ALU.mult, ALU.add))
            elif (h, k) == (7, 8):
                dve.wait_ge(s["exp"], t)
                ch.link(V.tensor_reduce(sg[:, :], gt[:, :, :], X, ALU.add))
                ch.link(V.reciprocal(sg[:, :], sg[:, :]))
                ch.link(V.tensor_tensor(gt[:, :, :], gt[:, :, :], sg[:, :].unsqueeze(2).to_broadcast([P, PH, TOPK]), ALU.mult))
            elif (h, k) == (7, 9):
                V.tensor_copy(ixg[:, 0:4, :], ef[:, 0:4, :]).then_inc(s["ix_lo"], 1)

        first_scores = vbf[:, 0, :], acc[:, :]

        def dve_half(dve, ch, half, step):
            h0 = 4 * half
            hs, ls = slice(h0, h0 + 4), slice(2 * h0, 2 * h0 + 8)
            if step < 8:
                if step % 4 == 0:
                    n = 2 * half + step // 4
                    dve.wait_ge(*((s["scc0"], n + 1) if n < 3 else (s["scc"], 1)))
                top16(ch, first_scores[half][:, step * NK:(step + 1) * NK], vals[:, 2 * h0 + step, :], idx[:, 2 * h0 + step, :])
            elif step < 12:
                j = h0 + step - 8
                if step == 8:
                    dve.wait_ge(s["scc"], 1)
                    ch.link(V.tensor_copy(idf[:, ls, :], idx[:, ls, :]))
                pairs_at = (work[:, 0:D], acc[:, :])[half][:, (step - 8) * 256:(step - 7) * 256]
                ch.link_plain(V.tensor_tensor(pairs_at.rearrange("p (x y) -> p x y", x=TOPK),
                                              vals[:, 2 * j, :].unsqueeze(2).to_broadcast([P, TOPK, TOPK]),
                                              vals[:, 2 * j + 1, :].unsqueeze(1).to_broadcast([P, TOPK, TOPK]), ALU.add))
                top16(ch, pairs_at, topv[:, j, :], pos[:, j, :])
            elif step == 12:
                V.tensor_tensor(gt[:, hs, :], topv[:, hs, :], topv[:, hs, 0:1].to_broadcast([P, 4, TOPK]), ALU.subtract).then_inc(s["top0"], 1)
                V.tensor_scalar(pa[:, 0, hs, :], pos[:, hs, :], 4, None, ALU.logical_shift_right)
                ch.link(V.tensor_scalar(pa[:, 1, hs, :], pos[:, hs, :], TOPK - 1, None, ALU.bitwise_and))
                ch.link(V.tensor_copy(paf[:, :, hs, :], pa[:, :, hs, :]))
            elif step < 15:
                c = step - 13
                eqh = (work[:, D:2 * D], acc[:, :])[half].rearrange("p (g k) -> p g k", k=TOPK)
                ch.link(V.tensor_tensor(eqh, paf[:, c, hs, :].rearrange("p h k -> p (h k)").unsqueeze(2).to_broadcast([P, P // 2, TOPK]),
                                        io[:, :].unsqueeze(1).to_broadcast([P, P // 2, TOPK]), ALU.is_equal))
                q4 = eqh.rearrange("p (h k) x -> p h k x", h=4)
                ch.link(V.tensor_tensor(q4, q4, idf.rearrange("p (h c) k -> p h c k", c=2)[:, hs, c, :].unsqueeze(2).to_broadcast([P, 4, TOPK, TOPK]), ALU.mult))
                ch.link(V.tensor_reduce(e2[:, c, hs, :].rearrange("p h k -> p (h k)"), eqh, X, ALU.add))
            else:
                ch.link(V.scalar_tensor_tensor(ef[:, hs, :], ef[:, hs, :], float(NK), e2[:, 1, hs, :], ALU.mult, ALU.add))
                V.tensor_copy(ixg[:, hs, :], ef[:, hs, :]).then_inc(s[("ix_lo", "ix_hi")[half]], 1)
                dve.wait_ge(s["exp0"], half + 1)
                ch.link(V.tensor_reduce(sg[:, hs], gt[:, hs, :], X, ALU.add))
                ch.link(V.reciprocal(sg[:, hs], sg[:, hs]))
                ch.link(V.tensor_tensor(gg[:, hs, :], gt[:, hs, :], sg[:, hs].unsqueeze(2).to_broadcast([P, 4, TOPK]), ALU.mult))

        def act_half(act, half):
            hs = slice(4 * half, 4 * half + 4)
            act.wait_ge(s["top0"], half + 1)
            nc.scalar.activation(gt[:, hs, :], gt[:, hs, :], ACT.Exp).then_inc(s["exp0"], 1)

        SLOTS = {(1, 2 * n): n for n in range(8)} | {(2, 11): 8, (2, 13): 9, (2, 15): 10, (3, 1): 11,
                                                     (3, 3): 12, (3, 5): 13, (3, 7): 14, (3, 12): 15}

        def pe_expert(pe, c, h, k):
            if isinstance(c, int) and c == 0 and h == 0:
                return
            hh = PH * c + h - 1
            pe.wait_ge(s["diag"], TOPK * hh + k + 1)
            pe.wait_ge(s_v[k % NB], 16 * (4 * hh + k // NB + 1))
            if (h, k) == (1, 0):
                free(pe, s["ysum"], c)
            for n in range(2):
                last = T.matmul(PB[:, n, :], dg[:, k % 2, :], vbf[:, k % NB, n * 512:(n + 1) * 512],
                                start=(h, k) == (1, 0), stop=(h, k) == (0, 15))
            last.then_inc(s["pv"], 1)

        def act_expert(act, c, h, k):
            if not (isinstance(c, int) and c == 0 and h == 0):
                hh = PH * c + h - 1
                if k == 0:
                    act.wait_ge(s["gate"], hh + 1)
                free(act, s["pv"], TOPK * hh + k - 1)
                nc.scalar.activation(dg[:, k % 2, :], ident[:, :], ACT.Copy, scale=wg[:, (h - 1) % 2, k:k + 1]).then_inc(s["diag"], 1)

        def act_gelu(act, c, h):
            act.wait_ge(s["dot"], TOPK * (PH * c + h + 1))
            nc.scalar.activation(hid[:, h % 2, :], hid[:, h % 2, :], ACT.Gelu).then_inc(s["gelu"], 1)

        def act_norm(act, c, k):
            if k == 7:
                act.wait_ge(s["yvar"], c)
                nc.scalar.activation(mv7[:, 1:2], mv7[:, 1:2], ACT.Sqrt).then_inc(s["ysq"], 1)
            elif k == 15:
                act.wait_ge(s["y"], c)
                act.dma_start(o["y"][bass.ds((c - 1) * CH, CH), :], acc[:, :]).then_inc(s["stored"], 16)

        def dve_norm(dve, ch, c, k):
            if k == 2:
                dve.wait_ge(s["pv"], TOPK * PH * c)
                V.tensor_tensor(acc[:, :], acc[:, :], two(0), ALU.add).then_inc(s["ysum"], 1)
                dve.wait_ge(s["ysum"], c)
            elif k == 3:
                V.bn_stats(st7[:, 0, :], acc[:, 0:512])
                ch.link_plain(V.bn_stats(st7[:, 1, :], acc[:, 512:D]))
            elif k == 4:
                ch.link(V.bn_aggr(mv7[:, :], st7[:, :, :]))
                V.tensor_scalar(mv7[:, 1:2], mv7[:, 1:2], EPS, None, ALU.add).then_inc(s["yvar"], 1)
            elif k == 8:
                dve.wait_ge(s["ysq"], c)
                ch.link(V.reciprocal(mv7[:, 1:2], mv7[:, 1:2]))
            elif k == 9:
                ch.link(V.tensor_scalar(acc[:, :], acc[:, :], mv7[:, 0:1], mv7[:, 1:2], ALU.subtract, ALU.mult))
            elif k == 11:
                V.tensor_tensor(acc[:, :], acc[:, :], g2[:, :], ALU.mult).then_inc(s["ymul"], 1)
                dve.wait_ge(s["ymul"], c)
            elif k == 13:
                V.tensor_tensor(acc[:, :], acc[:, :], b2[:, :], ALU.add).then_inc(s["y"], 1)


        def dve_start(dve, c):
            if not (isinstance(c, int) and c == 0):
                if not (isinstance(c, int) and c == 1):
                    free(dve, s["stored"], 16 * (c - 1))
                V.tensor_scalar(acc[:, :], x1g[:, :], ALPHA, None, ALU.mult).then_inc(s["acc0"], 1)
                dve.wait_ge(s["acc0"], c)
                V.tensor_copy(gg[:, :, :], gt[:, :, :])
            V.tensor_copy(x1g[:, :], x1[:, :]).then_inc(s["x1g"], 1)
            dve.wait_ge(s["x1g"], c + 1)

        with nc.Block() as block:
            @block.sync
            def _(sp):
                def load(t):
                    free(sp, s["ix_lo"], t)
                    sp.dma_start(work[:, :].rearrange("p (j t) -> p j t", j=16),
                                 mixt_d[:, :, bass.ds(t * CH, CH)].rearrange("j p t -> p j t")).then_inc(s["mt"], 16)
                    free(sp, s["x1g"], t)
                    sp.dma_start(x1[:, :], a["x_tok"][bass.ds(t * CH, CH), :]).then_inc(s["xr"], 16)

                load(0)
                for j in range(4):
                    sp.dma_start(wo[:, 4 * j:4 * j + 4, :], a["w_out"][:, 4 * j:4 * j + 4, :]).then_inc(s_wo[j], 16)
                for dst, name in ((g1, "ln1_g"), (b1, "ln1_b")):
                    sp.dma_start(dst[:, :], a[name].partition_broadcast(P)).then_inc(s["g1"], 16)
                for j in range(NHC):
                    sp.dma_start(wp[:, j, :, :], wp_d[j]).then_inc(s["wp"], 16)
                for dst, name in ((g2, "ln2_g"), (b2, "ln2_b")):
                    sp.dma_start(dst[:, :], a[name].partition_broadcast(P)).then_inc(s["g2"], 16)
                for c in steps(sp, NCH):
                    load(c + 1)
                sp.wait_ge(s["x1st"], 16)
                sp.dma_start(x1s, x1_d.partition_broadcast(P)).then_inc(s["smp"], 16)

            @block.gpsimd
            def _(pool):
                nc.gpsimd.iota(iou[:, :], [[1, TOPK]], 0, 0).then_inc(s["iou"], 1)
                pool.wait_ge(s["iou"], 1)

                def gather(buf, table, index, done):
                    pool.indirect_dma_start(out=buf, out_offset=None, in_=a[table],
                                            in_offset=bass.IndirectOffsetOnAxis(ap=index, axis=0)).then_inc(done, 16)

                def gathers(c, h, k):
                    hh = PH * c + h
                    u_now = not (isinstance(c, int) and c == NCH)
                    v_now = not (isinstance(c, int) and c == 0 and h == 0)
                    if (h, k) == (0, 0) and u_now:
                        pool.wait_ge(s["ix_lo"], c + 1)
                    if (h, k) == (4, 0):
                        pool.wait_ge(s["ix_hi"], c + 1)
                    if u_now:
                        free(pool, s["dot"], TOPK * hh + k + 1 - NB)
                    if v_now:
                        free(pool, s["pv"], TOPK * (hh - 1) + k + 1 - NB)
                    pool.sem_inc(s["passed"], 1)
                    if u_now:
                        gather(ub[:, k % NB, :], "peer_u", ixg[:, h, k:k + 1], s_u[k % NB])
                    if v_now:
                        gather(vbf[:, k % NB, :], "peer_v", ixg[:, (h - 1) % PH, k:k + 1], s_v[k % NB])

                for c in steps(pool, NCH):
                    for h in range(PH):
                        for k in range(TOPK):
                            gathers(c, h, k)
                for k in range(TOPK):
                    gathers(NCH, 0, k)
                pool.wait_ge(s["trc"], 1)
                for b in range(NSMP):
                    gather(us[:, b, :], "peer_u", ixs[:, b:b + 1], s_us[b])
                    gather(vs[:, b, :], "peer_v", ixs[:, b:b + 1], s_vs[b])

            @block.vector
            def _(dve):
                V.memset(wgs[:, :, :], 0.0)
                dve.wait_ge(s["iou"], 1)
                V.tensor_copy(io[:, :], iou[:, :]).then_inc(s["iota"], 1)
                dve.wait_ge(s["iota"], 1)
                dve.wait_ge(s["g1"], 32)
                first_ch = Chain(dve, c_0, 0, s["passed"])
                for k in range(TOPK):
                    dve_pick(dve, first_ch, 0, 2, k)
                for step in range(16):
                    dve_half(dve, first_ch, 0, step)
                dve.wait_ge(s["g2"], 32)
                for c in steps(dve, NCH):
                    ch = Chain(dve, c_p, PICK_LINKS * c, s["passed"])
                    cy = Chain(dve, c_y, NORM_LINKS * (c - 1), s["passed"])
                    first = isinstance(c, int) and c == 0
                    dve_start(dve, c)
                    for h in range(PH):
                        hh = PH * c + h
                        for k in range(TOPK):
                            dve.wait_ge(s_u[k % NB], 16 * (4 * hh + k // NB + 1))
                            V.tensor_tensor_reduce(out=ub[:, k % NB, :], in0=ub[:, k % NB, :], in1=x1g[:, :], scale=1.0, scalar=0.0,
                                                   op0=ALU.mult, op1=ALU.add, accum_out=hid[:, h % 2, k:k + 1]).then_inc(s["dot"], 1)
                            if h == 1 and not first:
                                dve_norm(dve, cy, c, k)
                            if first and (h, k) in SLOTS:
                                dve_half(dve, first_ch, 1, SLOTS[h, k])
                            if (h, k) == (1, 5) and not first:
                                V.tensor_copy(ixg[:, 4:8, :], ef[:, 4:8, :]).then_inc(s["ix_hi"], 1)
                            dve_pick(dve, ch, c + 1, h, k)
                        dve.wait_ge(s["gelu"], hh + 1)
                        if not (first and h < 2):
                            dve.wait_ge(s["pv"], TOPK * (hh - 1))
                        V.tensor_tensor(wg[:, h % 2, :], hid[:, h % 2, :], gg[:, h, :], ALU.mult).then_inc(s["gate"], 1)
                        dve.wait_ge(s["gate"], hh + 1)
                    assert first or cy.n == NORM_LINKS, cy.n
                c, r = NCH, NSMP
                cy = Chain(dve, c_y, NORM_LINKS * (c - 1), s["passed"])
                dve.wait_ge(s["stored"], 16 * (c - 1))
                V.tensor_scalar(acc[:, :], x1g[:, :], ALPHA, None, ALU.mult).then_inc(s["acc0"], 1)
                dve.wait_ge(s["acc0"], c)
                dve.wait_ge(s["tr"], 1)
                V.tensor_copy(ixs[:, :], PB[:, 4, 0:r])
                V.tensor_copy(ggs[:, :], PB[:, 4, r:2 * r]).then_inc(s["trc"], 1)
                dve.wait_ge(s["smp"], 16)

                def gate_sample(b):
                    dve.wait_ge(s["gates"], b + 1)
                    V.tensor_tensor(wgs[:, b, b:b + 1], hids[:, b:b + 1], ggs[:, b:b + 1], ALU.mult).then_inc(s["gz"], 1)

                for b in range(r):
                    dve.wait_ge(s_us[b], 16)
                    last = V.tensor_tensor_reduce(out=us[:, b, :], in0=us[:, b, :], in1=x1s[:, b, :], scale=1.0, scalar=0.0,
                                                  op0=ALU.mult, op1=ALU.add, accum_out=hids[:, b:b + 1])
                    last.then_inc(s["dots"], 1)
                    if b > 0:
                        gate_sample(b - 1)
                gate_sample(r - 1)
                for k in range(TOPK):
                    dve_norm(dve, cy, c, k)
                dve.wait_ge(s["go"], 1)
                ch = Chain(dve, c_s, 0, s["passed"])
                ch.link(V.scalar_tensor_tensor(x1[0:r, :], x1[0:r, :], ALPHA, two(6)[0:r, :], ALU.mult, ALU.add))
                for n in range(2):
                    last = V.bn_stats(st6[0:r, n, :], x1[0:r, n * 512:(n + 1) * 512])
                ch.link(last)
                ch.link(V.bn_aggr(mv[0:r, :], st6[0:r, :, :]))
                V.tensor_scalar(mv[0:r, 1:2], mv[0:r, 1:2], EPS, None, ALU.add).then_inc(s["var"], 1)
                dve.wait_ge(s["sq"], NCH + 2)
                ch.link(V.reciprocal(mv[0:r, 1:2], mv[0:r, 1:2]))
                ch.link(V.tensor_scalar(x1[0:r, :], x1[0:r, :], mv[0:r, 0:1], mv[0:r, 1:2], ALU.subtract, ALU.mult))
                ch.link(V.tensor_tensor(x1[0:r, :], x1[0:r, :], g2[0:r, :], ALU.mult))
                V.tensor_tensor(x1[0:r, :], x1[0:r, :], b2[0:r, :], ALU.add).then_inc(s["x1"], 1)

            @block.scalar
            def _(act):
                for h in range(PH - 1):
                    for k in range(TOPK):
                        act_pick(act, 0, h, k)
                act_half(act, 0)
                for c in steps(act, NCH):
                    for h in range(PH):
                        for k in range(TOPK):
                            act_expert(act, c, h, k)
                            if isinstance(c, int) and c == 0 and (h, k) == (3, 9):
                                act_half(act, 1)
                            if h == 1 and not (isinstance(c, int) and c == 0):
                                act_norm(act, c, k)
                            act_pick(act, c + 1, h, k)
                        act_gelu(act, c, h)
                act.wait_ge(s["x1"], NCH + 1)
                act.dma_start(x1_d, x1[0:NSMP, :]).then_inc(s["x1st"], 16)
                for k in range(TOPK):
                    act_expert(act, NCH, 0, k)
                for b in range(NSMP):
                    act.wait_ge(s["dots"], b + 1)
                    nc.scalar.activation(hids[:, b:b + 1], hids[:, b:b + 1], ACT.Gelu).then_inc(s["gates"], 1)
                for k in range(TOPK):
                    act_norm(act, NCH, k)
                act.wait_ge(s["var"], NCH + 2)
                nc.scalar.activation(mv[0:NSMP, 1:2], mv[0:NSMP, 1:2], ACT.Sqrt).then_inc(s["sq"], 1)
                act.wait_ge(s["x1"], NCH + 2)
                act.dma_start(o["y"][SEQ:NTOK, :], x1[0:NSMP, :]).then_inc(s["stored"], 16)
                act.wait_ge(s["stored"], 16 * (NCH + 1))

            @block.tensor
            def _(pe):
                for k in range(16):
                    if k % 4 == 0:
                        pe.wait_ge(s_wo[k // 4], 16)
                    for h in range(2):
                        pe_pick(pe, 0, h, k)
                for h in range(2, PH):
                    if h == 3:
                        pe.wait_ge(s["wp"], 16 * NHC)
                    for k in range(TOPK):
                        pe_pick(pe, 0, h, k)
                for c in steps(pe, NCH):
                    for h in range(PH):
                        for k in range(TOPK):
                            pe_expert(pe, c, h, k)
                            pe_pick(pe, c + 1, h, k)
                pe.wait_ge(s["ix_lo"], NCH + 1)
                T.transpose(PB[:, 4, 0:NSMP], e2[0:NSMP, 0, :, :].rearrange("p h k -> p (h k)"), ident[0:NSMP, 0:NSMP])
                T.transpose(PB[:, 4, NSMP:2 * NSMP], gt[0:NSMP, :, :].rearrange("p h k -> p (h k)"), ident[0:NSMP, 0:NSMP]).then_inc(s["tr"], 1)
                for k in range(TOPK):
                    pe_expert(pe, NCH, 0, k)
                for b in range(NSMP):
                    pe.wait_ge(s["gz"], b + 1)
                    pe.wait_ge(s_vs[b], 16)
                    for n in range(2):
                        last = T.matmul(PB[0:NSMP, 6 + n, :], wgs[:, b, :], vs[:, b, n * 512:(n + 1) * 512],
                                        start=b == 0, stop=b == NSMP - 1)
                last.then_inc(s["go"], 1)


def kernel(x_prompt, x_sample, state_ssd, state_ssd_conv, state_mlstm_c, state_mlstm_n, state_mlstm_m,
           state_mlstm_conv, w_in, conv_ssd_w, conv_ssd_b, dt_bias, a_log, d_skip, ssd_norm_g, conv_m_w, conv_m_b,
           w_mq, w_mk, b_igate, b_fgate, mlstm_norm_g, w_out, ln1_g, ln1_b, peer_wq, peer_keys, peer_u, peer_v,
           ln2_g, ln2_b):
    import concourse.bacc as bacc
    from concourse.bass_utils import run_bass_kernel_spmd

    x = np.concatenate([x_prompt[0], x_sample[:, 0]], axis=0)
    w = np.asarray(w_in[0])
    cols = np.cumsum((D, D + 2 * NG * NST, NH, D, D, D, MH, MH))
    z, xbc, dtw, um, vm, om, iw, fw = np.split(w, cols[:-1], axis=1)

    def k_major(m):
        return m.reshape(-1, P, m.shape[-1]).transpose(1, 0, 2)

    chan = np.concatenate([xbc, um], axis=1).reshape(KD, P, NCT, P).transpose(2, 1, 0, 3)
    tok = np.concatenate([z, vm, om], axis=1).reshape(KD, P, NTB, TW).transpose(2, 1, 0, 3)
    row = np.zeros((D, P), w.dtype)
    row[:, 0:NH], row[:, 32:32 + MH], row[:, 64:64 + MH] = dtw, iw, fw
    gate_b = np.zeros((16, 4), w.dtype)
    gate_b[0:NH, 0], gate_b[0:MH, 1], gate_b[0:MH, 2], gate_b[0:NH, 3] = dt_bias[0], b_igate[0], b_fgate[0], a_log[0]
    conv_w = np.concatenate([np.concatenate([conv_ssd_w[0], conv_m_w[0]], axis=1),
                             np.concatenate([conv_ssd_b[0], conv_m_b[0]])[None]], axis=0)
    conv_s = np.concatenate([state_ssd_conv[0], state_mlstm_conv[0]], axis=2)
    wq = np.asarray(peer_wq[0]).reshape(D, NHC, P)
    arrays = {
        "x_tok": np.concatenate([x, np.zeros((NPAD - NTOK, D), x.dtype)], axis=0),
        "x_t": k_major(np.asarray(x).T),
        "w_ch": chan, "w_tok": tok, "w_row": k_major(row), "gate_b": gate_b,
        "conv_w": conv_w.T.reshape(NCT, P, TAPS + 1),
        "conv_s": conv_s.transpose(2, 1, 0).reshape(NCT, P, 3, NSMP),
        "m_state": np.asarray(state_mlstm_m[0]).T,
        "n_state": np.asarray(state_mlstm_n[0]).reshape(NSMP, MH * KT, P).transpose(2, 1, 0),
        "ssd_state": np.asarray(state_ssd[0]).reshape(NSMP, NH * HD, NST),
        "c_state": np.asarray(state_mlstm_c[0]).reshape(NSMP, MH * DK, DK),
        "d_skip": np.asarray(d_skip[0]),
        "d_skip_ch": np.repeat(np.asarray(d_skip[0]), HD).reshape(8, P).T,
        "ssd_g": np.asarray(ssd_norm_g[0]), "mlstm_g": np.asarray(mlstm_norm_g[0]).reshape(-1),
        "w_mq": np.asarray(w_mq[0]).reshape(MH, KT, P, DK).transpose(2, 0, 1, 3),
        "w_mk": np.asarray(w_mk[0]).reshape(MH, KT, P, DK).transpose(2, 0, 1, 3),
        "w_out": k_major(np.asarray(w_out[0])),
        "ln1_g": np.asarray(ln1_g[0]), "ln1_b": np.asarray(ln1_b[0]),
        "ln2_g": np.asarray(ln2_g[0]), "ln2_b": np.asarray(ln2_b[0]),
        "wq_t": wq.transpose(1, 2, 0),
        "keys_t": np.asarray(peer_keys[0]).reshape(NHC, NK, P).transpose(0, 2, 1),
        "peer_u": np.asarray(peer_u[0]), "peer_v": np.asarray(peer_v[0]),
    }
    outs = {"y": (NTOK, D), "conv_p": (NCT, P, 3), "conv_s": (NCT, P, 3, NSMP), "p_ssd": (P, D),
            "p_c": (P, MH * KT, DK), "p_n": (P, MH * KT), "p_m": (MH, 1), "s_ssd": (NSMP, NH * HD, NST),
            "s_c": (NSMP, MH * DK, DK), "s_n": (P, MH * KT, NSMP), "s_m": (MH, NSMP)}
    nc = bacc.Bacc("TRN2", target_bir_lowering=False, num_devices=1)
    given, a, o = {}, {}, {}
    for name, v in arrays.items():
        v = np.ascontiguousarray(v)
        given["in_" + name] = v
        a[name] = nc.dram_tensor("in_" + name, v.shape, mybir.dt.from_np(v.dtype), kind="ExternalInput").ap()
    for name, shape in outs.items():
        o[name] = nc.dram_tensor("out_" + name, shape, mybir.dt.float32, kind="ExternalOutput").ap()
    build(nc, a, o)
    got = run_bass_kernel_spmd(nc, [given], core_ids=[0]).results[0]
    r = {name: got["out_" + name] for name in outs}
    conv_p = r["conv_p"].reshape(NCT * P, 3).T
    conv_q = r["conv_s"].reshape(NCT * P, 3, NSMP).transpose(2, 1, 0)
    nx = D + 2 * NG * NST
    return (
        r["y"][None, 0:SEQ], r["y"][SEQ:NTOK, None],
        r["p_ssd"].T.reshape(1, 1, NH, HD, NST), conv_p[None, None, :, 0:nx],
        r["p_c"].transpose(1, 0, 2).reshape(1, 1, MH, DK, DK), r["p_n"].T.reshape(1, 1, MH, DK),
        r["p_m"].reshape(1, 1, MH), conv_p[None, None, :, nx:],
        r["s_ssd"].reshape(1, NSMP, NH, HD, NST), conv_q[None, :, :, 0:nx],
        r["s_c"].reshape(1, NSMP, MH, DK, DK), r["s_n"].transpose(2, 1, 0).reshape(1, NSMP, MH, DK),
        r["s_m"].T.reshape(1, NSMP, MH), conv_q[None, :, :, nx:],
    )
```
